# Optimizing a Trainium2 kernel written in Bass

```python
import jax, jax.numpy as jnp
from jax import lax
import numpy as np

D_MODEL = 1024
BATCH = 1
SEQ = 512
DEPTH = 1

N_HEADS = 8
HEAD_DIM = 64
ATTN_WIDTH = N_HEADS * HEAD_DIM
KV_LATENT = 128
IDX_HEADS = 4
IDX_DIM = 32
TOPK_MAX = 256
Q_BLOCK = 128
ATTN_SCALE = HEAD_DIM ** -0.5
IDX_W_SCALE = (IDX_HEADS ** -0.5) * (IDX_DIM ** -0.5)
POOL_WINDOWS = (2, 4, 8, 16)
POOL_GROUPS = 4
POOL_GROUP_DIM = 128
POOL_WIDTH = POOL_GROUPS * POOL_GROUP_DIM
N_EXPERTS = 32
TOP_K = 4
D_FF = D_MODEL // 2
MOE_BLOCK = 512
SWIGLU_LIMIT = 7.0
SWIGLU_ALPHA = 1.702
RMS_EPS = 1e-6
COL_WIDTHS = (ATTN_WIDTH, KV_LATENT, IDX_HEADS * IDX_DIM, IDX_DIM, IDX_HEADS, POOL_WIDTH, D_MODEL, D_MODEL)
IN_WIDTH = sum(COL_WIDTHS)
SPLIT_OFFSETS = tuple(int(v) for v in np.cumsum(COL_WIDTHS)[:-1])

kernel_name = 'hybrid_dsa_pool_moe_adaln'

def rms_norm(x, g):
    xf = x.astype(jnp.float32)
    y = xf * lax.rsqrt(jnp.mean(xf * xf, axis=-1, keepdims=True) + RMS_EPS)
    return (y * g.astype(jnp.float32)).astype(x.dtype)

def dsa_attention(q, ckv, qi, ki, wi, w_uk, w_uv):
    b_, L = q.shape[0], q.shape[1]
    k_sel = min(TOPK_MAX, L // 4)
    nb = L // Q_BLOCK
    key_pos = jnp.arange(L, dtype=jnp.int32)

    def to_blocks(t):
        return jnp.moveaxis(t.reshape((b_, nb, Q_BLOCK) + t.shape[2:]), 1, 0)

    def block(args):
        q_b, qi_b, wi_b, start = args
        qpos = start + jnp.arange(Q_BLOCK, dtype=jnp.int32)
        causal = key_pos[None, :] <= qpos[:, None]
        raw = jnp.einsum('bqhd,bsd->bqhs', qi_b, ki, preferred_element_type=jnp.float32)
        score = jnp.einsum('bqhs,bqh->bqs', jax.nn.relu(raw), wi_b.astype(jnp.float32) * IDX_W_SCALE)
        score = jnp.where(causal[None], score, -jnp.inf)
        _, idx = lax.top_k(score, k_sel)
        valid = idx <= qpos[None, :, None]
        kv_sel = jax.vmap(lambda kv, i: kv[i])(ckv, idx)
        q_lat = jnp.einsum('bqhd,lhd->bqhl', q_b, w_uk)
        logits = jnp.einsum('bqhl,bqkl->bqhk', q_lat, kv_sel, preferred_element_type=jnp.float32) * ATTN_SCALE
        logits = jnp.where(valid[:, :, None, :], logits, -jnp.inf)
        p = jax.nn.softmax(logits, axis=-1).astype(kv_sel.dtype)
        o_lat = jnp.einsum('bqhk,bqkl->bqhl', p, kv_sel)
        return jnp.einsum('bqhl,lhd->bqhd', o_lat, w_uv)

    starts = jnp.arange(nb, dtype=jnp.int32) * Q_BLOCK
    out = lax.map(block, (to_blocks(q), to_blocks(qi), to_blocks(wi), starts))
    return jnp.moveaxis(out, 0, 1).reshape(b_, L, ATTN_WIDTH)

def multiscale_pool(a, w_pool, pool_scale):
    b_, L, _ = a.shape
    af = a.astype(jnp.float32)
    cs = jnp.cumsum(af, axis=1)
    pos = jnp.arange(1, L + 1, dtype=jnp.float32)
    outs = []
    for g, w in enumerate(POOL_WINDOWS):
        sl = slice(g * POOL_GROUP_DIM, (g + 1) * POOL_GROUP_DIM)
        cs_g = cs[..., sl]
        prev = jnp.pad(cs_g, ((0, 0), (w, 0), (0, 0)))[:, :L]
        mean = (cs_g - prev) / jnp.minimum(pos, float(w))[:, None]
        outs.append(mean - af[..., sl])
    d = jnp.stack(outs, axis=2).astype(a.dtype)
    z = jnp.einsum('blgc,gcd->blgd', d, w_pool).reshape(b_, L, POOL_WIDTH)
    return z * pool_scale

def moe(h, w_router, b_router, w_gu, b_gu, w_down, b_down):
    b_, L, D = h.shape
    hf = h.reshape(b_ * L, D)
    n_tok = b_ * L
    n_asg = n_tok * TOP_K
    logits = (hf @ w_router + b_router).astype(jnp.float32)
    top_val, top_idx = lax.top_k(logits, TOP_K)
    wts = jax.nn.softmax(top_val, axis=-1)
    flat_e = top_idx.reshape(-1)
    order = jnp.argsort(flat_e)
    e_sorted = flat_e[order]
    tok = order // TOP_K
    w_sorted = wts.reshape(-1)[order]
    sizes = jnp.bincount(flat_e, length=N_EXPERTS).astype(jnp.int32)
    padded = ((sizes + MOE_BLOCK - 1) // MOE_BLOCK) * MOE_BLOCK
    start_unpad = jnp.cumsum(sizes) - sizes
    end_pad = jnp.cumsum(padded)
    start_pad = end_pad - padded
    rank = jnp.arange(n_asg, dtype=jnp.int32) - start_unpad[e_sorted]
    dest = start_pad[e_sorted] + rank
    n_blocks = -(-n_asg // MOE_BLOCK) + N_EXPERTS
    n_rows = n_blocks * MOE_BLOCK
    xs = jnp.zeros((n_rows, D), h.dtype).at[dest].set(hf[tok])
    blk_start = jnp.arange(n_blocks, dtype=jnp.int32) * MOE_BLOCK
    blk_e = jnp.minimum(jnp.searchsorted(end_pad, blk_start, side='right'), N_EXPERTS - 1)

    def expert_block(args):
        xb, e = args
        gu = xb @ w_gu[e] + b_gu[e]
        gt, up = gu[:, :D_FF], gu[:, D_FF:]
        gt = jnp.minimum(gt, SWIGLU_LIMIT)
        up = jnp.clip(up, -SWIGLU_LIMIT, SWIGLU_LIMIT)
        act = gt * jax.nn.sigmoid(SWIGLU_ALPHA * gt) * (up + 1.0)
        return act @ w_down[e] + b_down[e]

    ys = lax.map(expert_block, (xs.reshape(n_blocks, MOE_BLOCK, D), blk_e)).reshape(n_rows, D)
    y = ys[dest] * w_sorted[:, None].astype(ys.dtype)
    return jax.ops.segment_sum(y, tok, num_segments=n_tok).reshape(b_, L, D)

def setup_inputs(seed: int = 0) -> dict:
    key = jax.random.key(seed)
    ks = jax.random.split(key, 24)
    f32 = jnp.float32
    nrm = lambda k, shp, s: jax.random.normal(k, shp, f32) * s
    D = D_MODEL
    return {
        'x': nrm(ks[0], (BATCH, SEQ, D), 1.0),
        'c': nrm(ks[1], (BATCH, D), 1.0),
        'norm1_g': 1.0 + nrm(ks[2], (DEPTH, D), 0.05),
        'norm2_g': 1.0 + nrm(ks[3], (DEPTH, D), 0.05),
        'w_ada': nrm(ks[4], (DEPTH, D, 6 * D), 0.5 * D ** -0.5),
        'b_ada': nrm(ks[5], (DEPTH, 6 * D), 0.02),
        'w_in': nrm(ks[6], (DEPTH, D, IN_WIDTH), D ** -0.5),
        'kv_norm_g': 1.0 + nrm(ks[7], (DEPTH, KV_LATENT), 0.05),
        'w_uk': nrm(ks[8], (DEPTH, KV_LATENT, N_HEADS, HEAD_DIM), HEAD_DIM ** -0.5),
        'w_uv': nrm(ks[9], (DEPTH, KV_LATENT, N_HEADS, HEAD_DIM), KV_LATENT ** -0.5),
        'w_pool': nrm(ks[10], (DEPTH, POOL_GROUPS, POOL_GROUP_DIM, POOL_GROUP_DIM), POOL_GROUP_DIM ** -0.5),
        'pool_scale': 1.0 + nrm(ks[11], (DEPTH, POOL_WIDTH), 0.1),
        'w_a_up': nrm(ks[12], (DEPTH, ATTN_WIDTH, D), ATTN_WIDTH ** -0.5),
        'w_b_up': nrm(ks[13], (DEPTH, POOL_WIDTH, D), POOL_WIDTH ** -0.5),
        'w_out': nrm(ks[14], (DEPTH, D, D), D ** -0.5),
        'w_router': nrm(ks[15], (DEPTH, D, N_EXPERTS), D ** -0.5),
        'b_router': nrm(ks[16], (DEPTH, N_EXPERTS), 0.01),
        'w_gu': nrm(ks[17], (DEPTH, N_EXPERTS, D, 2 * D_FF), D ** -0.5),
        'b_gu': nrm(ks[18], (DEPTH, N_EXPERTS, 2 * D_FF), 0.02),
        'w_down': nrm(ks[19], (DEPTH, N_EXPERTS, D_FF, D), D_FF ** -0.5),
        'b_down': nrm(ks[20], (DEPTH, N_EXPERTS, D), 0.02),
        'final_g': 1.0 + nrm(ks[21], (D,), 0.05),
    }

def reference(x, c, norm1_g, norm2_g, w_ada, b_ada, w_in, kv_norm_g, w_uk, w_uv, w_pool, pool_scale,
              w_a_up, w_b_up, w_out, w_router, b_router, w_gu, b_gu, w_down, b_down, final_g):
    b_, L, _ = x.shape
    cond = jax.nn.silu(c)
    for l in range(DEPTH):
        ada = (cond @ w_ada[l] + b_ada[l])[:, None, :]
        sh1, sc1, g1, sh2, sc2, g2 = jnp.split(ada, 6, axis=-1)
        h = rms_norm(x, norm1_g[l]) * (1.0 + sc1) + sh1
        p = h @ w_in[l]
        q, ckv, qi, ki, wi, a_pool, gate_a, gate_b = jnp.split(p, SPLIT_OFFSETS, axis=-1)
        q = q.reshape(b_, L, N_HEADS, HEAD_DIM)
        qi = qi.reshape(b_, L, IDX_HEADS, IDX_DIM)
        ckv = rms_norm(ckv, kv_norm_g[l])
        o_a = dsa_attention(q, ckv, qi, ki, wi, w_uk[l], w_uv[l])
        o_b = multiscale_pool(a_pool, w_pool[l], pool_scale[l])
        merged = jax.nn.sigmoid(gate_a) * (o_a @ w_a_up[l]) + jax.nn.sigmoid(gate_b) * (o_b @ w_b_up[l])
        x = x + g1 * (merged @ w_out[l])
        h2 = rms_norm(x, norm2_g[l]) * (1.0 + sc2) + sh2
        x = x + g2 * moe(h2, w_router[l], b_router[l], w_gu[l], b_gu[l], w_down[l], b_down[l])
    return rms_norm(x, final_g)


_drawn_inputs = setup_inputs


def setup_inputs(seed=0):
    import zlib

    import numpy as np

    out = dict(_drawn_inputs(seed))
    spreads = {}
    factors = {'norm1_g': 2.991,
     'kv_norm_g': 4.879,
     'b_router': 11.006,
     'b_gu': 8.0,
     'b_down': 23.288,
     'norm2_g': 2.769}
    for name, (base, spread) in spreads.items():
        noise = np.random.default_rng([zlib.crc32(name.encode()), seed]).standard_normal(out[name].shape)
        drawn = base * np.exp(spread * noise) if base else spread * noise
        out[name] = __import__('jax').numpy.asarray(drawn.astype(out[name].dtype))
    for name, factor in factors.items():
        out[name] = (out[name] * factor).astype(out[name].dtype)
    return out
```

```python
from contextlib import ExitStack

import concourse.bass as bass
from concourse import mybir
from concourse.alu_op_type import AluOpType as ALU

F32 = mybir.dt.float32
BF16 = mybir.dt.bfloat16
U32 = mybir.dt.uint32
ACT = mybir.ActivationFunctionType
AX = mybir.AxisListType

P = 128
T, D = 512, 1024
C = T // P
KD = D // P
H, HD = 8, 64
AW = H * HD
LAT = 128
IH, IDIM = 4, 32
PG = 4
WINDOWS = (2, 4, 8, 16)
PAD = 16
PW = PG * P
NE, TOPK, DFF = 32, 4, 512
KF = DFF // P
LIMIT, ALPHA, EPS = 7.0, 1.702, 1e-6
K_SEL = min(256, T // 4)
SCALE = HD ** -0.5
IDX_SCALE = (IH ** -0.5) * (IDIM ** -0.5)
COL_Q, COL_TOK = 0, AW
TOKW = LAT + IH * IDIM + IDIM + IH
COL_POOL = COL_TOK + TOKW
COL_GA = COL_POOL + PW
COL_GB = COL_GA + D

MASKED = -1e38
TAKEN = -3e38
HIDDEN = -1e30
NOWHERE = 4096.0

SLOTS = 128
HX = D + NE
CH = 512


def trunk(nc, x, c, norm1_g, norm2_g, w_ada, b_ada, w_in, kv_norm_g, w_uk, w_uv, w_pool, pool_scale,
          w_a_up, w_b_up, w_out, w_router, b_router, w_gu, b_gu, w_down, b_down, final_g, out,
          slots=SLOTS, until=None):
    ctx = ExitStack()
    with ctx:
        def sb(name, shape, dt=F32):
            return ctx.enter_context(nc.sbuf_tensor(name, shape, dt))

        def sem(name):
            return ctx.enter_context(nc.semaphore(name))

        h2_dram = nc.dram_tensor("h2_rows", (T, HX), F32).ap()
        y_dram = nc.dram_tensor("moe_rows", (T, D), F32).ap()
        ada_dram = nc.dram_tensor("ada_rows", (4, D), F32).ap()

        ring = sb("ring", [P, 6, 4096])
        X = sb("X", [P, C, D])
        hT = sb("hT", [P, KD, T])
        mix = sb("mix", [P, 4096])
        attn = sb("attn", [P, 5184])
        small = sb("small", [P, 2048])

        q_latT = ring[:, 4, :].rearrange("p (h t) -> p h t", h=H)
        xn = ring[:, 4, :].rearrange("p (c d) -> p c d", c=C)
        zT = ring[:, 5, 0:2048].rearrange("p (g t) -> p g t", g=PG)
        qT = ring[:, 5, 2048:4096].rearrange("p (g t) -> p g t", g=PG)
        dT = qT
        h2 = ring[:, 4, :].rearrange("p (c d) -> p c d", c=C)
        acc_in = mix[:, :].rearrange("p (j n) -> p j n", j=8)
        acc = [acc_in[:, j, :] if j < 8 else dT[:, j - 8, :] for j in range(12)]
        mT = mix[:, :].rearrange("p (k t) -> p k t", k=KD)
        h2T = hT
        pT = attn[:, 0:2048].rearrange("p (s h q) -> p s h q", s=C, h=4)
        o_latT = attn[:, 2048:3072].rearrange("p (h q) -> p h q", h=H)
        Lt = attn[:, 3072:5120].rearrange("p (i s) -> p i s", i=4)
        g1b = attn[:, 0:1024]
        A2b = attn[:, 1024:2048]
        sh2b = attn[:, 2048:3072]
        g2b = attn[:, 3072:4096]
        sq = attn[:, 3072:4096]
        n2b = attn[:, 4096:5120]
        ada_half = [small[0:97:32, 0:512], small[0:97:32, 1536:2048]]
        win = attn[:, 4096:4096 + 2 * (PAD + T)].rearrange("p (i t) -> p i t", i=2)
        apad = sb("apad", [P, PG, PAD + T])
        oT = apad[:, :, PAD:PAD + T]
        T3 = sb("T3", [P, 3, T])
        ckvT, qiT, kiT = (T3[:, i, :] for i in range(3))
        ckv = sb("ckv", [P, C, LAT])
        qk = ring[:, 5, 0:512].rearrange("p (i t) -> p i t", i=2)
        wi = sb("wi", [P, C, IH])
        uk = small[:, 0:512]
        ukT = ring[:, 5, 512:1024].rearrange("p (i t) -> p i t", i=4)
        uvp = sb("uvp", [P, H, P])
        wpool = small[:, 1536:2048].rearrange("p (g d) -> p g d", g=PG)
        relu = small[:, 512:1536].rearrange("p (i s) -> p i s", i=2)
        score = small[:, 0:512]
        maskb = sb("maskb", [P, 1280])
        bias_of = [maskb[:, 64 * ch * (ch + 1):64 * ch * (ch + 1) + P * (ch + 1)] for ch in range(C)]
        icnt = sb("icnt", [P, PG, PAD])
        ident = sb("ident", [P, P])
        ones = sb("ones", [P, P])
        iota = sb("iota", [P, P])
        tri = sb("tri", [P, P], BF16)
        onesb = sb("onesb", [P, P], BF16)
        tokid = sb("tokid", [P, C, 3], BF16)
        causal = sb("causal", [P, P])
        kvgb = sb("kvgb", [P, LAT])
        sv = sb("sv", [28, P])
        svT = sb("svT", [P, 28])
        cnd = sb("cnd", [P, 3, KD])
        col = sb("col", [P, 64])
        sh1c, A1, ss, rstd, ss2, rstd2 = (col[:, 0:8], col[:, 8:16], col[:, 16:20], col[:, 20:24],
                                          col[:, 24:28], col[:, 28:32])
        ss3, rstd3, ss4, rstd4 = (col[:, 32 + 4 * i:36 + 4 * i] for i in range(4))
        eps = col[:, 48:49]
        t8 = col[:, 49:57]
        am = sb("am", [P, 4, C * H])
        top8 = sb("top8", [P, 8])
        wr = sb("wr", [P, KD, NE])
        br = sb("br", [NE, 1])
        lgT = attn[0:NE, 0:T]
        lg = sb("lg", [P, C, NE + 8])
        lr = attn[:, 640:640 + C * (NE + 8)].rearrange("p (c e) -> p c e", c=C)
        m8 = sb("m8", [P, C, 8])
        nm1 = sb("nm1", [P, C])
        ex = attn[:, 512:512 + C * NE].rearrange("p (c e) -> p c e", c=C)
        mask = sb("mask", [P, C, NE])
        maskh = sb("maskh", [P, C, NE], BF16)
        sm = sb("sm", [P, 2, C])
        wts = sb("wts", [P, C, NE])
        wth = sb("wth", [P, C, NE])
        rankm = sb("rankm", [P, C, NE])
        OHN = 16
        oh = attn[:, 2048:3072].bitcast(BF16).rearrange("p (i s) -> p i s", i=OHN)
        ixa = sb("ixa", [P, 2, NE])
        idx = sb("idx", [P, NE], U32)
        cmax = sb("cmax", [P, 1])
        cmaxi = sb("cmaxi", [P, 1], U32)
        b3 = small[0:3 * NE, 0:512].bitcast(BF16)
        braw = hT[0:3 * NE, 0:2, :].rearrange("p a t -> p (a t)")
        bres = hT[0:3 * NE, 2:4, :].rearrange("p a t -> p (a t)")
        sel3 = sb("sel3", [3 * NE, NE], BF16)
        XG = apad[:, :, :].rearrange("p g t -> p (g t)").rearrange("p (b d) -> p b d", b=2)
        xgT = mix[:, 0:1024].rearrange("p (k s) -> p k s", k=KD)
        Y = mix[:, 1024:3072].rearrange("p (b d) -> p b d", b=2)
        gt = mix[:, 3072:3584]
        up1 = mix[:, 3584:4096]
        th = attn[:, 512:1024]
        av = attn[:, 1024:1536]
        actT = attn[:, 1536:2048].rearrange("p (k s) -> p k s", k=KF)
        WC = sb("WC", [P, 2])
        iug = sb("iug", [P, 2], U32)
        ius = sb("ius", [P, 2], U32)
        wtT = attn[0:NE, 2048:2048 + T]
        bdn = hT[0:NE, 0:2, :]
        fgb = hT[:, 2:4, :].rearrange("p a t -> p (a t)")
        Yin = ring[:, 0, :].rearrange("p (c d) -> p c d", c=C)
        res = ring[:, 1, :].rearrange("p (c d) -> p c d", c=C)
        zero = ring[:, 5, 0:512]
        ps = ctx.enter_context(nc.psum_tensor("ps", [P, 8, CH], F32))

        def ada_piece(j):
            return w_ada[0, :, j * CH:(j + 1) * CH].rearrange("(p k) n -> p k n", k=KD)

        def in_piece(at, width):
            return w_in[0, :, at:at + width].rearrange("(k p) n -> p k n", p=P)

        PIECES = ([("a", j, ada_piece(j)) for j in range(4)]
                  + [("tok", 0, in_piece(COL_TOK, TOKW)), ("q", 0, in_piece(COL_Q, AW))]
                  + [("a", 4, ada_piece(4)), ("a", 5, ada_piece(5)), ("pool", 0, in_piece(COL_POOL, PW))]
                  + [("a", 6, ada_piece(6)), ("a", 7, ada_piece(7)), ("gb", 0, in_piece(COL_GB, CH))]
                  + [("a", 8, ada_piece(8)), ("a", 9, ada_piece(9)), ("gb", 1, in_piece(COL_GB + CH, CH))]
                  + [("a", 10, ada_piece(10)), ("a", 11, ada_piece(11))]
                  + [("wb", 0, w_b_up[0].rearrange("(k p) n -> p k n", p=P))]
                  + [("ga", i, in_piece(COL_GA + i * CH, CH)) for i in range(2)]
                  + [("wa", 0, w_a_up[0].rearrange("(k p) n -> p k n", p=P))]
                  + [("wo", i, w_out[0, :, i * CH:(i + 1) * CH].rearrange("(k p) n -> p k n", p=P))
                     for i in range(2)])
        FR = 4
        NFP = len(PIECES)
        place = {(k, i): n for n, (k, i, _) in enumerate(PIECES)}
        LAST_JOB = {("tok", 0): ("tok", C - 1), ("q", 0): ("q", 3), ("pool", 0): ("pool", PG - 1),
                    ("gb", 0): ("gb", 3), ("gb", 1): ("gb", 7), ("wb", 0): ("B", KD - 1),
                    ("ga", 0): ("ga", 3), ("ga", 1): ("ga", 7), ("wa", 0): ("A", KD - 1),
                    ("wo", 0): ("out", 2 * C - 2), ("wo", 1): ("out", 2 * C - 1)}

        def piece(kind, i=0):
            s = place[kind, i] % FR
            src = PIECES[place[kind, i]][2]
            k, n = src.shape[1], src.shape[2]
            return ring[:, s, 0:k * n].rearrange("p (k n) -> p k n", k=k)

        JOBS = ([("sv", 0, "D"), ("uk", 0, "A")]
                + [("xT", i, "A") for i in range(8)]
                + [("adac", 0, "D")]
                + [("tok", i, "D") for i in range(C)] + [("tr", i, "A") for i in range(C)]
                + [("idx", 4 + i, "A") for i in range(4)]
                + [("q", i, "A") for i in range(4)] + [("qlat", h, "A") for h in range(H)]
                + [("idx", 8 + i, "A") for i in range(4)]
                + [("pool", i, "A") for i in range(PG)]
                + [("idx", 12 + i, "A") for i in range(4)]
                + [("z", i, "A") for i in range(PG)])
        for g in range(8):
            JOBS += [("L", 4 * g + i, "D") for i in range(4)] + [("gb", g, "A")]
            JOBS += [("PT", 4 * g + i, "A") for i in range(4)] + [("O", g, "A")]
            if g % 2:
                JOBS += [("V", g // 2, "A")]
            if g == 1:
                JOBS += [("row", j, "D") for j in range(4, 8)]
        JOBS += [("row", j, "D") for j in range(8, 12)]
        JOBS += [("B", m, "D") for m in range(KD)]
        for m in range(KD):
            JOBS += [("ga", m, "A"), ("A", m, "D")]
        for ch in range(C):
            JOBS += [("out", 2 * ch, "D"), ("out", 2 * ch + 1, "D")]
            if ch:
                JOBS += [("h2T", 2 * ch - 2, "A"), ("h2T", 2 * ch - 1, "A")]
        JOBS += [("h2T", 6, "A"), ("h2T", 7, "A"), ("rout", 0, "A"), ("rt", 0, "D"), ("rank", 0, "D"),
                 ("ix", 0, "D"), ("ix", 1, "D")]
        number = {(k, i): n for n, (k, i, _) in enumerate(JOBS)}
        emptied = [sum(1 for j in JOBS[:n + 1] if j[2] == JOBS[n][2]) for n in range(len(JOBS))]
        NJ = len(JOBS)

        def bank(kind, i=0):
            return ps[:, number[kind, i] % 8, :]

        piece_in = [sem(f"piece_in{i}") for i in range(6)]
        acc_ok = sem("acc_ok")
        job_done = sem("job_done")
        by_act, by_vec = sem("by_act"), sem("by_vec")
        c_in, x_in, sv_in, kvg_in = sem("c_in"), sem("x_in"), sem("sv_in"), sem("kvg_in")
        uk_in, uv_in, pool_in, wr_in, bg_in = (sem("uk_in"), sem("uv_in"), sem("pool_in"),
                                               sem("wr_in"), sem("bg_in"))
        brow_in, row_out, rows_in, g2_in = sem("brow_in"), sem("row_out"), sem("rows_in"), sem("g2_in")
        h2_out, wt_out, zero_out = sem("h2_out"), sem("wt_out"), sem("zero_out")
        consts, cnt_ok, icnt_ok = sem("consts"), sem("cnt_ok"), sem("icnt_ok")
        th_c = sem("th_c")
        ss_ok, rstd_ok, xn_ok = sem("ss_ok"), sem("rstd_ok"), sem("xn_ok")
        hT_ok = sem("hT_ok")
        ss2_ok, rstd2_ok, tok_ok = sem("ss2_ok"), sem("rstd2_ok"), sem("tok_ok")
        relu_used = sem("relu_used")
        d_ok = sem("d_ok")
        select_ok = sem("select_ok")
        max_ok, exp_ok, prob_ok = sem("max_ok"), sem("exp_ok"), sem("prob_ok")
        ss3_ok, h2_ok = sem("ss3_ok"), sem("h2_ok")
        nm_ok, ex_ok, wt_ok = sem("nm_ok"), sem("ex_ok"), sem("wt_ok")
        iug_ok, ius_ok, wc_ok = sem("iug_ok"), sem("ius_ok"), sem("wc_ok")
        pool_steps, dve_steps = sem("pool_steps"), sem("dve_steps")
        up_ok, prod_ok = sem("up_ok"), sem("prod_ok")
        mask_ok, oh_ok, oh_used, idx_ok = sem("mask_ok"), sem("oh_ok"), sem("oh_used"), sem("idx_ok")
        b3_ok = sem("b3_ok")
        act_chain, dve_chain, pool_chain = sem("act_chain"), sem("dve_chain"), sem("pool_chain")
        xg_clear = sem("xg_clear")
        xg_in = [sem("xg_in0"), sem("xg_in1")]
        tx_done, xgT_ok = sem("tx_done"), sem("xgT_ok")
        gu_done, gt_ok, th_ok, av_ok = sem("gu_done"), sem("gt_ok"), sem("th_ok"), sem("av_ok")
        ta_done, actT_ok, dn_done, y_ok = sem("ta_done"), sem("actT_ok"), sem("dn_done"), sem("y_ok")
        y_added = sem("y_added")
        ov_go, ov_w, ov_oh, ov_ix, ov_idx, ov_xg = (sem("ov_" + n) for n in
                                                    ("go", "w", "oh", "ix", "idx", "xg"))
        ov_tx, ov_xt, ov_gu, ov_gt, ov_th, ov_av = (sem("ov_" + n) for n in
                                                    ("tx", "xt", "gu", "gt", "th", "av"))
        ov_ta, ov_at, ov_dn, ov_y, ov_add = (sem("ov_" + n) for n in ("ta", "at", "dn", "y", "add"))
        ov_rk, ov_i1, ov_up, ov_wc = (sem("ov_" + n) for n in ("rk", "i1", "up", "wc"))
        OVER = (T - 1) // slots
        moe_done, bd_in, fg_in, y_in = sem("moe_done"), sem("bd_in"), sem("fg_in"), sem("y_in")
        wtT_done, wtT_ok, yb_done = sem("wtT_done"), sem("wtT_ok"), sem("yb_done")
        x2_ok, ss4_ok, res_ok, out_done = sem("x2_ok"), sem("ss4_ok"), sem("res_ok"), sem("out_done")

        def rows(dram):
            return dram.rearrange("(c p) d -> p c d", p=P)

        def spread(row, n=D):
            return row.rearrange("(o n) -> o n", o=1).broadcast_to([P, n])

        def expert_pieces(e):
            gu = w_gu[0, bass.ds(e, 1), :, :].rearrange("a (k p) n -> p (a k) n", p=P)
            dn = w_down[0, bass.ds(e, 1), :, :].rearrange("a (k p) n -> p (a k) n", p=P)
            return gu[:, :, 0:DFF], gu[:, :, DFF:2 * DFF], dn

        def slot3(s):
            return (ring[:, s, :].rearrange("p (k n) -> p k n", k=KD),
                    ring[:, s + 1, :].rearrange("p (k n) -> p k n", k=KD),
                    ring[:, s + 2, :].rearrange("p (k n) -> p k n", k=KF))

        block = ctx.enter_context(nc.Block())

        @block.sync
        def _(sp):
            sp.dma_start(cnd[:, 0, :], c[0, :].rearrange("(p k) -> p k", k=KD)).then_inc(c_in, 16)
            sp.dma_start(X[:, :, :], rows(x[0])).then_inc(x_in, 16)
            sp.dma_start(sv[0:16, :], b_ada[0, 0:2 * D].rearrange("(r n) -> r n", n=P)).then_inc(sv_in, 16)
            sp.dma_start(sv[16:24, :], norm1_g[0].rearrange("(r n) -> r n", n=P)).then_inc(sv_in, 16)
            sp.dma_start(sv[24:28, :], pool_scale[0].rearrange("(r n) -> r n", n=P)).then_inc(sv_in, 16)

            def used(n):
                kind, i, _ = PIECES[n]
                if kind == "a":
                    sp.wait_ge(acc_ok, i + 1)
                else:
                    sp.wait_ge(job_done, number[LAST_JOB[kind, i]] + 1)

            for n, (kind, i, src) in enumerate(PIECES):
                if n >= FR:
                    used(n - FR)
                sp.dma_start(piece(kind, i), src).then_inc(piece_in[n % FR], 16)
                if n == 3:
                    sp.dma_start(kvgb[:, :], spread(kv_norm_g[0], LAT)).then_inc(kvg_in, 16)
                if n == 5:
                    sp.dma_start(wr[:, :, :], w_router[0].rearrange("(k p) n -> p k n", p=P)).then_inc(wr_in, 16)
                    sp.dma_start(br[:, :], b_router[0].rearrange("(e o) -> e o", o=1)).then_inc(wr_in, 16)
            srcs = expert_pieces(0)
            dst = slot3(0)
            for j in range(3):
                used(NFP - 3 + j)
                sp.dma_start(dst[j], srcs[j]).then_inc(piece_in[j], 16)
            srcs = expert_pieces(1)
            dst = slot3(3)
            for j in range(3):
                if j == 0:
                    used(NFP - 4)
                if j == 1:
                    sp.wait_ge(h2_out, 16 * C)
                    sp.wait_ge(job_done, number["h2T", 7] + 1)
                    sp.wait_ge(zero_out, 16 * 8)
                sp.dma_start(dst[j], srcs[j]).then_inc(piece_in[3 + j], 16)
            with sp.Fori(1, NE // 2) as i:
                for b in range(2):
                    e = i * 2 + b
                    srcs, dst = expert_pieces(e), slot3(3 * b)
                    sp.wait_ge(gu_done, e * 2 - 3)
                    sp.dma_start(dst[0], srcs[0]).then_inc(piece_in[3 * b], 16)
                    sp.wait_ge(gu_done, e * 2 - 2)
                    sp.dma_start(dst[1], srcs[1]).then_inc(piece_in[3 * b + 1], 16)
                    sp.wait_ge(dn_done, e - 1)
                    sp.dma_start(dst[2], srcs[2]).then_inc(piece_in[3 * b + 2], 16)
            most = sp.value_load(cmaxi[0:1, 0:1], min_val=0, max_val=T)
            with sp.If(most > slots):
                with sp.Fori(0, OVER) as r:
                    with sp.Fori(0, NE) as e:
                        sp.wait_ge(ov_go, r * NE + e + 1)
                        for d_, s_ in zip(slot3(0), expert_pieces(e)):
                            sp.dma_start(d_, s_).then_inc(ov_w, 16)
            sp.wait_ge(b3_ok, 1)
            sp.dma_start(bdn, b_down[0].rearrange("e (a n) -> e a n", a=2)).then_inc(bd_in, 16)
            sp.dma_start(fgb, spread(final_g)).then_inc(fg_in, 16)
            sp.wait_ge(moe_done, 1)
            sp.dma_start(Yin, rows(y_dram)).then_inc(y_in, 16)
            for ch in range(C):
                sp.wait_ge(res_ok, ch + 1)
                sp.dma_start(rows(out[0])[:, ch, :], res[:, ch, :]).then_inc(out_done, 16)
            sp.wait_ge(out_done, 16 * C)

        @block.gpsimd
        def _(pool):
            chain = [0]

            def link(ins):
                chain[0] += 1
                ins.then_inc(pool_chain, 1)
                pool.wait_ge(pool_chain, chain[0])

            nc.gpsimd.memset(ones[:, :], 1.0)
            nc.gpsimd.memset(eps, EPS)
            nc.gpsimd.memset(onesb[:, :], 1.0)
            link(nc.gpsimd.memset(ident[:, :], 0.0))
            link(nc.gpsimd.affine_select(out=ident[:, :], in_=ident[:, :], compare_op=ALU.not_equal, fill=1.0,
                                         base=0, pattern=[[-1, P]], channel_multiplier=1))
            nc.gpsimd.drain().then_inc(consts, 1)
            link(nc.gpsimd.memset(uvp[:, :, :], 0.0))
            link(nc.gpsimd.memset(causal[:, :], 0.0))
            nc.gpsimd.affine_select(out=causal[:, :], in_=causal[:, :], compare_op=ALU.is_ge, fill=MASKED,
                                    base=0, pattern=[[-1, P]], channel_multiplier=1)
            link(nc.gpsimd.memset(bias_of[0], 0.0))
            nc.gpsimd.affine_select(out=bias_of[0], in_=bias_of[0], compare_op=ALU.is_ge, fill=HIDDEN,
                                    base=0, pattern=[[-1, P]], channel_multiplier=1)
            nc.gpsimd.affine_select(out=tri[:, :], in_=onesb[:, :], compare_op=ALU.is_gt, fill=0.0,
                                    base=0, pattern=[[1, P]], channel_multiplier=-1)
            nc.gpsimd.iota(iota[:, :], pattern=[[1, P]], base=0, channel_multiplier=0,
                           allow_small_or_imprecise_dtypes=True)
            nc.gpsimd.iota(tokid[:, :, 0], pattern=[[1, C]], base=0, channel_multiplier=0,
                           allow_small_or_imprecise_dtypes=True)
            nc.gpsimd.iota(tokid[:, :, 1], pattern=[[0, C]], base=0, channel_multiplier=1,
                           allow_small_or_imprecise_dtypes=True)
            nc.gpsimd.memset(tokid[:, :, 2], 1.0)
            link(nc.gpsimd.memset(sel3[:, :], 0.0))
            for part in range(3):
                link(nc.gpsimd.affine_select(out=sel3[:, :], in_=sel3[:, :], compare_op=ALU.not_equal, fill=1.0,
                                             base=-part * NE, pattern=[[-1, NE]], channel_multiplier=1))
            for g in range(PG):
                nc.gpsimd.iota(icnt[:, g, :], pattern=[[1, PAD]], base=1, channel_multiplier=0,
                               allow_small_or_imprecise_dtypes=True)
            nc.gpsimd.memset(lg[:, :, :], MASKED)
            nc.gpsimd.memset(apad[:, :, 0:PAD], 0.0)
            nc.gpsimd.memset(win[:, :, 0:PAD], 0.0)
            nc.gpsimd.drain().then_inc(consts, 1)
            pool.dma_start(uk, w_uk[0].rearrange("l h d -> l (h d)")).then_inc(uk_in, 16)
            pool.dma_start(wpool, w_pool[0].rearrange("g c d -> c g d")).then_inc(pool_in, 16)
            for h in range(H):
                at = HD * (h % 2)
                pool.dma_start(uvp[:, h, at:at + HD], w_uv[0, :, h, :]).then_inc(uv_in, 16)
            pool.wait_ge(consts, 2)
            for g, w in enumerate(WINDOWS):
                last = nc.gpsimd.tensor_scalar(icnt[:, g, :], icnt[:, g, :], float(w), 0.0, ALU.min, ALU.max)
            last.then_inc(cnt_ok, 1)
            pool.wait_ge(icnt_ok, 1)

            for g, w in enumerate(WINDOWS):
                pool.wait_ge(by_act, emptied[number["pool", g]])
                if g == 0:
                    pool.wait_ge(job_done, number["qlat", H - 1] + 1)
                src, span, n = apad[:, g, :], 1, 0
                while span < w:
                    dst = win[:, n % 2, :]
                    link(nc.gpsimd.tensor_tensor(dst[:, PAD:PAD + T], src[:, PAD:PAD + T],
                                                 src[:, PAD - span:PAD - span + T], ALU.add))
                    src, span, n = dst, 2 * span, n + 1
                link(nc.gpsimd.tensor_tensor(dT[:, g, 0:PAD], src[:, PAD:2 * PAD], icnt[:, g, :], ALU.mult))
                link(nc.gpsimd.tensor_scalar(dT[:, g, PAD:T], src[:, 2 * PAD:PAD + T], 1.0 / w, 0.0,
                                             ALU.mult, ALU.add))
                nc.gpsimd.tensor_tensor(dT[:, g, :], dT[:, g, :], apad[:, g, PAD:PAD + T],
                                        ALU.subtract).then_inc(d_ok, 1)

            pool.wait_ge(select_ok, 1)
            pool.wait_ge(job_done, number["z", PG - 1] + 1)
            for half in range(2):
                pool.dma_start(ada_half[half],
                               b_ada[0, 2 * D:6 * D].rearrange("(r a n) -> r a n", r=4, a=2)[:, half, :]
                               ).then_inc(brow_in, 16)
            pool.wait_ge(by_vec, emptied[number["row", 11]])
            for half in range(2):
                pool.dma_start(ada_dram.rearrange("r (a n) -> r a n", a=2)[:, half, :],
                               ada_half[half]).then_inc(row_out, 16)
            pool.wait_ge(row_out, 32)
            pool.wait_ge(job_done, number["V", C - 1] + 1)
            pool.dma_start(g1b, spread(ada_dram[0])).then_inc(rows_in, 16)
            pool.dma_start(sh2b, spread(ada_dram[1])).then_inc(rows_in, 16)
            pool.dma_start(A2b, spread(ada_dram[2])).then_inc(rows_in, 16)
            pool.dma_start(n2b, spread(norm2_g[0])).then_inc(rows_in, 16)
            pool.wait_ge(job_done, number["B", KD - 1] + 1)
            link(nc.gpsimd.memset(zero, 0.0))
            yz = y_dram.rearrange("(p a) (b n) -> p (a b) n", a=T // P, n=CH)
            for j in range(8):
                pool.dma_start(yz[:, j, :], zero).then_inc(zero_out, 16)
            pool.wait_ge(job_done, number["A", KD - 1] + 1)
            link(nc.gpsimd.memset(XG[:, :, :], 0.0))
            for ch in range(C):
                pool.wait_ge(h2_ok, ch + 1)
                pool.dma_start(rows(h2_dram)[:, ch, 0:D], h2[:, ch, :]).then_inc(h2_out, 16)
            pool.wait_ge(ss3_ok, C)
            pool.dma_start(g2b, spread(ada_dram[3])).then_inc(g2_in, 16)
            pool.wait_ge(job_done, number["rout", 0] + 1)
            for part in range(3):
                pool.dma_start(braw[part * NE:(part + 1) * NE, :], b_gu[0]).then_inc(bg_in, 16)
            pool.wait_ge(bg_in, 48)
            link(nc.gpsimd.tensor_copy(b3, braw))
            link(nc.gpsimd.tensor_tensor(bres, braw, b3, ALU.subtract))
            nc.gpsimd.tensor_copy(b3[NE:2 * NE, :], bres[NE:2 * NE, :])
            link(nc.gpsimd.tensor_copy(b3[2 * NE:3 * NE, :], bres[2 * NE:3 * NE, :]))
            link(nc.gpsimd.tensor_tensor(braw[2 * NE:3 * NE, :], bres[2 * NE:3 * NE, :],
                                         b3[2 * NE:3 * NE, :], ALU.subtract))
            nc.gpsimd.tensor_copy(b3[2 * NE:3 * NE, :], braw[2 * NE:3 * NE, :]).then_inc(b3_ok, 1)
            pool.wait_ge(b3_ok, 1)

            pool.wait_ge(wt_ok, 1)
            pool.dma_start(rows(h2_dram)[:, :, D:HX], wth[:, :, :]).then_inc(wt_out, 16)
            last_row = pool.to_reg(T - 1)

            def gather(b, done):
                pool.indirect_dma_start(out=XG[:, b, :], out_offset=None, in_=h2_dram,
                                        in_offset=bass.IndirectOffsetOnAxis(ap=iug[:, b:b + 1], axis=0),
                                        bounds_check=last_row, oob_is_err=False).then_inc(done, 16)

            def scatter(b, which, done):
                pool.indirect_dma_start(out=y_dram, in_=Y[:, b, :], in_offset=None,
                                        out_offset=bass.IndirectOffsetOnAxis(ap=which, axis=0),
                                        bounds_check=last_row, oob_is_err=False,
                                        compute_op=ALU.add).then_inc(done, 16)

            pool.wait_ge(h2_out, 16 * C)
            pool.wait_ge(wt_out, 16)
            pool.wait_ge(idx_ok, 1)
            for b in range(2):
                link(nc.gpsimd.tensor_copy(iug[:, b:b + 1], idx[:, b:b + 1]))
                gather(b, xg_in[b])
            pool.wait_ge(zero_out, 16 * 8)

            def wait_apart(s_, value):
                pool.wait_ge(s_, value)
                pool.sem_inc(pool_steps, 1)

            def gather_ahead(e, b):
                wait_apart(wc_ok, e + 1)
                nc.gpsimd.tensor_copy(iug[:, b:b + 1], idx[:, bass.ds(e + 2, 1)]).then_inc(iug_ok, 1)
                wait_apart(iug_ok, e + 1)
                gather(b, xg_in[b])

            def add_rows(e, b, first=False):
                if not first:
                    wait_apart(y_added, e * 16)
                nc.gpsimd.tensor_copy(ius[:, b:b + 1], idx[:, bass.ds(e, 1)]).then_inc(ius_ok, 1)
                pool.wait_ge(ius_ok, e + 1)
                wait_apart(y_ok, e + 1)
                scatter(b, ius[:, b:b + 1], y_added)

            gather_ahead(0, 0)
            gather_ahead(1, 1)
            add_rows(0, 0, first=True)
            with pool.Fori(1, NE // 2 - 1) as i:
                gather_ahead(i * 2, 0)
                add_rows(i * 2 - 1, 1)
                gather_ahead(i * 2 + 1, 1)
                add_rows(i * 2, 0)
            add_rows(NE - 3, 1)
            add_rows(NE - 2, 0)
            add_rows(NE - 1, 1)
            pool.wait_ge(y_added, 16 * NE)
            most = pool.value_load(cmaxi[0:1, 0:1], min_val=0, max_val=T)
            with pool.If(most > slots):
                pool.sem_inc(ov_go, 1)
                with pool.Fori(0, OVER) as r:
                    with pool.Fori(0, NE) as e:
                        n = r * NE + e
                        wait_apart(ov_idx, n + 1)
                        gather(0, ov_xg)
                        wait_apart(ov_y, n + 1)
                        scatter(0, iug[:, 0:1], ov_add)
                        pool.wait_ge(ov_add, n * 16 + 16)
                        pool.sem_inc(ov_go, 1)
            pool.sem_inc(moe_done, 1)

        @block.scalar
        def _(act):
            chain = [0]

            def link(ins):
                chain[0] += 1
                ins.then_inc(act_chain, 1)
                act.wait_ge(act_chain, chain[0])

            def job(kind, i=0):
                act.wait_ge(job_done, number[kind, i] + 1)
                return bank(kind, i)

            act.wait_ge(c_in, 16)
            nc.scalar.activation(cnd[:, 1, :], cnd[:, 0, :], ACT.Tanh, scale=0.5).then_inc(th_c, 1)
            act.wait_ge(x_in, 16)
            act.wait_ge(consts, 1)
            for ch in range(C):
                link(nc.scalar.activation(xn[:, ch, :], X[:, ch, :], ACT.Square, accum_out=ss[:, ch:ch + 1]))
            nc.scalar.activation(ss, ss, ACT.Sqrt, scale=1.0 / D, bias=eps).then_inc(ss_ok, 1)
            act.wait_ge(rstd_ok, 1)
            for ch in range(C):
                nc.scalar.activation(xn[:, ch, :], X[:, ch, :], ACT.Copy,
                                     scale=rstd[:, ch:ch + 1]).then_inc(xn_ok, 1)
            nc.scalar.activation(ukT[:, :, :].rearrange("p a l -> p (a l)"), job("uk"), ACT.Copy).then_inc(by_act, 1)
            for i in range(8):
                ch, half = i // 2, i % 2
                nc.scalar.activation(hT[:, 4 * half:4 * half + 4, ch * P:(ch + 1) * P],
                                     job("xT", i).rearrange("p (k t) -> p k t", k=4), ACT.Copy).then_inc(by_act, 1)
            for ch in range(C):
                link(nc.scalar.activation(ckv[:, ch, :], job("tok", ch)[:, 0:LAT], ACT.Square,
                                          accum_out=ss2[:, ch:ch + 1]))
                nc.scalar.activation(ss2[:, ch:ch + 1], ss2[:, ch:ch + 1], ACT.Sqrt, scale=1.0 / LAT,
                                     bias=eps).then_inc(ss2_ok, 1)
            for ch in range(C):
                nc.scalar.activation(T3[:, :, ch * P:(ch + 1) * P],
                                     job("tr", ch)[:, 0:3 * P].rearrange("p (a t) -> p a t", a=3),
                                     ACT.Copy).then_inc(by_act, 1)

            relus = [0]

            def index_chunk(ch):
                n = P * (ch + 1)
                for h in range(IH):
                    src = job("idx", 4 * ch + h)
                    if relus[0] >= 2:
                        act.wait_ge(relu_used, relus[0] - 1)
                    nc.scalar.activation(relu[:, relus[0] % 2, 0:n], src[:, 0:n], ACT.Relu).then_inc(by_act, 1)
                    relus[0] += 1

            index_chunk(1)
            for i in range(4):
                nc.scalar.activation(qT[:, i, :], job("q", i), ACT.Copy).then_inc(by_act, 1)
            for h in range(H):
                nc.scalar.activation(q_latT[:, h, :], job("qlat", h), ACT.Copy).then_inc(by_act, 1)
            index_chunk(2)
            for g in range(PG):
                nc.scalar.activation(apad[:, g, PAD:PAD + T], job("pool", g), ACT.Copy).then_inc(by_act, 1)
            index_chunk(3)
            for g in range(PG):
                nc.scalar.activation(zT[:, g, :], job("z", g), ACT.Copy,
                                     scale=svT[:, 24 + g:25 + g]).then_inc(by_act, 1)
            for g in range(8):
                ch, hh = g // 2, g % 2
                n = P * (ch + 1)
                for i in range(4):
                    s = 4 * g + i
                    act.wait_ge(max_ok, s + 1)
                    nc.scalar.activation(Lt[:, i, 0:n], Lt[:, i, 0:n], ACT.Exp, scale=SCALE,
                                         bias=am[:, 1, s:s + 1], accum_out=am[:, 2, s:s + 1]).then_inc(exp_ok, 1)
                nc.scalar.activation(mT[:, g, :], job("gb", g), ACT.Tanh, scale=0.5).then_inc(by_act, 1)
                for i in range(4):
                    src = job("PT", 4 * g + i)
                    nc.scalar.activation(pT[:, 0:ch + 1, i, :], src[:, 0:n].rearrange("p (s q) -> p s q", q=P),
                                         ACT.Copy).then_inc(by_act, 1)
                nc.scalar.activation(o_latT[:, 4 * hh:4 * hh + 4, :].rearrange("p h q -> p (h q)"),
                                     job("O", g), ACT.Copy).then_inc(by_act, 1)
                if hh:
                    nc.scalar.activation(oT[:, :, ch * P:(ch + 1) * P],
                                         job("V", ch).rearrange("p (a q) -> p a q", a=4),
                                         ACT.Copy).then_inc(by_act, 1)
            for m in range(KD):
                src = job("ga", m)
                if m >= 2:
                    act.wait_ge(by_vec, emptied[number["A", m - 2]])
                nc.scalar.activation(relu[:, m % 2, :], src, ACT.Tanh, scale=0.5).then_inc(by_act, 1)
            def h2T_copy(ch):
                for half in range(2):
                    nc.scalar.activation(h2T[:, 4 * half:4 * half + 4, ch * P:(ch + 1) * P],
                                         job("h2T", 2 * ch + half).rearrange("p (k t) -> p k t", k=4),
                                         ACT.Copy).then_inc(by_act, 1)

            for ch in range(C):
                act.wait_ge(by_vec, emptied[number["out", 2 * ch + 1]])
                link(nc.scalar.activation(sq, X[:, ch, :], ACT.Square, accum_out=ss3[:, ch:ch + 1]))
                nc.scalar.activation(ss3[:, ch:ch + 1], ss3[:, ch:ch + 1], ACT.Sqrt, scale=1.0 / D,
                                     bias=eps).then_inc(ss3_ok, 1)
                if ch:
                    h2T_copy(ch - 1)
            h2T_copy(C - 1)
            act.wait_ge(wr_in, 32)
            nc.scalar.activation(lgT, job("rout")[0:NE, :], ACT.Identity, bias=br[:, 0:1]).then_inc(by_act, 1)
            act.wait_ge(nm_ok, 1)
            for ch in range(C):
                nc.scalar.activation(ex[:, ch, :], lg[:, ch, 0:NE], ACT.Exp, bias=nm1[:, ch:ch + 1]).then_inc(ex_ok, 1)

            def xgT_copy(ok):
                nc.scalar.activation(xgT[:, 0:4, :].rearrange("p k s -> p (k s)"), ps[:, 4, :], ACT.Copy)
                nc.scalar.activation(xgT[:, 4:8, :].rearrange("p k s -> p (k s)"), ps[:, 5, :],
                                     ACT.Copy).then_inc(ok, 1)

            def tanh_gate(e):
                act.wait_ge(gt_ok, e + 1)
                nc.scalar.activation(th, gt, ACT.Tanh, scale=0.5 * ALPHA).then_inc(th_ok, 1)

            def token_weights(e, b):
                nc.scalar.activation(WC[:, b:b + 1], XG[:, b, bass.ds(e + D, 1)], ACT.Copy).then_inc(wc_ok, 1)

            def weighted(e, b, reused=True):
                act.wait_ge(dn_done, e + 1)
                if reused:
                    act.wait_ge(y_added, e * 16 - 16)
                act.wait_ge(wt_ok, 1)
                nc.scalar.activation(Y[:, b, 0:CH], ps[:, 2, :], ACT.Copy, scale=WC[:, b:b + 1])
                nc.scalar.activation(Y[:, b, CH:D], ps[:, 3, :], ACT.Copy, scale=WC[:, b:b + 1]).then_inc(y_ok, 1)

            def actT_copy(e):
                act.wait_ge(ta_done, e + 1)
                nc.scalar.activation(actT[:, :, :].rearrange("p k s -> p (k s)"), ps[:, 6, :], ACT.Copy).then_inc(actT_ok, 1)

            def expert(e, b, reused=True, last=False):
                tanh_gate(e)
                if not last:
                    act.wait_ge(tx_done, e + 2)
                    xgT_copy(xgT_ok)
                weighted(e - 1, 1 - b, reused)
                actT_copy(e)
                if not last:
                    act.wait_ge(y_ok, e)
                    token_weights(e + 1, 1 - b)

            act.wait_ge(tx_done, 1)
            xgT_copy(xgT_ok)
            token_weights(0, 0)
            tanh_gate(0)
            act.wait_ge(tx_done, 2)
            xgT_copy(xgT_ok)
            token_weights(1, 1)
            actT_copy(0)
            expert(1, 1, reused=False)
            expert(2, 0, reused=False)
            with act.Fori(1, NE // 2 - 1) as i:
                expert(i * 2 + 1, 1)
                expert(i * 2 + 2, 0)
            expert(NE - 1, 1, last=True)
            weighted(NE - 1, 1)

            most = act.value_load(cmaxi[0:1, 0:1], min_val=0, max_val=T)
            with act.If(most > slots):
                with act.Fori(0, OVER) as r:
                    with act.Fori(0, NE) as e:
                        n = r * NE + e
                        act.wait_ge(ov_tx, n + 1)
                        xgT_copy(ov_xt)
                        act.wait_ge(ov_gt, n + 1)
                        nc.scalar.activation(th, gt, ACT.Tanh, scale=0.5 * ALPHA).then_inc(ov_th, 1)
                        act.wait_ge(ov_ta, n + 1)
                        nc.scalar.activation(actT[:, :, :].rearrange("p k s -> p (k s)"), ps[:, 6, :],
                                             ACT.Copy).then_inc(ov_at, 1)
                        nc.scalar.activation(WC[:, 0:1], XG[:, 0, bass.ds(e + D, 1)], ACT.Copy).then_inc(ov_wc, 1)
                        act.wait_ge(ov_wc, n + 1)
                        act.wait_ge(ov_dn, n + 1)
                        for half in range(2):
                            last = nc.scalar.activation(Y[:, 0, half * CH:(half + 1) * CH], ps[:, 2 + half, :],
                                                        ACT.Copy, scale=WC[:, 0:1])
                        last.then_inc(ov_y, 1)

            act.wait_ge(wtT_done, 1)
            nc.scalar.activation(wtT, ps[0:NE, 7, :], ACT.Copy).then_inc(wtT_ok, 1)
            for ch in range(C):
                act.wait_ge(x2_ok, ch + 1)
                link(nc.scalar.activation(res[:, ch, :], X[:, ch, :], ACT.Square, accum_out=ss4[:, ch:ch + 1]))
                nc.scalar.activation(ss4[:, ch:ch + 1], ss4[:, ch:ch + 1], ACT.Sqrt, scale=1.0 / D,
                                     bias=eps).then_inc(ss4_ok, 1)

        @block.vector
        def _(dve):
            chain = [0]

            def link(ins):
                chain[0] += 1
                ins.then_inc(dve_chain, 1)
                dve.wait_ge(dve_chain, chain[0])

            def job(kind, i=0):
                dve.wait_ge(job_done, number[kind, i] + 1)
                return bank(kind, i)

            v = nc.vector
            dve.wait_ge(th_c, 1)
            link(v.scalar_tensor_tensor(out=cnd[:, 1, :], in0=cnd[:, 1, :], scalar=1.0, in1=cnd[:, 0, :],
                                        op0=ALU.add, op1=ALU.mult))
            link(v.tensor_scalar(cnd[:, 2, :], cnd[:, 1, :], 0.5, None, ALU.mult))
            dve.wait_ge(ss_ok, 1)
            v.reciprocal(rstd, ss).then_inc(rstd_ok, 1)
            v.tensor_copy(svT[:, :], job("sv")[:, 0:28]).then_inc(by_vec, 1)

            def ada(j):
                n = place["a", j]
                dve.wait_ge(piece_in[n % FR], 16 * (n // FR + 1))
                if j == 8:
                    dve.wait_ge(job_done, number["z", PG - 1] + 1)
                w, a = piece("a", j), acc[j]
                link(v.tensor_scalar(a, w[:, 0, :], cnd[:, 2, 0:1], None, ALU.mult))
                for k in range(1, KD):
                    ins = v.scalar_tensor_tensor(out=a, in0=w[:, k, :], scalar=cnd[:, 2, k:k + 1], in1=a,
                                                 op0=ALU.mult, op1=ALU.add)
                    if k < KD - 1:
                        link(ins)
                    else:
                        ins.then_inc(acc_ok, 1)

            for j in range(4):
                ada(j)
            b_ = job("adac")
            v.tensor_tensor(sh1c, b_[:, 0:8], svT[:, 0:8], ALU.add)
            link(v.tensor_tensor(A1, b_[:, 8:16], svT[:, 8:16], ALU.add))
            v.scalar_tensor_tensor(out=A1, in0=A1, scalar=1.0, in1=svT[:, 16:24], op0=ALU.add,
                                   op1=ALU.mult).then_inc(by_vec, 1)
            dve.wait_ge(by_vec, emptied[number["adac", 0]])
            dve.wait_ge(by_act, emptied[number["xT", 7]])
            for k in range(KD):
                v.tensor_scalar(hT[:, k, :], hT[:, k, :], A1[:, k:k + 1], sh1c[:, k:k + 1], ALU.mult,
                                ALU.add).then_inc(hT_ok, 1)
            dve.wait_ge(kvg_in, 16)
            for ch in range(C):
                b_ = job("tok", ch)
                dve.wait_ge(ss2_ok, ch + 1)
                if ch >= 2:
                    dve.wait_ge(job_done, number["tr", ch - 2] + 1)
                link(v.reciprocal(rstd2[:, ch:ch + 1], ss2[:, ch:ch + 1]))
                v.scalar_tensor_tensor(out=ckv[:, ch, :], in0=b_[:, 0:LAT], scalar=rstd2[:, ch:ch + 1],
                                       in1=kvgb[:, :], op0=ALU.mult, op1=ALU.mult)
                v.tensor_copy(qk[:, ch % 2, 0:P], b_[:, LAT:LAT + P])
                v.tensor_copy(qk[:, ch % 2, P:2 * P].rearrange("p (a d) -> p a d", a=IH),
                              b_[:, 2 * P:2 * P + IDIM].rearrange("p (a d) -> p a d", a=1).broadcast_to([P, IH, IDIM]))
                v.tensor_scalar(wi[:, ch, :], b_[:, 2 * P + IDIM:2 * P + IDIM + IH], IDX_SCALE, None,
                                ALU.mult).then_inc(by_vec, 1)
            dve.wait_ge(by_vec, emptied[number["tok", C - 1]])

            relus = [0]

            def select(ch):
                n = P * (ch + 1)
                s = score[:, 0:n]
                for h in range(IH):
                    dve.wait_ge(by_act, emptied[number["idx", 4 * ch + h]])
                    r = relu[:, relus[0] % 2, 0:n]
                    w = wi[:, ch, h:h + 1]
                    if h == 0:
                        ins = v.tensor_scalar(s, r, w, None, ALU.mult)
                    else:
                        ins = v.scalar_tensor_tensor(out=s, in0=r, scalar=w, in1=s, op0=ALU.mult, op1=ALU.add)
                    relus[0] += 1
                    ins.then_inc(relu_used, 1)
                    dve.wait_ge(relu_used, relus[0])
                link(v.tensor_tensor(score[:, n - P:n], score[:, n - P:n], causal[:, :], ALU.add))
                for _ in range(K_SEL // 8):
                    link(v.max(out=top8[:, :], in_=s))
                    link(v.match_replace(out=s, in_to_replace=top8[:, :], in_values=s, imm_value=TAKEN))
                link(v.tensor_scalar(bias_of[ch], s, 2 * MASKED, HIDDEN, ALU.is_gt, ALU.mult))

            dve.wait_ge(consts, 2)
            dve.wait_ge(cnt_ok, 1)
            v.reciprocal(icnt[:, :, :], icnt[:, :, :]).then_inc(icnt_ok, 1)
            select(1)
            ada(4)
            ada(5)
            select(2)
            ada(6)
            ada(7)
            select(3)
            dve.drain().then_inc(select_ok, 1)

            def ada_rows(j):
                r, half = (j - 4) // 2, (j - 4) % 2
                row = small[32 * r:32 * r + 1, 1536 * half:1536 * half + CH]
                v.tensor_tensor(row, job("row", j)[32 * r:32 * r + 1, :], row, ALU.add).then_inc(by_vec, 1)

            dve.wait_ge(d_ok, PG)
            for g in range(8):
                ch = g // 2
                n = P * (ch + 1)
                for i in range(4):
                    s = 4 * g + i
                    v.tensor_tensor_reduce(out=Lt[:, i, 0:n], in0=job("L", s)[:, 0:n], in1=bias_of[ch], scale=1.0,
                                           scalar=-3.0e38, op0=ALU.add, op1=ALU.max,
                                           accum_out=am[:, 0, s:s + 1]).then_inc(by_vec, 1)
                    dve.wait_ge(by_vec, emptied[number["L", s]])
                    v.tensor_scalar(am[:, 1, s:s + 1], am[:, 0, s:s + 1], -SCALE, None, ALU.mult).then_inc(max_ok, 1)
                for i in range(4):
                    s = 4 * g + i
                    dve.wait_ge(exp_ok, s + 1)
                    link(v.reciprocal(am[:, 3, s:s + 1], am[:, 2, s:s + 1]))
                    v.tensor_scalar(Lt[:, i, 0:n], Lt[:, i, 0:n], am[:, 3, s:s + 1], None,
                                    ALU.mult).then_inc(prob_ok, 1)
                if g == 1:
                    dve.wait_ge(brow_in, 32)
                    for j in range(4, 8):
                        ada_rows(j)
                if 3 <= g < 7:
                    ada(g + 5)
            for j in range(8, 12):
                ada_rows(j)
            for m in range(KD):
                b_ = job("B", m)
                dve.wait_ge(by_act, emptied[number["gb", m]])
                v.scalar_tensor_tensor(out=mT[:, m, :], in0=mT[:, m, :], scalar=1.0, in1=b_, op0=ALU.add,
                                       op1=ALU.mult).then_inc(by_vec, 1)
            for m in range(KD):
                b_ = job("A", m)
                dve.wait_ge(by_act, emptied[number["ga", m]])
                t = relu[:, m % 2, :]
                link(v.scalar_tensor_tensor(out=t, in0=t, scalar=1.0, in1=b_, op0=ALU.add, op1=ALU.mult))
                v.tensor_tensor(mT[:, m, :], mT[:, m, :], t, ALU.add).then_inc(by_vec, 1)
            dve.wait_ge(rows_in, 64)
            link(v.scalar_tensor_tensor(out=A2b, in0=A2b, scalar=1.0, in1=n2b, op0=ALU.add, op1=ALU.mult))

            def h2_rows(ch):
                dve.wait_ge(ss3_ok, ch + 1)
                link(v.reciprocal(rstd3[:, ch:ch + 1], ss3[:, ch:ch + 1]))
                link(v.scalar_tensor_tensor(out=h2[:, ch, :], in0=X[:, ch, :], scalar=rstd3[:, ch:ch + 1],
                                            in1=A2b, op0=ALU.mult, op1=ALU.mult))
                v.tensor_tensor(h2[:, ch, :], h2[:, ch, :], sh2b, ALU.add).then_inc(h2_ok, 1)

            for ch in range(C):
                if ch:
                    h2_rows(ch - 1)
                for half in range(2):
                    b_ = job("out", 2 * ch + half)
                    sl = slice(half * CH, (half + 1) * CH)
                    t = relu[:, half, :]
                    link(v.scalar_tensor_tensor(out=t, in0=b_, scalar=0.5, in1=g1b[:, sl], op0=ALU.mult,
                                                op1=ALU.mult))
                    v.tensor_tensor(X[:, ch, sl], X[:, ch, sl], t, ALU.add).then_inc(by_vec, 1)
            dve.wait_ge(by_vec, emptied[number["out", 2 * C - 1]])
            h2_rows(C - 1)

            v.tensor_copy(lg[:, :, 0:NE], job("rt")[:, 0:C * NE].rearrange("p (c e) -> p c e", c=C)).then_inc(by_vec, 1)
            dve.wait_ge(by_vec, emptied[number["rt", 0]])
            for ch in range(C):
                last = v.max(out=m8[:, ch, :], in_=lg[:, ch, 0:NE])
            link(last)
            v.tensor_scalar(nm1[:, :], m8[:, :, 0], -1.0, None, ALU.mult).then_inc(nm_ok, 1)
            link(v.memset(m8[:, :, TOPK:8], MASKED))
            for ch in range(C):
                last = v.match_replace(out=lr[:, ch, :], in_to_replace=m8[:, ch, :], in_values=lg[:, ch, :],
                                       imm_value=TAKEN)
            link(last)
            link(v.tensor_scalar(mask[:, :, :], lr[:, :, 0:NE], 2 * MASKED, None, ALU.is_lt))
            v.tensor_copy(maskh[:, :, :], mask[:, :, :]).then_inc(mask_ok, 1)
            dve.wait_ge(ex_ok, C)
            link(v.tensor_tensor(wts[:, :, :], ex[:, :, :], mask[:, :, :], ALU.mult))
            link(v.reduce_sum(sm[:, 0, :], wts[:, :, :], axis=AX.X))
            link(v.reciprocal(sm[:, 1, :], sm[:, 0, :]))
            for ch in range(C):
                last = v.tensor_scalar(wts[:, ch, :], wts[:, ch, :], sm[:, 1, ch:ch + 1], None, ALU.mult)
            link(last)
            v.tensor_scalar(wth[:, :, :], wts[:, :, :], 0.5, None, ALU.mult).then_inc(wt_ok, 1)
            b_ = job("rank")
            v.tensor_reduce(cmax[:, :], b_[:, C * NE:(C + 1) * NE], op=ALU.max, axis=AX.X)
            link(v.scalar_tensor_tensor(out=rankm[:, :, :], in0=b_[:, 0:C * NE].rearrange("p (c e) -> p c e", c=C),
                                        scalar=1.0, in1=mask[:, :, :], op0=ALU.add, op1=ALU.mult))
            v.tensor_copy(cmaxi[:, :], cmax[:, :])
            v.tensor_scalar(rankm[:, :, :], rankm[:, :, :], -1.0, None, ALU.add).then_inc(by_vec, 1)
            dve.wait_ge(by_vec, emptied[number["rank", 0]])

            def token_rows(b_, lo, n):
                b_ = b_.rearrange("p (e a) -> p e a", a=3)
                v.tensor_scalar(ixa[:, 0, lo:lo + n], b_[:, :, 2], -NOWHERE, NOWHERE, ALU.mult, ALU.add)
                link(v.tensor_scalar(ixa[:, 1, lo:lo + n], b_[:, :, 0], float(P), None, ALU.mult))
                link(v.tensor_tensor(ixa[:, 1, lo:lo + n], b_[:, :, 1], ixa[:, 1, lo:lo + n], ALU.add))
                return v.tensor_tensor(idx[:, lo:lo + n], ixa[:, 0, lo:lo + n], ixa[:, 1, lo:lo + n], ALU.add)

            for e in range(NE):
                for ch in range(C):
                    n = e * C + ch
                    if n >= OHN:
                        dve.wait_ge(oh_used, n // C - OHN // C + 1)
                    v.tensor_scalar(oh[:, n % OHN, :], iota[:, :], rankm[:, ch, e:e + 1], None,
                                    ALU.is_equal).then_inc(oh_ok, 1)
                if e == 3:
                    dve.wait_ge(oh_used, 2)
                    token_rows(bank("ix", 0)[:, 0:6], 0, 2).then_inc(idx_ok, 1)
            dve.wait_ge(oh_used, NE)
            token_rows(bank("ix", 1)[:, 0:3 * (NE - 2)], 2, NE - 2).then_inc(idx_ok, 1)

            with dve.Fori(0, NE) as e:
                dve.wait_ge(gu_done, e * 2 + 1)
                v.tensor_scalar(gt, ps[:, 0, :], LIMIT, None, ALU.min).then_inc(gt_ok, 1)
                dve.wait_ge(gu_done, e * 2 + 2)
                v.tensor_scalar(up1, ps[:, 1, :], LIMIT, -LIMIT, ALU.min, ALU.max).then_inc(up_ok, 1)
                dve.wait_ge(up_ok, e + 1)
                v.scalar_tensor_tensor(out=up1, in0=up1, scalar=1.0, in1=gt, op0=ALU.add,
                                       op1=ALU.mult).then_inc(prod_ok, 1)
                dve.wait_ge(prod_ok, e + 1)
                dve.wait_ge(th_ok, e + 1)
                v.scalar_tensor_tensor(out=av, in0=th, scalar=1.0, in1=up1, op0=ALU.add,
                                       op1=ALU.mult).then_inc(av_ok, 1)

            most = dve.value_load(cmaxi[0:1, 0:1], min_val=0, max_val=T)
            with dve.If(most > slots):
                with dve.Fori(0, OVER) as r:
                    v.tensor_scalar(rankm[:, :, :], rankm[:, :, :], -float(slots), None, ALU.add).then_inc(ov_rk, 1)
                    dve.wait_ge(ov_rk, r + 1)
                    dve.sem_inc(dve_steps, 1)
                    with dve.Fori(0, NE) as e:
                        n = r * NE + e
                        dve.wait_ge(ov_go, n + 1)
                        for ch in range(C):
                            last = v.tensor_scalar(oh[:, ch, :], iota[:, :], rankm[:, ch, bass.ds(e, 1)], None,
                                                   ALU.is_equal)
                        last.then_inc(ov_oh, 1)
                        dve.wait_ge(ov_ix, n + 1)
                        b_ = ps[:, 7, :]
                        v.tensor_scalar(ixa[:, 0, 0:1], b_[:, 2:3], -NOWHERE, NOWHERE, ALU.mult, ALU.add)
                        v.tensor_scalar(ixa[:, 1, 0:1], b_[:, 0:1], float(P), None, ALU.mult).then_inc(ov_i1, 1)
                        dve.wait_ge(ov_i1, n * 2 + 1)
                        v.tensor_tensor(ixa[:, 1, 0:1], b_[:, 1:2], ixa[:, 1, 0:1], ALU.add).then_inc(ov_i1, 1)
                        dve.wait_ge(ov_i1, n * 2 + 2)
                        v.tensor_tensor(iug[:, 0:1], ixa[:, 0, 0:1], ixa[:, 1, 0:1], ALU.add).then_inc(ov_idx, 1)
                        dve.wait_ge(ov_gu, n * 2 + 1)
                        v.tensor_scalar(gt, ps[:, 0, :], LIMIT, None, ALU.min).then_inc(ov_gt, 1)
                        dve.wait_ge(ov_gu, n * 2 + 2)
                        v.tensor_scalar(up1, ps[:, 1, :], LIMIT, -LIMIT, ALU.min, ALU.max).then_inc(ov_up, 1)
                        dve.wait_ge(ov_up, n * 2 + 1)
                        v.scalar_tensor_tensor(out=up1, in0=up1, scalar=1.0, in1=gt, op0=ALU.add,
                                               op1=ALU.mult).then_inc(ov_up, 1)
                        dve.wait_ge(ov_up, n * 2 + 2)
                        dve.wait_ge(ov_th, n + 1)
                        v.scalar_tensor_tensor(out=av, in0=th, scalar=1.0, in1=up1, op0=ALU.add,
                                               op1=ALU.mult).then_inc(ov_av, 1)

            dve.wait_ge(g2_in, 16)
            for ch in range(C):
                for half in range(2):
                    sl = slice(half * CH, (half + 1) * CH)
                    t = relu[:, half, :]
                    dve.wait_ge(yb_done, 2 * ch + half + 1)
                    link(v.tensor_tensor(t, ps[:, (2 * ch + half) % 8, :], g2b[:, sl], ALU.mult))
                    link(v.tensor_tensor(X[:, ch, sl], X[:, ch, sl], t, ALU.add))
            dve.wait_ge(y_in, 16)
            dve.wait_ge(fg_in, 16)

            def result(ch):
                dve.wait_ge(ss4_ok, ch + 1)
                link(v.reciprocal(rstd4[:, ch:ch + 1], ss4[:, ch:ch + 1]))
                v.scalar_tensor_tensor(out=res[:, ch, :], in0=X[:, ch, :], scalar=rstd4[:, ch:ch + 1], in1=fgb,
                                       op0=ALU.mult, op1=ALU.mult).then_inc(res_ok, 1)

            for ch in range(C):
                link(v.tensor_tensor(Yin[:, ch, :], Yin[:, ch, :], g2b, ALU.mult))
                v.tensor_tensor(X[:, ch, :], X[:, ch, :], Yin[:, ch, :], ALU.add).then_inc(x2_ok, 1)
                if ch:
                    result(ch - 1)
            dve.wait_ge(x2_ok, C)
            result(C - 1)

        @block.tensor
        def _(pe):
            mm = nc.tensor.matmul

            def start(kind, i=0):
                n = number[kind, i]
                if n >= 8:
                    pe.wait_ge(by_act if JOBS[n - 8][2] == "A" else by_vec, emptied[n - 8])
                return bank(kind, i)

            def have(kind, i=0):
                n = place[kind, i]
                pe.wait_ge(piece_in[n % FR], 16 * (n // FR + 1))
                return piece(kind, i)

            def chain(out_, pairs, done=None, by=1, start_=True):
                for n, (a, b) in enumerate(pairs):
                    last = mm(out_, a, b, start=(n == 0 and start_), stop=(n == len(pairs) - 1))
                if done is not None:
                    last.then_inc(done, by)
                return last

            def emptied_by(kind, i=0):
                n = number[kind, i]
                pe.wait_ge(by_act if JOBS[n][2] == "A" else by_vec, emptied[n])

            pe.wait_ge(consts, 1)
            pe.wait_ge(sv_in, 48)
            nc.tensor.transpose(start("sv")[:, 0:28], sv[:, :], ident[0:28, 0:28]).then_inc(job_done, 1)
            b_ = start("uk")
            pe.wait_ge(uk_in, 16)
            for i in range(4):
                last = nc.tensor.transpose(b_[:, i * P:(i + 1) * P], uk[:, i * P:(i + 1) * P], ident[:, :])
            last.then_inc(job_done, 1)
            for i in range(8):
                ch, half = i // 2, i % 2
                b_ = start("xT", i)
                pe.wait_ge(xn_ok, ch + 1)
                for k in range(4):
                    at = (4 * half + k) * P
                    last = nc.tensor.transpose(b_[:, k * P:(k + 1) * P], xn[:, ch, at:at + P], ident[:, :])
                last.then_inc(job_done, 1)
            b_ = start("adac")
            for j in range(4):
                pe.wait_ge(acc_ok, j + 1)
                for q in range(4):
                    last = mm(b_[:, 4 * j + q:4 * j + q + 1], acc[j][:, q * P:(q + 1) * P], ones[:, 0:1],
                              start=True, stop=True)
            last.then_inc(job_done, 1)
            w = have("tok")
            for ch in range(C):
                b_ = start("tok", ch)
                for k in range(KD):
                    pe.wait_ge(hT_ok, k + 1)
                    last = mm(b_[:, 0:TOKW], hT[:, k, ch * P:(ch + 1) * P], w[:, k, :], start=(k == 0), stop=(k == KD - 1))
                last.then_inc(job_done, 1)
            for ch in range(C):
                b_ = start("tr", ch)
                emptied_by("tok", ch)
                nc.tensor.transpose(b_[:, 0:P], ckv[:, ch, :], ident[:, :])
                nc.tensor.transpose(b_[:, P:2 * P], qk[:, ch % 2, 0:P], ident[:, :])
                nc.tensor.transpose(b_[:, 2 * P:3 * P], qk[:, ch % 2, P:2 * P], ident[:, :]).then_inc(job_done, 1)

            def index_chunk(ch):
                emptied_by("tr", C - 1)
                for h in range(IH):
                    b_ = start("idx", 4 * ch + h)
                    r = slice(IDIM * h, IDIM * (h + 1))
                    mm(b_[:, 0:P * (ch + 1)], qiT[r, ch * P:(ch + 1) * P], kiT[r, 0:P * (ch + 1)], start=True,
                       stop=True, tile_position=(IDIM * h, 0)).then_inc(job_done, 1)

            def by_feature(kind, i, w, m):
                b_ = start(kind, i)
                return chain(b_, [(w[:, k, m * P:(m + 1) * P], hT[:, k, :]) for k in range(KD)], job_done)

            index_chunk(1)
            w = have("q")
            for m in range(4):
                by_feature("q", m, w, m)
            for h in range(H):
                b_ = start("qlat", h)
                emptied_by("q", h // 2)
                r = slice(HD * (h % 2), HD * (h % 2) + HD)
                mm(b_, ukT[r, h // 2, :], qT[r, h // 2, :], start=True, stop=True,
                   tile_position=(HD * (h % 2), 0)).then_inc(job_done, 1)
            index_chunk(2)
            w = have("pool")
            for m in range(PG):
                by_feature("pool", m, w, m)
            index_chunk(3)
            pe.wait_ge(pool_in, 16)
            for g in range(PG):
                b_ = start("z", g)
                pe.wait_ge(d_ok, g + 1)
                mm(b_, wpool[:, g, :], dT[:, g, :], start=True, stop=True).then_inc(job_done, 1)

            def ada_sum(j):
                b_ = start("row", j)
                pe.wait_ge(acc_ok, j + 1)
                mm(b_, ones[:, :], acc[j], start=True, stop=True).then_inc(job_done, 1)

            for g in range(8):
                ch, hh = g // 2, g % 2
                n = P * (ch + 1)
                for i in range(4):
                    b_ = start("L", 4 * g + i)
                    h = 4 * hh + i
                    emptied_by("qlat", h)
                    mm(b_[:, 0:n], q_latT[:, h, ch * P:(ch + 1) * P], ckvT[:, 0:n], start=True,
                       stop=True).then_inc(job_done, 1)
                by_feature("gb", g, have("gb", g // 4), g % 4)
                for i in range(4):
                    b_ = start("PT", 4 * g + i)
                    pe.wait_ge(prob_ok, 4 * g + i + 1)
                    for s in range(ch + 1):
                        last = nc.tensor.transpose(b_[:, s * P:(s + 1) * P], Lt[:, i, s * P:(s + 1) * P], ident[:, :])
                    last.then_inc(job_done, 1)
                b_ = start("O", g)
                emptied_by("PT", 4 * g + 3)
                chain(b_, [(ckv[:, s, :], pT[:, s, :, :].rearrange("p h q -> p (h q)")) for s in range(ch + 1)], job_done)
                if hh:
                    b_ = start("V", ch)
                    pe.wait_ge(uv_in, 16 * H)
                    emptied_by("O", g)
                    for a in range(4):
                        last = chain(b_[:, a * P:(a + 1) * P],
                                     [(uvp[:, 2 * a + q, :], o_latT[:, 2 * a + q, :]) for q in range(2)])
                    last.then_inc(job_done, 1)
                if g == 1:
                    for j in range(4, 8):
                        ada_sum(j)
            for j in range(8, 12):
                ada_sum(j)
            w = have("wb")
            emptied_by("z", PG - 1)
            for m in range(KD):
                chain(start("B", m), [(w[:, k, m * P:(m + 1) * P], zT[:, k, :]) for k in range(4)], job_done)
            emptied_by("V", C - 1)
            wa = have("wa")
            for m in range(KD):
                by_feature("ga", m, have("ga", m // 4), m % 4)
                chain(start("A", m), [(wa[:, k, m * P:(m + 1) * P], oT[:, k, :]) for k in range(4)], job_done)

            def h2_turn(ch):
                pe.wait_ge(h2_ok, ch + 1)
                for half in range(2):
                    b_ = start("h2T", 2 * ch + half)
                    for k in range(4):
                        at = (4 * half + k) * P
                        last = nc.tensor.transpose(b_[:, k * P:(k + 1) * P], h2[:, ch, at:at + P], ident[:, :])
                    last.then_inc(job_done, 1)

            wo = [have("wo", half) for half in range(2)]
            for ch in range(C):
                for half in range(2):
                    b_ = start("out", 2 * ch + half)
                    for k in range(KD):
                        emptied_by("A", k)
                        last = mm(b_, mT[:, k, ch * P:(ch + 1) * P], wo[half][:, k, :], start=(k == 0), stop=(k == KD - 1))
                    last.then_inc(job_done, 1)
                if ch:
                    h2_turn(ch - 1)
            h2_turn(C - 1)
            b_ = start("rout")
            emptied_by("h2T", 7)
            pe.wait_ge(wr_in, 32)
            chain(b_[0:NE, :], [(wr[:, k, :], h2T[:, k, :]) for k in range(KD)], job_done)
            b_ = start("rt")
            emptied_by("rout")
            for ch in range(C):
                last = nc.tensor.transpose(b_[:, ch * NE:(ch + 1) * NE], lgT[:, ch * P:(ch + 1) * P], ident[0:NE, 0:NE])
            last.then_inc(job_done, 1)
            b_ = start("rank")
            pe.wait_ge(mask_ok, 1)
            pe.wait_ge(consts, 2)
            for ch in range(C):
                chain(b_[:, ch * NE:(ch + 1) * NE], [(onesb[:, :], maskh[:, k, :]) for k in range(ch)]
                      + [(tri[:, :], maskh[:, ch, :])])
            chain(b_[:, C * NE:(C + 1) * NE], [(onesb[:, :], maskh[:, k, :]) for k in range(C)], job_done)
            for part, lo, hi in ((0, 0, 2), (1, 2, NE)):
                b_ = start("ix", part)
                for e in range(lo, hi):
                    at = 3 * (e - lo)
                    for ch in range(C):
                        n = e * C + ch
                        pe.wait_ge(oh_ok, n + 1)
                        last = mm(b_[:, at:at + 3], oh[:, n % OHN, :], tokid[:, ch, :], start=(ch == 0), stop=(ch == C - 1))
                    last.then_inc(oh_used, 1)

            pe.wait_ge(idx_ok, 2)
            pe.wait_ge(b3_ok, 1)

            def turn_rows(b, done):
                for k in range(KD):
                    last = nc.tensor.transpose(ps[:, 4 + k // 4, (k % 4) * P:(k % 4 + 1) * P],
                                               XG[:, b, k * P:(k + 1) * P], ident[:, :])
                last.then_inc(done, 1)

            def up_half(e, half, w, done, used=None):
                pe.wait_ge(b3_ok, 1)
                mm(ps[:, half, :], sel3[:, bass.ds(e, 1)].broadcast_to([3 * NE, P]), b3[:, half * CH:(half + 1) * CH],
                   start=True, stop=False)
                for k in range(KD):
                    last = mm(ps[:, half, :], xgT[:, k, :], w[:, k, :], start=False, stop=(k == KD - 1))
                last.then_inc(done, 1)

            def turn_act(done):
                for k in range(KF):
                    last = nc.tensor.transpose(ps[:, 6, k * P:(k + 1) * P], av[:, k * P:(k + 1) * P], ident[:, :])
                last.then_inc(done, 1)

            def down(w, done):
                for half in range(2):
                    for k in range(KF):
                        last = mm(ps[:, 2 + half, :], actT[:, k, :], w[:, k, half * CH:(half + 1) * CH],
                                  start=(k == 0), stop=(k == KF - 1))
                last.then_inc(done, 1)

            front_of = [sum(1 for n in range(NFP) if n % FR == s) for s in range(FR)] + [0, 0]

            def expert(e, b, half_e, first=False, last=False):
                w = slot3(3 * b)
                pe.wait_ge(xgT_ok, e + 1)
                for half in range(2):
                    pe.wait_ge(piece_in[3 * b + half], half_e * 16 + 16 * (front_of[3 * b + half] + 1))
                    up_half(e, half, w[half], gu_done)
                if not last:
                    pe.wait_ge(xg_in[1 - b], (half_e + b) * 16 + 16)
                    turn_rows(1 - b, tx_done)
                if not first:
                    pb = 1 - b
                    pe.wait_ge(piece_in[3 * pb + 2], (half_e + b - 1) * 16 + 16 * (front_of[3 * pb + 2] + 1))
                    pe.wait_ge(actT_ok, e)
                    if not isinstance(e, int) or e > 1:
                        pe.wait_ge(y_ok, e - 1)
                    down(slot3(3 * pb)[2], dn_done)
                pe.wait_ge(av_ok, e + 1)
                turn_act(ta_done)

            pe.wait_ge(xg_in[0], 16)
            turn_rows(0, tx_done)
            expert(0, 0, 0, first=True)
            expert(1, 1, 0)
            with pe.Fori(1, NE // 2 - 1) as i:
                expert(i * 2, 0, i)
                expert(i * 2 + 1, 1, i)
            expert(NE - 2, 0, NE // 2 - 1)
            expert(NE - 1, 1, NE // 2 - 1, last=True)
            pe.wait_ge(actT_ok, NE)
            pe.wait_ge(y_ok, NE - 1)
            pe.wait_ge(piece_in[5], 16 * (NE // 2))
            down(slot3(3)[2], dn_done)

            most = pe.value_load(cmaxi[0:1, 0:1], min_val=0, max_val=T)
            with pe.If(most > slots):
                with pe.Fori(0, OVER) as r:
                    with pe.Fori(0, NE) as e:
                        n = r * NE + e
                        pe.wait_ge(ov_oh, n + 1)
                        for ch in range(C):
                            last = mm(ps[:, 7, 0:3], oh[:, ch, :], tokid[:, ch, :], start=(ch == 0), stop=(ch == C - 1))
                        last.then_inc(ov_ix, 1)
                        pe.wait_ge(ov_xg, n * 16 + 16)
                        turn_rows(0, ov_tx)
                        pe.wait_ge(ov_xt, n + 1)
                        pe.wait_ge(ov_w, n * 48 + 48)
                        w = slot3(0)
                        for half in range(2):
                            up_half(e, half, w[half], ov_gu)
                        pe.wait_ge(ov_av, n + 1)
                        turn_act(ov_ta)
                        pe.wait_ge(ov_at, n + 1)
                        down(w[2], ov_dn)
                pe.wait_ge(ov_y, OVER * NE)

            pe.wait_ge(wt_ok, 1)
            for ch in range(C):
                last = nc.tensor.transpose(ps[0:NE, 7, ch * P:(ch + 1) * P], wts[:, ch, :], ident[:, :])
            last.then_inc(wtT_done, 1)
            pe.wait_ge(wtT_ok, 1)
            pe.wait_ge(bd_in, 16)
            pe.wait_ge(y_ok, NE)
            for ch in range(C):
                for half in range(2):
                    mm(ps[:, (2 * ch + half) % 8, :], wtT[:, ch * P:(ch + 1) * P], bdn[:, half, :], start=True,
                       stop=True).then_inc(yb_done, 1)


_INS = ['x', 'c', 'norm1_g', 'norm2_g', 'w_ada', 'b_ada', 'w_in', 'kv_norm_g', 'w_uk', 'w_uv', 'w_pool',
        'pool_scale', 'w_a_up', 'w_b_up', 'w_out', 'w_router', 'b_router', 'w_gu', 'b_gu', 'w_down', 'b_down',
        'final_g']


def kernel(**inputs):
    import numpy as _np
    import concourse.bacc as _bacc
    from concourse import mybir as _mybir
    from concourse.bass_utils import run_bass_kernel_spmd as _run

    nc = _bacc.Bacc("TRN2", target_bir_lowering=False, num_devices=1)
    arrays, args = {}, []
    for name in _INS:
        a = _np.ascontiguousarray(inputs[name])
        arrays[f"in_{name}_dram"] = a
        args.append(nc.dram_tensor(f"in_{name}_dram", a.shape, _mybir.dt.from_np(a.dtype), kind="ExternalInput").ap())
    args.append(nc.dram_tensor("out_0_dram", (1, T, D), F32, kind="ExternalOutput").ap())
    trunk(nc, *args)
    r = _run(nc, [arrays], core_ids=[0])
    return r.results[0]["out_0_dram"]
```

```python
from contextlib import ExitStack

import concourse.bass as bass
from concourse import mybir
from concourse.alu_op_type import AluOpType as ALU

F32 = mybir.dt.float32
BF16 = mybir.dt.bfloat16
F32R = mybir.dt.float32r
U32 = mybir.dt.uint32
ACT = mybir.ActivationFunctionType
AX = mybir.AxisListType

P = 128
T, D = 512, 1024
C = T // P
KD = D // P
H, HD = 8, 64
AW = H * HD
LAT = 128
IH, IDIM = 4, 32
PG = 4
WINDOWS = (2, 4, 8, 16)
PAD = 16
PW = PG * P
NE, TOPK, DFF = 32, 4, 512
KF = DFF // P
LIMIT, ALPHA, EPS = 7.0, 1.702, 1e-6
K_SEL = min(256, T // 4)
SCALE = HD ** -0.5
IDX_SCALE = (IH ** -0.5) * (IDIM ** -0.5)
COL_Q, COL_TOK = 0, AW
TOKW = LAT + IH * IDIM + IDIM + IH
COL_POOL = COL_TOK + TOKW
COL_GA = COL_POOL + PW
COL_GB = COL_GA + D

MASKED = -1e38
TAKEN = -3e38
HIDDEN = -1e30
NOWHERE = 4096.0

SLOTS = 96
HX = D + NE
CH = 512
GK = 2
GP = KD // GK
NG = 4


def trunk(nc, x, c, norm1_g, norm2_g, w_ada, b_ada, w_in, kv_norm_g, w_uk, w_uv, w_pool, pool_scale,
          w_a_up, w_b_up, w_out, w_router, b_router, w_gu, b_gu, w_down, b_down, final_g, out,
          slots=SLOTS, until=None):
    ctx = ExitStack()
    with ctx:
        def sb(name, shape, dt=F32):
            return ctx.enter_context(nc.sbuf_tensor(name, shape, dt))

        def sem(name):
            return ctx.enter_context(nc.semaphore(name))

        h2_dram = nc.dram_tensor("h2_rows", (T, HX), F32).ap()
        y_dram = nc.dram_tensor("moe_rows", (T, D), F32).ap()
        ada_dram = nc.dram_tensor("ada_rows", (4, D), F32).ap()

        ring = sb("ring", [P, 4, 4096])
        X = sb("X", [P, C, D])
        mix = sb("mix", [P, 4096])
        attn = sb("attn", [P, 5184])
        small = sb("small", [P, 2048])
        apad = sb("apad", [P, PG, PAD + T])
        T3 = sb("T3", [P, 3, T])
        ckv = sb("ckv", [P, C, LAT])
        wi = sb("wi", [P, C, IH])
        uvp = sb("uvp", [P, H, P])
        maskb = sb("maskb", [P, 1280])
        icnt = sb("icnt", [P, PG, PAD])
        ident = sb("ident", [P, P])
        ones = sb("ones", [P, P])
        iota = sb("iota", [P, P], BF16)
        tri = sb("tri", [P, P], BF16)
        onesb = sb("onesb", [P, P], BF16)
        tokid = sb("tokid", [P, C, 3], BF16)
        causal = sb("causal", [P, P])
        kvgb = sb("kvgb", [P, LAT])
        sv = sb("sv", [28, P])
        svT = sb("svT", [P, 28])
        cnd = sb("cnd", [P, 3, KD])
        col = sb("col", [P, 64])
        am = sb("am", [P, 4, C * H])
        top8 = sb("top8", [P, 8])
        wr = sb("wr", [P, KD, NE])
        br = sb("br", [NE, 1])
        lg = sb("lg", [P, C, NE + 8])
        m8 = sb("m8", [P, C, 8])
        nm1 = sb("nm1", [P, C])
        mask = sb("mask", [P, C, NE])
        maskh = sb("maskh", [P, C, NE], BF16)
        sm = sb("sm", [P, 2, C])
        wts = sb("wts", [P, C, NE])
        wth = sb("wth", [P, C, NE])
        rankm = sb("rankm", [P, C, NE])
        ixa = sb("ixa", [P, 2, NE])
        idx = sb("idx", [P, NE], U32)
        cmax = sb("cmax", [P, 1])
        cmaxi = sb("cmaxi", [P, 1], U32)
        sel3 = sb("sel3", [3 * NE, NE], BF16)
        WC = sb("WC", [P, 2])
        iug = sb("iug", [P, 2], U32)
        ius = sb("ius", [P, 2], U32)
        ps = ctx.enter_context(nc.psum_tensor("ps", [P, 8, CH], F32))
        early = ExitStack()
        hT = early.enter_context(nc.sbuf_tensor("hT", [P, KD, T], F32))
        area_b = early.enter_context(nc.sbuf_tensor("area_b", [P, 4096], F32))
        area_a = early.enter_context(nc.sbuf_tensor("area_a", [P, 4096], F32))
        early.close()
        late = sb("late", [P, 4, T])
        xhl = sb("xhl", [P, 2, KD, P], F32R)[:, :, :, 0:slots]
        whl = sb("whl", [P, NG, 2, GK, CH], F32R)

        q_latT = area_a[:, :].rearrange("p (h t) -> p h t", h=H)
        xn = area_a[:, :].rearrange("p (c d) -> p c d", c=C)
        zT = area_b[:, 0:2048].rearrange("p (g t) -> p g t", g=PG)
        qT = area_b[:, 2048:4096].rearrange("p (g t) -> p g t", g=PG)
        dT = qT
        h2 = area_a[:, :].rearrange("p (c d) -> p c d", c=C)
        acc_in = mix[:, :].rearrange("p (j n) -> p j n", j=8)
        acc = [acc_in[:, j, :] if j < 8 else dT[:, j - 8, :] for j in range(12)]
        mT = mix[:, :].rearrange("p (k t) -> p k t", k=KD)
        h2T = hT
        pT = attn[:, 0:2048].rearrange("p (s h q) -> p s h q", s=C, h=4)
        o_latT = attn[:, 2048:3072].rearrange("p (h q) -> p h q", h=H)
        Lt = attn[:, 3072:5120].rearrange("p (i s) -> p i s", i=4)
        g1b = attn[:, 0:1024]
        A2b = attn[:, 1024:2048]
        sh2b = attn[:, 2048:3072]
        g2b = attn[:, 3072:4096]
        sq = attn[:, 3072:4096]
        n2b = attn[:, 4096:5120]
        ada_half = [small[0:97:32, 0:512], small[0:97:32, 1536:2048]]
        win = attn[:, 4096:4096 + 2 * (PAD + T)].rearrange("p (i t) -> p i t", i=2)
        oT = apad[:, :, PAD:PAD + T]
        ckvT, qiT, kiT = (T3[:, i, :] for i in range(3))
        qk = area_b[:, 0:512].rearrange("p (i t) -> p i t", i=2)
        uk = small[:, 0:512]
        ukT = area_b[:, 512:1024].rearrange("p (i t) -> p i t", i=4)
        wpool = small[:, 1536:2048].rearrange("p (g d) -> p g d", g=PG)
        relu = small[:, 512:1536].rearrange("p (i s) -> p i s", i=2)
        score = small[:, 0:512]
        bias_of = [maskb[:, 64 * ch * (ch + 1):64 * ch * (ch + 1) + P * (ch + 1)] for ch in range(C)]
        sh1c, A1, ss, rstd, ss2, rstd2 = (col[:, 0:8], col[:, 8:16], col[:, 16:20], col[:, 20:24],
                                          col[:, 24:28], col[:, 28:32])
        ss3, rstd3, ss4, rstd4 = (col[:, 32 + 4 * i:36 + 4 * i] for i in range(4))
        eps = col[:, 48:49]
        t8 = col[:, 49:57]
        lgT = T3[0:NE, 2, :]
        lr = attn[:, 640:640 + C * (NE + 8)].rearrange("p (c e) -> p c e", c=C)
        ex = attn[:, 512:512 + C * NE].rearrange("p (c e) -> p c e", c=C)
        OHE = 4
        ohw = OHE * C * slots // 2
        oh = [attn[:, at:at + ohw].bitcast(BF16).rearrange("p (e c s) -> p e c s", e=OHE, c=C)
              for at in (2048, 4096)]
        b3 = small[0:3 * NE, 0:512].bitcast(BF16)
        braw = T3[0:3 * NE, 0:2, :].rearrange("p a t -> p (a t)")
        bres = uvp[0:3 * NE, :, :].rearrange("p a t -> p (a t)")
        XG = apad[:, :, :].rearrange("p g t -> p (g t)").rearrange("p (b d) -> p b d", b=2)
        xgT = mix[:, 0:KD * slots].rearrange("p (k s) -> p k s", k=KD)
        Y = mix[:, 1024:3072].rearrange("p (b d) -> p b d", b=2)
        gt = mix[0:slots, 3072:3584]
        up1 = mix[0:slots, 3584:4096]
        th = attn[0:slots, 512:1024]
        av = attn[0:slots, 1024:1536]
        actT = attn[:, 1536:1536 + KF * slots].rearrange("p (k s) -> p k s", k=KF)
        wtT = attn[0:NE, 2048:2048 + T]
        bdn = late[0:NE, 0:2, :]
        fgb = late[:, 2:4, :].rearrange("p a t -> p (a t)")
        Yin = ring[:, 0, :].rearrange("p (c d) -> p c d", c=C)
        res = ring[:, 1, :].rearrange("p (c d) -> p c d", c=C)
        zero = area_b[:, 0:512]

        def ada_piece(j):
            return w_ada[0, :, j * CH:(j + 1) * CH].rearrange("(p k) n -> p k n", k=KD)

        def in_piece(at, width):
            return w_in[0, :, at:at + width].rearrange("(k p) n -> p k n", p=P)

        PIECES = ([("a", j, ada_piece(j)) for j in range(4)]
                  + [("tok", 0, in_piece(COL_TOK, TOKW)), ("q", 0, in_piece(COL_Q, AW))]
                  + [("a", 4, ada_piece(4)), ("a", 5, ada_piece(5)), ("pool", 0, in_piece(COL_POOL, PW))]
                  + [("a", 6, ada_piece(6)), ("a", 7, ada_piece(7)), ("gb", 0, in_piece(COL_GB, CH))]
                  + [("a", 8, ada_piece(8)), ("a", 9, ada_piece(9)), ("gb", 1, in_piece(COL_GB + CH, CH))]
                  + [("a", 10, ada_piece(10)), ("a", 11, ada_piece(11))]
                  + [("wb", 0, w_b_up[0].rearrange("(k p) n -> p k n", p=P))]
                  + [("ga", i, in_piece(COL_GA + i * CH, CH)) for i in range(2)]
                  + [("wa", 0, w_a_up[0].rearrange("(k p) n -> p k n", p=P))]
                  + [("wo", i, w_out[0, :, i * CH:(i + 1) * CH].rearrange("(k p) n -> p k n", p=P))
                     for i in range(2)])
        FR = 4
        NFP = len(PIECES)
        place = {(k, i): n for n, (k, i, _) in enumerate(PIECES)}
        LAST_JOB = {("tok", 0): ("tok", C - 1), ("q", 0): ("q", 3), ("pool", 0): ("pool", PG - 1),
                    ("gb", 0): ("gb", 3), ("gb", 1): ("gb", 7), ("wb", 0): ("B", KD - 1),
                    ("ga", 0): ("ga", 3), ("ga", 1): ("ga", 7), ("wa", 0): ("A", KD - 1),
                    ("wo", 0): ("out", 2 * C - 2), ("wo", 1): ("out", 2 * C - 1)}

        def piece(kind, i=0):
            s = place[kind, i] % FR
            src = PIECES[place[kind, i]][2]
            k, n = src.shape[1], src.shape[2]
            return ring[:, s, 0:k * n].rearrange("p (k n) -> p k n", k=k)

        JOBS = ([("sv", 0, "D")]
                + [("xT", i, "A") for i in range(8)]
                + [("adac", 0, "D")]
                + [("tok", i, "D") for i in range(C)] + [("uk", 0, "A")] + [("tr", i, "A") for i in range(C)]
                + [("idx", 4 + i, "A") for i in range(4)]
                + [("q", i, "A") for i in range(4)] + [("qlat", h, "A") for h in range(H)]
                + [("idx", 8 + i, "A") for i in range(4)]
                + [("pool", i, "A") for i in range(PG)]
                + [("idx", 12 + i, "A") for i in range(4)]
                + [("z", i, "A") for i in range(PG)])
        NGR = 2 * C
        JOBS += [("L", i, "D") for i in range(4)] + [("gb", 0, "A")]
        for g in range(NGR):
            JOBS += [("PT", 4 * g + i, "A") for i in range(4)]
            if g < NGR - 1:
                JOBS += [("L", 4 * g + 4 + i, "D") for i in range(4)]
            JOBS += [("O", g, "A")]
            if g < NGR - 1:
                JOBS += [("gb", g + 1, "A")]
            if g % 2:
                JOBS += [("V", g // 2, "A")]
            if g == 1:
                JOBS += [("row", j, "D") for j in range(4, 8)]
        JOBS += [("row", j, "D") for j in range(8, 12)]
        JOBS += [("B", m, "D") for m in range(KD)]
        for m in range(KD):
            JOBS += [("ga", m, "A"), ("A", m, "D")]
        for ch in range(C):
            JOBS += [("out", 2 * ch, "D"), ("out", 2 * ch + 1, "D")]
            if ch:
                JOBS += [("h2T", 2 * ch - 2, "A"), ("h2T", 2 * ch - 1, "A")]
            if ch > 1:
                JOBS += [("rout", ch - 2, "A")]
        JOBS += [("rout", 2, "A"), ("h2T", 6, "A"), ("h2T", 7, "A"), ("rout", 3, "A"), ("rt", 0, "D"), ("rank", 0, "D"),
                 ("ix", 0, "D"), ("ix", 1, "D")]
        number = {(k, i): n for n, (k, i, _) in enumerate(JOBS)}
        emptied = [sum(1 for j in JOBS[:n + 1] if j[2] == JOBS[n][2]) for n in range(len(JOBS))]
        NJ = len(JOBS)

        def bank(kind, i=0):
            return ps[:, number[kind, i] % 8, :]

        piece_in = [sem(f"piece_in{i}") for i in range(4)]
        acc_ok = sem("acc_ok")
        job_done = sem("job_done")
        by_act, by_vec = sem("by_act"), sem("by_vec")
        c_in, x_in, sv_in, kvg_in = sem("c_in"), sem("x_in"), sem("sv_in"), sem("kvg_in")
        uk_in, uv_in, pool_in, wr_in, bg_in = (sem("uk_in"), sem("uv_in"), sem("pool_in"),
                                               sem("wr_in"), sem("bg_in"))
        brow_in, row_out, rows_in, g2_in = sem("brow_in"), sem("row_out"), sem("rows_in"), sem("g2_in")
        h2_out, wt_out, zero_out = sem("h2_out"), sem("wt_out"), sem("zero_out")
        consts, cnt_ok, icnt_ok = sem("consts"), sem("cnt_ok"), sem("icnt_ok")
        th_c = sem("th_c")
        ss_ok, rstd_ok, xn_ok = sem("ss_ok"), sem("rstd_ok"), sem("xn_ok")
        hT_ok = sem("hT_ok")
        ss2_ok, rstd2_ok, tok_ok = sem("ss2_ok"), sem("rstd2_ok"), sem("tok_ok")
        relu_used = sem("relu_used")
        d_ok = sem("d_ok")
        select_ok = sem("select_ok")
        max_ok, exp_ok, prob_ok = sem("max_ok"), sem("exp_ok"), sem("prob_ok")
        ss3_ok, h2_ok = sem("ss3_ok"), sem("h2_ok")
        nm_ok, ex_ok, wt_ok = sem("nm_ok"), sem("ex_ok"), sem("wt_ok")
        iug_ok, ius_ok, wc_ok = sem("iug_ok"), sem("ius_ok"), sem("wc_ok")
        pool_steps, dve_steps = sem("pool_steps"), sem("dve_steps")
        up_ok, prod_ok = sem("up_ok"), sem("prod_ok")
        mask_ok, oh_ok, oh_used, idx_ok = sem("mask_ok"), sem("oh_ok"), sem("oh_used"), sem("idx_ok")
        b3_ok = sem("b3_ok")
        act_chain, dve_chain, pool_chain = sem("act_chain"), sem("dve_chain"), sem("pool_chain")
        xg_clear = sem("xg_clear")
        xg_in = [sem("xg_in0"), sem("xg_in1")]
        tx_done = sem("tx_done")
        gt_ok, th_ok, av_ok = sem("gt_ok"), sem("th_ok"), sem("av_ok")
        hi_ok, lo_ok = sem("hi_ok"), sem("lo_ok")
        granule_used = sem("granule_used")
        xh_ok, xl_ok = sem("xh_ok"), sem("xl_ok")
        ta_done, actT_ok, dn_done, y_ok = sem("ta_done"), sem("actT_ok"), sem("dn_done"), sem("y_ok")
        y_added = sem("y_added")
        ov_go, ov_w, ov_oh, ov_ix, ov_idx, ov_xg = (sem("ov_" + n) for n in
                                                    ("go", "w", "oh", "ix", "idx", "xg"))
        ov_tx, ov_xt, ov_gu, ov_gt, ov_th, ov_av = (sem("ov_" + n) for n in
                                                    ("tx", "xt", "gu", "gt", "th", "av"))
        ov_ta, ov_at, ov_dn, ov_y, ov_add = (sem("ov_" + n) for n in ("ta", "at", "dn", "y", "add"))
        ov_rk, ov_i1, ov_up, ov_wc = (sem("ov_" + n) for n in ("rk", "i1", "up", "wc"))
        OVER = (T - 1) // slots
        moe_done, bd_in, fg_in, y_in = sem("moe_done"), sem("bd_in"), sem("fg_in"), [sem(f"y_in{i}") for i in range(C)]
        wtT_done, wtT_ok, yb_done = sem("wtT_done"), sem("wtT_ok"), sem("yb_done")
        x2_ok, ss4_ok, res_ok, out_done = sem("x2_ok"), sem("ss4_ok"), sem("res_ok"), sem("out_done")

        def rows(dram):
            return dram.rearrange("(c p) d -> p c d", p=P)

        def spread(row, n=D):
            return row.rearrange("(o n) -> o n", o=1).broadcast_to([P, n])

        def expert_pieces(e):
            gu = w_gu[0, bass.ds(e, 1), :, :].rearrange("a (k p) n -> p (a k) n", p=P)
            dn = w_down[0, bass.ds(e, 1), :, :].rearrange("a (k p) n -> p (a k) n", p=P)
            return gu[:, :, 0:DFF], gu[:, :, DFF:2 * DFF], dn

        SG, SU, SD = (NFP - 4) % FR, (NFP - 3) % FR, ((NFP - 2) % FR, (NFP - 1) % FR)
        gate_w, up_w = (ring[:, s, :].rearrange("p (k n) -> p k n", k=KD) for s in (SG, SU))
        down_w = [ring[:, s, :].rearrange("p (k n) -> p k n", k=KF) for s in SD]
        front_of = [sum(1 for n in range(NFP) if n % FR == s) for s in range(FR)]

        def came(eng, slot, n):
            eng.wait_ge(piece_in[slot], n * 16 + 16 * (front_of[slot] + 1))

        def turned(b):
            return ps[:, b, :].rearrange("p (k s) -> p k s", k=4)[:, :, 0:slots]

        block = ctx.enter_context(nc.Block())

        @block.sync
        def _(sp):
            sp.dma_start(cnd[:, 0, :], c[0, :].rearrange("(p k) -> p k", k=KD)).then_inc(c_in, 16)
            sp.dma_start(X[:, :, :], rows(x[0])).then_inc(x_in, 16)
            sp.dma_start(sv[0:16, :], b_ada[0, 0:2 * D].rearrange("(r n) -> r n", n=P)).then_inc(sv_in, 16)
            sp.dma_start(sv[16:24, :], norm1_g[0].rearrange("(r n) -> r n", n=P)).then_inc(sv_in, 16)
            sp.dma_start(sv[24:28, :], pool_scale[0].rearrange("(r n) -> r n", n=P)).then_inc(sv_in, 16)

            def used(n):
                kind, i, _ = PIECES[n]
                if kind == "a":
                    sp.wait_ge(acc_ok, i + 1)
                else:
                    sp.wait_ge(job_done, number[LAST_JOB[kind, i]] + 1)

            for n, (kind, i, src) in enumerate(PIECES):
                if n >= FR:
                    used(n - FR)
                sp.dma_start(piece(kind, i), src).then_inc(piece_in[n % FR], 16)
                if n == 3:
                    sp.dma_start(kvgb[:, :], spread(kv_norm_g[0], LAT)).then_inc(kvg_in, 16)
                if n == 5:
                    sp.dma_start(wr[:, :, :], w_router[0].rearrange("(k p) n -> p k n", p=P)).then_inc(wr_in, 16)
                    sp.dma_start(br[:, :], b_router[0].rearrange("(e o) -> e o", o=1)).then_inc(wr_in, 16)
            srcs = expert_pieces(0)
            for j, (slot, dst) in enumerate(((SG, gate_w), (SU, up_w), (SD[0], down_w[0]))):
                used(NFP - 4 + j)
                sp.dma_start(dst, srcs[j]).then_inc(piece_in[slot], 16)

            def load_gate(e):
                sp.wait_ge(lo_ok, e * 2 * GP - GP)
                sp.dma_start(gate_w, expert_pieces(e)[0]).then_inc(piece_in[SG], 16)

            def load_rest(e, b, first=False, last=False):
                if first:
                    used(NFP - 1)
                    sp.dma_start(down_w[b], expert_pieces(e)[2]).then_inc(piece_in[SD[b]], 16)
                sp.wait_ge(lo_ok, e * 2 * GP)
                sp.dma_start(up_w, expert_pieces(e)[1]).then_inc(piece_in[SU], 16)
                if not last:
                    load_gate(e + 1)
                if not first:
                    sp.wait_ge(dn_done, e - 1)
                    sp.dma_start(down_w[b], expert_pieces(e)[2]).then_inc(piece_in[SD[b]], 16)

            load_gate(1)
            load_rest(1, 1, first=True)
            with sp.Fori(1, NE // 2 - 1) as i:
                load_rest(i * 2, 0)
                load_rest(i * 2 + 1, 1)
            load_rest(NE - 2, 0)
            load_rest(NE - 1, 1, last=True)
            most = sp.value_load(cmaxi[0:1, 0:1], min_val=0, max_val=T)
            with sp.If(most > slots):
                with sp.Fori(0, OVER) as r:
                    with sp.Fori(0, NE) as e:
                        sp.wait_ge(ov_go, r * NE + e + 1)
                        for d_, s_ in zip((gate_w, up_w, down_w[0]), expert_pieces(e)):
                            sp.dma_start(d_, s_).then_inc(ov_w, 16)
            sp.wait_ge(job_done, number["rout", C - 1] + 1)
            sp.dma_start(bdn, b_down[0].rearrange("e (a n) -> e a n", a=2)).then_inc(bd_in, 16)
            sp.dma_start(fgb, spread(final_g)).then_inc(fg_in, 16)
            sp.wait_ge(moe_done, 1)
            for ch in range(C):
                sp.dma_start(Yin[:, ch, :], rows(y_dram)[:, ch, :]).then_inc(y_in[ch], 16)
            for ch in range(C):
                sp.wait_ge(res_ok, ch + 1)
                sp.dma_start(rows(out[0])[:, ch, :], res[:, ch, :]).then_inc(out_done, 16)
            sp.wait_ge(out_done, 16 * C)

        @block.gpsimd
        def _(pool):
            chain = [0]

            def link(ins):
                chain[0] += 1
                ins.then_inc(pool_chain, 1)
                pool.wait_ge(pool_chain, chain[0])

            nc.gpsimd.memset(ones[:, :], 1.0)
            nc.gpsimd.memset(eps, EPS)
            nc.gpsimd.memset(onesb[:, :], 1.0)
            link(nc.gpsimd.memset(ident[:, :], 0.0))
            link(nc.gpsimd.affine_select(out=ident[:, :], in_=ident[:, :], compare_op=ALU.not_equal, fill=1.0,
                                         base=0, pattern=[[-1, P]], channel_multiplier=1))
            nc.gpsimd.drain().then_inc(consts, 1)
            link(nc.gpsimd.memset(uvp[:, :, :], 0.0))
            link(nc.gpsimd.memset(causal[:, :], 0.0))
            nc.gpsimd.affine_select(out=causal[:, :], in_=causal[:, :], compare_op=ALU.is_ge, fill=MASKED,
                                    base=0, pattern=[[-1, P]], channel_multiplier=1)
            link(nc.gpsimd.memset(bias_of[0], 0.0))
            nc.gpsimd.affine_select(out=bias_of[0], in_=bias_of[0], compare_op=ALU.is_ge, fill=HIDDEN,
                                    base=0, pattern=[[-1, P]], channel_multiplier=1)
            nc.gpsimd.affine_select(out=tri[:, :], in_=onesb[:, :], compare_op=ALU.is_gt, fill=0.0,
                                    base=0, pattern=[[1, P]], channel_multiplier=-1)
            nc.gpsimd.iota(iota[:, :], pattern=[[1, P]], base=0, channel_multiplier=0,
                           allow_small_or_imprecise_dtypes=True)
            nc.gpsimd.iota(tokid[:, :, 0], pattern=[[1, C]], base=0, channel_multiplier=0,
                           allow_small_or_imprecise_dtypes=True)
            nc.gpsimd.iota(tokid[:, :, 1], pattern=[[0, C]], base=0, channel_multiplier=1,
                           allow_small_or_imprecise_dtypes=True)
            nc.gpsimd.memset(tokid[:, :, 2], 1.0)
            link(nc.gpsimd.memset(sel3[:, :], 0.0))
            for part in range(3):
                link(nc.gpsimd.affine_select(out=sel3[:, :], in_=sel3[:, :], compare_op=ALU.not_equal, fill=1.0,
                                             base=-part * NE, pattern=[[-1, NE]], channel_multiplier=1))
            for g in range(PG):
                nc.gpsimd.iota(icnt[:, g, :], pattern=[[1, PAD]], base=1, channel_multiplier=0,
                               allow_small_or_imprecise_dtypes=True)
            nc.gpsimd.memset(lg[:, :, :], MASKED)
            nc.gpsimd.memset(apad[:, :, 0:PAD], 0.0)
            nc.gpsimd.memset(win[:, :, 0:PAD], 0.0)
            nc.gpsimd.drain().then_inc(consts, 1)
            pool.wait_ge(piece_in[place["tok", 0] % FR], 16 * (place["tok", 0] // FR + 1))
            pool.dma_start(uk, w_uk[0].rearrange("l h d -> l (h d)")).then_inc(uk_in, 16)
            pool.dma_start(wpool, w_pool[0].rearrange("g c d -> c g d")).then_inc(pool_in, 16)
            for h in range(H):
                at = HD * (h % 2)
                pool.dma_start(uvp[:, h, at:at + HD], w_uv[0, :, h, :]).then_inc(uv_in, 16)
            pool.wait_ge(consts, 2)
            for g, w in enumerate(WINDOWS):
                last = nc.gpsimd.tensor_scalar(icnt[:, g, :], icnt[:, g, :], float(w), 0.0, ALU.min, ALU.max)
            last.then_inc(cnt_ok, 1)
            pool.wait_ge(icnt_ok, 1)

            for g, w in enumerate(WINDOWS):
                pool.wait_ge(by_act, emptied[number["pool", g]])
                if g == 0:
                    pool.wait_ge(job_done, number["qlat", H - 1] + 1)
                src, span, n = apad[:, g, :], 1, 0
                while span < w:
                    dst = win[:, n % 2, :]
                    link(nc.gpsimd.tensor_tensor(dst[:, PAD:PAD + T], src[:, PAD:PAD + T],
                                                 src[:, PAD - span:PAD - span + T], ALU.add))
                    src, span, n = dst, 2 * span, n + 1
                link(nc.gpsimd.tensor_tensor(dT[:, g, 0:PAD], src[:, PAD:2 * PAD], icnt[:, g, :], ALU.mult))
                link(nc.gpsimd.tensor_scalar(dT[:, g, PAD:T], src[:, 2 * PAD:PAD + T], 1.0 / w, 0.0,
                                             ALU.mult, ALU.add))
                nc.gpsimd.tensor_tensor(dT[:, g, :], dT[:, g, :], apad[:, g, PAD:PAD + T],
                                        ALU.subtract).then_inc(d_ok, 1)

            pool.wait_ge(select_ok, 1)
            pool.wait_ge(job_done, number["z", PG - 1] + 1)
            for half in range(2):
                pool.dma_start(ada_half[half],
                               b_ada[0, 2 * D:6 * D].rearrange("(r a n) -> r a n", r=4, a=2)[:, half, :]
                               ).then_inc(brow_in, 16)
            pool.wait_ge(by_vec, emptied[number["row", 11]])
            for half in range(2):
                pool.dma_start(ada_dram.rearrange("r (a n) -> r a n", a=2)[:, half, :],
                               ada_half[half]).then_inc(row_out, 16)
            pool.wait_ge(row_out, 32)
            pool.wait_ge(job_done, number["V", C - 1] + 1)
            pool.dma_start(g1b, spread(ada_dram[0])).then_inc(rows_in, 16)
            pool.dma_start(sh2b, spread(ada_dram[1])).then_inc(rows_in, 16)
            pool.dma_start(A2b, spread(ada_dram[2])).then_inc(rows_in, 16)
            pool.dma_start(n2b, spread(norm2_g[0])).then_inc(rows_in, 16)
            for part in range(3):
                pool.dma_start(braw[part * NE:(part + 1) * NE, :], b_gu[0]).then_inc(bg_in, 16)
            pool.wait_ge(bg_in, 48)
            link(nc.gpsimd.tensor_copy(b3, braw))
            link(nc.gpsimd.tensor_tensor(bres, braw, b3, ALU.subtract))
            nc.gpsimd.tensor_copy(b3[NE:2 * NE, :], bres[NE:2 * NE, :])
            link(nc.gpsimd.tensor_copy(b3[2 * NE:3 * NE, :], bres[2 * NE:3 * NE, :]))
            link(nc.gpsimd.tensor_tensor(braw[2 * NE:3 * NE, :], bres[2 * NE:3 * NE, :],
                                         b3[2 * NE:3 * NE, :], ALU.subtract))
            nc.gpsimd.tensor_copy(b3[2 * NE:3 * NE, :], braw[2 * NE:3 * NE, :]).then_inc(b3_ok, 1)
            pool.wait_ge(b3_ok, 1)
            pool.wait_ge(job_done, number["B", KD - 1] + 1)
            link(nc.gpsimd.memset(zero, 0.0))
            yz = y_dram.rearrange("(p a) (b n) -> p (a b) n", a=T // P, n=CH)
            for j in range(8):
                pool.dma_start(yz[:, j, :], zero).then_inc(zero_out, 16)
            pool.wait_ge(job_done, number["A", KD - 1] + 1)
            link(nc.gpsimd.memset(XG[:, :, :], 0.0))
            for ch in range(C):
                pool.wait_ge(h2_ok, ch + 1)
                pool.dma_start(rows(h2_dram)[:, ch, 0:D], h2[:, ch, :]).then_inc(h2_out, 16)
            pool.wait_ge(ss3_ok, C)
            pool.dma_start(g2b, spread(ada_dram[3])).then_inc(g2_in, 16)
            pool.wait_ge(wt_ok, 1)
            pool.dma_start(rows(h2_dram)[:, :, D:HX], wth[:, :, :]).then_inc(wt_out, 16)
            last_row = pool.to_reg(T - 1)

            def gather(b, done):
                pool.indirect_dma_start(out=XG[0:slots, b, :], out_offset=None, in_=h2_dram,
                                        in_offset=bass.IndirectOffsetOnAxis(ap=iug[0:slots, b:b + 1], axis=0),
                                        bounds_check=last_row, oob_is_err=False).then_inc(done, 16)

            def scatter(b, which, done):
                pool.indirect_dma_start(out=y_dram, in_=Y[0:slots, b, :], in_offset=None,
                                        out_offset=bass.IndirectOffsetOnAxis(ap=which, axis=0),
                                        bounds_check=last_row, oob_is_err=False,
                                        compute_op=ALU.add).then_inc(done, 16)

            pool.wait_ge(h2_out, 16 * C)
            pool.wait_ge(wt_out, 16)
            pool.wait_ge(idx_ok, 1)
            for b in range(2):
                link(nc.gpsimd.tensor_copy(iug[:, b:b + 1], idx[:, b:b + 1]))
                gather(b, xg_in[b])
            pool.wait_ge(zero_out, 16 * 8)

            def wait_apart(s_, value):
                pool.wait_ge(s_, value)
                pool.sem_inc(pool_steps, 1)

            def gather_ahead(e, b):
                wait_apart(wc_ok, e + 1)
                nc.gpsimd.tensor_copy(iug[:, b:b + 1], idx[:, bass.ds(e + 2, 1)]).then_inc(iug_ok, 1)
                wait_apart(iug_ok, e + 1)
                gather(b, xg_in[b])

            def add_rows(e, b, first=False):
                if not first:
                    wait_apart(y_added, e * 16)
                nc.gpsimd.tensor_copy(ius[:, b:b + 1], idx[:, bass.ds(e, 1)]).then_inc(ius_ok, 1)
                pool.wait_ge(ius_ok, e + 1)
                wait_apart(y_ok, e + 1)
                scatter(b, ius[0:slots, b:b + 1], y_added)

            gather_ahead(0, 0)
            gather_ahead(1, 1)
            add_rows(0, 0, first=True)
            with pool.Fori(1, NE // 2 - 1) as i:
                gather_ahead(i * 2, 0)
                add_rows(i * 2 - 1, 1)
                gather_ahead(i * 2 + 1, 1)
                add_rows(i * 2, 0)
            add_rows(NE - 3, 1)
            add_rows(NE - 2, 0)
            add_rows(NE - 1, 1)
            pool.wait_ge(y_added, 16 * NE)
            most = pool.value_load(cmaxi[0:1, 0:1], min_val=0, max_val=T)
            with pool.If(most > slots):
                pool.sem_inc(ov_go, 1)
                with pool.Fori(0, OVER) as r:
                    with pool.Fori(0, NE) as e:
                        n = r * NE + e
                        wait_apart(ov_idx, n + 1)
                        gather(0, ov_xg)
                        wait_apart(ov_y, n + 1)
                        scatter(0, iug[0:slots, 0:1], ov_add)
                        pool.wait_ge(ov_add, n * 16 + 16)
                        pool.sem_inc(ov_go, 1)
            pool.sem_inc(moe_done, 1)

        @block.scalar
        def _(act):
            chain = [0]

            def link(ins):
                chain[0] += 1
                ins.then_inc(act_chain, 1)
                act.wait_ge(act_chain, chain[0])

            def job(kind, i=0):
                act.wait_ge(job_done, number[kind, i] + 1)
                return bank(kind, i)

            act.wait_ge(c_in, 16)
            nc.scalar.activation(cnd[:, 1, :], cnd[:, 0, :], ACT.Tanh, scale=0.5).then_inc(th_c, 1)
            act.wait_ge(x_in, 16)
            act.wait_ge(consts, 1)
            for ch in range(C):
                link(nc.scalar.activation(xn[:, ch, :], X[:, ch, :], ACT.Square, accum_out=ss[:, ch:ch + 1]))
            nc.scalar.activation(ss, ss, ACT.Sqrt, scale=1.0 / D, bias=eps).then_inc(ss_ok, 1)
            act.wait_ge(rstd_ok, 1)
            for ch in range(C):
                nc.scalar.activation(xn[:, ch, :], X[:, ch, :], ACT.Copy,
                                     scale=rstd[:, ch:ch + 1]).then_inc(xn_ok, 1)
            for i in range(8):
                ch, half = i // 2, i % 2
                nc.scalar.activation(hT[:, 4 * half:4 * half + 4, ch * P:(ch + 1) * P],
                                     job("xT", i).rearrange("p (k t) -> p k t", k=4), ACT.Copy).then_inc(by_act, 1)
            for ch in range(C):
                link(nc.scalar.activation(ckv[:, ch, :], job("tok", ch)[:, 0:LAT], ACT.Square,
                                          accum_out=ss2[:, ch:ch + 1]))
                nc.scalar.activation(ss2[:, ch:ch + 1], ss2[:, ch:ch + 1], ACT.Sqrt, scale=1.0 / LAT,
                                     bias=eps).then_inc(ss2_ok, 1)
            nc.scalar.activation(ukT[:, :, :].rearrange("p a l -> p (a l)"), job("uk"), ACT.Copy).then_inc(by_act, 1)
            for ch in range(C):
                nc.scalar.activation(T3[:, :, ch * P:(ch + 1) * P],
                                     job("tr", ch)[:, 0:3 * P].rearrange("p (a t) -> p a t", a=3),
                                     ACT.Copy).then_inc(by_act, 1)

            relus = [0]

            def index_chunk(ch):
                n = P * (ch + 1)
                for h in range(IH):
                    src = job("idx", 4 * ch + h)
                    if relus[0] >= 2:
                        act.wait_ge(relu_used, relus[0] - 1)
                    nc.scalar.activation(relu[:, relus[0] % 2, 0:n], src[:, 0:n], ACT.Relu).then_inc(by_act, 1)
                    relus[0] += 1

            index_chunk(1)
            for i in range(4):
                nc.scalar.activation(qT[:, i, :], job("q", i), ACT.Copy).then_inc(by_act, 1)
            for h in range(H):
                nc.scalar.activation(q_latT[:, h, :], job("qlat", h), ACT.Copy).then_inc(by_act, 1)
            index_chunk(2)
            for g in range(PG):
                nc.scalar.activation(apad[:, g, PAD:PAD + T], job("pool", g), ACT.Copy).then_inc(by_act, 1)
            index_chunk(3)
            for g in range(PG):
                nc.scalar.activation(zT[:, g, :], job("z", g), ACT.Copy,
                                     scale=svT[:, 24 + g:25 + g]).then_inc(by_act, 1)
            def exponentials(g):
                n = P * (g // 2 + 1)
                for i in range(4):
                    s = 4 * g + i
                    act.wait_ge(max_ok, s + 1)
                    nc.scalar.activation(Lt[:, i, 0:n], Lt[:, i, 0:n], ACT.Exp, scale=SCALE,
                                         bias=am[:, 1, s:s + 1], accum_out=am[:, 2, s:s + 1]).then_inc(exp_ok, 1)

            def gate_b(g):
                nc.scalar.activation(mT[:, g, :], job("gb", g), ACT.Tanh, scale=0.5).then_inc(by_act, 1)

            exponentials(0)
            gate_b(0)
            for g in range(NGR):
                ch, hh = g // 2, g % 2
                n = P * (ch + 1)
                for i in range(4):
                    src = job("PT", 4 * g + i)
                    nc.scalar.activation(pT[:, 0:ch + 1, i, :], src[:, 0:n].rearrange("p (s q) -> p s q", q=P),
                                         ACT.Copy).then_inc(by_act, 1)
                nc.scalar.activation(o_latT[:, 4 * hh:4 * hh + 4, :].rearrange("p h q -> p (h q)"),
                                     job("O", g), ACT.Copy).then_inc(by_act, 1)
                if g < NGR - 1:
                    exponentials(g + 1)
                    gate_b(g + 1)
                if hh:
                    nc.scalar.activation(oT[:, :, ch * P:(ch + 1) * P],
                                         job("V", ch).rearrange("p (a q) -> p a q", a=4),
                                         ACT.Copy).then_inc(by_act, 1)
            for m in range(KD):
                src = job("ga", m)
                if m >= 2:
                    act.wait_ge(by_vec, emptied[number["A", m - 2]])
                nc.scalar.activation(relu[:, m % 2, :], src, ACT.Tanh, scale=0.5).then_inc(by_act, 1)
            def weights_high(e, up, first=False):
                came(act, SU if up else SG, e)
                w = up_w if up else gate_w
                for j in range(GP):
                    if not first:
                        act.wait_ge(granule_used, e * 2 * GP + (up * GP + j - NG + 1))
                    nc.scalar.activation(whl[:, j % NG, 0, :, :], w[:, j * GK:(j + 1) * GK, :],
                                         ACT.Copy).then_inc(hi_ok, 1)

            def h2T_copy(ch):
                for half in range(2):
                    nc.scalar.activation(h2T[:, 4 * half:4 * half + 4, ch * P:(ch + 1) * P],
                                         job("h2T", 2 * ch + half).rearrange("p (k t) -> p k t", k=4),
                                         ACT.Copy).then_inc(by_act, 1)

            def logits(ch):
                act.wait_ge(wr_in, 32)
                nc.scalar.activation(lgT[:, ch * P:(ch + 1) * P], job("rout", ch)[0:NE, 0:P], ACT.Identity,
                                     bias=br[:, 0:1]).then_inc(by_act, 1)

            for ch in range(C):
                act.wait_ge(by_vec, emptied[number["out", 2 * ch + 1]])
                link(nc.scalar.activation(sq, X[:, ch, :], ACT.Square, accum_out=ss3[:, ch:ch + 1]))
                nc.scalar.activation(ss3[:, ch:ch + 1], ss3[:, ch:ch + 1], ACT.Sqrt, scale=1.0 / D,
                                     bias=eps).then_inc(ss3_ok, 1)
                if ch:
                    h2T_copy(ch - 1)
                if ch > 1:
                    logits(ch - 2)
            logits(C - 2)
            h2T_copy(C - 1)
            logits(C - 1)
            act.wait_ge(nm_ok, 1)
            for ch in range(C):
                nc.scalar.activation(ex[:, ch, :], lg[:, ch, 0:NE], ACT.Exp, bias=nm1[:, ch:ch + 1]).then_inc(ex_ok, 1)
            act.wait_ge(h2_out, 16 * C)
            act.wait_ge(zero_out, 16 * 8)
            weights_high(0, 0, first=True)

            def xgT_copy(ok):
                nc.scalar.activation(xgT[:, 0:4, :], turned(4), ACT.Copy)
                nc.scalar.activation(xgT[:, 4:8, :], turned(5), ACT.Copy).then_inc(ok, 1)

            def rows_high(e):
                act.wait_ge(tx_done, e + 1)
                nc.scalar.activation(xhl[:, 0, 0:4, :], turned(4), ACT.Copy)
                nc.scalar.activation(xhl[:, 0, 4:8, :], turned(5), ACT.Copy).then_inc(xh_ok, 1)

            def tanh_gate(e):
                act.wait_ge(gt_ok, e + 1)
                nc.scalar.activation(th, gt, ACT.Tanh, scale=0.5 * ALPHA).then_inc(th_ok, 1)

            def token_weights(e, b):
                nc.scalar.activation(WC[0:slots, b:b + 1], XG[0:slots, b, bass.ds(e + D, 1)], ACT.Copy).then_inc(wc_ok, 1)

            def weighted(e, b, reused=True):
                act.wait_ge(dn_done, e + 1)
                if reused:
                    act.wait_ge(y_added, e * 16 - 16)
                act.wait_ge(wt_ok, 1)
                nc.scalar.activation(Y[0:slots, b, 0:CH], ps[0:slots, 2, :], ACT.Copy, scale=WC[0:slots, b:b + 1])
                nc.scalar.activation(Y[0:slots, b, CH:D], ps[0:slots, 3, :], ACT.Copy,
                                     scale=WC[0:slots, b:b + 1]).then_inc(y_ok, 1)

            def actT_copy(e):
                act.wait_ge(ta_done, e + 1)
                nc.scalar.activation(actT[:, :, :], turned(6), ACT.Copy).then_inc(actT_ok, 1)

            def expert(e, b, reused=True, last=False):
                weights_high(e, 1)
                tanh_gate(e)
                if not last:
                    weights_high(e + 1, 0)
                    rows_high(e + 1)
                weighted(e - 1, 1 - b, reused)
                actT_copy(e)
                if not last:
                    act.wait_ge(y_ok, e)
                    token_weights(e + 1, 1 - b)

            rows_high(0)
            token_weights(0, 0)
            weights_high(0, 1)
            tanh_gate(0)
            weights_high(1, 0)
            rows_high(1)
            token_weights(1, 1)
            actT_copy(0)
            expert(1, 1, reused=False)
            expert(2, 0, reused=False)
            with act.Fori(1, NE // 2 - 1) as i:
                expert(i * 2 + 1, 1)
                expert(i * 2 + 2, 0)
            expert(NE - 1, 1, last=True)
            weighted(NE - 1, 1)

            most = act.value_load(cmaxi[0:1, 0:1], min_val=0, max_val=T)
            with act.If(most > slots):
                with act.Fori(0, OVER) as r:
                    with act.Fori(0, NE) as e:
                        n = r * NE + e
                        act.wait_ge(ov_tx, n + 1)
                        xgT_copy(ov_xt)
                        act.wait_ge(ov_gt, n + 1)
                        nc.scalar.activation(th, gt, ACT.Tanh, scale=0.5 * ALPHA).then_inc(ov_th, 1)
                        act.wait_ge(ov_ta, n + 1)
                        nc.scalar.activation(actT[:, :, :], turned(6), ACT.Copy).then_inc(ov_at, 1)
                        nc.scalar.activation(WC[0:slots, 0:1], XG[0:slots, 0, bass.ds(e + D, 1)], ACT.Copy).then_inc(ov_wc, 1)
                        act.wait_ge(ov_wc, n + 1)
                        act.wait_ge(ov_dn, n + 1)
                        for half in range(2):
                            last = nc.scalar.activation(Y[0:slots, 0, half * CH:(half + 1) * CH],
                                                        ps[0:slots, 2 + half, :], ACT.Copy, scale=WC[0:slots, 0:1])
                        last.then_inc(ov_y, 1)

            act.wait_ge(wtT_done, 1)
            nc.scalar.activation(wtT, ps[0:NE, 7, :], ACT.Copy).then_inc(wtT_ok, 1)
            for ch in range(C):
                act.wait_ge(x2_ok, ch + 1)
                link(nc.scalar.activation(res[:, ch, :], X[:, ch, :], ACT.Square, accum_out=ss4[:, ch:ch + 1]))
                nc.scalar.activation(ss4[:, ch:ch + 1], ss4[:, ch:ch + 1], ACT.Sqrt, scale=1.0 / D,
                                     bias=eps).then_inc(ss4_ok, 1)

        @block.vector
        def _(dve):
            chain = [0]

            def link(ins):
                chain[0] += 1
                ins.then_inc(dve_chain, 1)
                dve.wait_ge(dve_chain, chain[0])

            def job(kind, i=0):
                dve.wait_ge(job_done, number[kind, i] + 1)
                return bank(kind, i)

            v = nc.vector
            dve.wait_ge(th_c, 1)
            link(v.scalar_tensor_tensor(out=cnd[:, 1, :], in0=cnd[:, 1, :], scalar=1.0, in1=cnd[:, 0, :],
                                        op0=ALU.add, op1=ALU.mult))
            link(v.tensor_scalar(cnd[:, 2, :], cnd[:, 1, :], 0.5, None, ALU.mult))
            dve.wait_ge(ss_ok, 1)
            v.reciprocal(rstd, ss).then_inc(rstd_ok, 1)
            v.tensor_copy(svT[:, :], job("sv")[:, 0:28]).then_inc(by_vec, 1)

            def ada(j):
                n = place["a", j]
                dve.wait_ge(piece_in[n % FR], 16 * (n // FR + 1))
                if j == 8:
                    dve.wait_ge(job_done, number["z", PG - 1] + 1)
                w, a = piece("a", j), acc[j]
                link(v.tensor_scalar(a, w[:, 0, :], cnd[:, 2, 0:1], None, ALU.mult))
                for k in range(1, KD):
                    ins = v.scalar_tensor_tensor(out=a, in0=w[:, k, :], scalar=cnd[:, 2, k:k + 1], in1=a,
                                                 op0=ALU.mult, op1=ALU.add)
                    if k < KD - 1:
                        link(ins)
                    else:
                        ins.then_inc(acc_ok, 1)

            for j in range(4):
                ada(j)
            b_ = job("adac")
            v.tensor_tensor(sh1c, b_[:, 0:8], svT[:, 0:8], ALU.add)
            link(v.tensor_tensor(A1, b_[:, 8:16], svT[:, 8:16], ALU.add))
            v.scalar_tensor_tensor(out=A1, in0=A1, scalar=1.0, in1=svT[:, 16:24], op0=ALU.add,
                                   op1=ALU.mult).then_inc(by_vec, 1)
            dve.wait_ge(by_vec, emptied[number["adac", 0]])
            dve.wait_ge(by_act, emptied[number["xT", 7]])
            for k in range(KD):
                v.tensor_scalar(hT[:, k, :], hT[:, k, :], A1[:, k:k + 1], sh1c[:, k:k + 1], ALU.mult,
                                ALU.add).then_inc(hT_ok, 1)
            dve.wait_ge(kvg_in, 16)
            for ch in range(C):
                b_ = job("tok", ch)
                dve.wait_ge(ss2_ok, ch + 1)
                if ch >= 2:
                    dve.wait_ge(job_done, number["tr", ch - 2] + 1)
                link(v.reciprocal(rstd2[:, ch:ch + 1], ss2[:, ch:ch + 1]))
                v.scalar_tensor_tensor(out=ckv[:, ch, :], in0=b_[:, 0:LAT], scalar=rstd2[:, ch:ch + 1],
                                       in1=kvgb[:, :], op0=ALU.mult, op1=ALU.mult)
                v.tensor_copy(qk[:, ch % 2, 0:P], b_[:, LAT:LAT + P])
                v.tensor_copy(qk[:, ch % 2, P:2 * P].rearrange("p (a d) -> p a d", a=IH),
                              b_[:, 2 * P:2 * P + IDIM].rearrange("p (a d) -> p a d", a=1).broadcast_to([P, IH, IDIM]))
                v.tensor_scalar(wi[:, ch, :], b_[:, 2 * P + IDIM:2 * P + IDIM + IH], IDX_SCALE, None,
                                ALU.mult).then_inc(by_vec, 1)
            dve.wait_ge(by_vec, emptied[number["tok", C - 1]])

            relus = [0]

            def select(ch, apart=False):
                n = P * (ch + 1)
                s = score[:, 0:n]
                for h in range(IH):
                    dve.wait_ge(by_act, emptied[number["idx", 4 * ch + h]])
                    r = relu[:, relus[0] % 2, 0:n]
                    w = wi[:, ch, h:h + 1]
                    if h == 0:
                        ins = v.tensor_scalar(s, r, w, None, ALU.mult)
                    else:
                        to = r if apart and h == IH - 1 else s
                        ins = v.scalar_tensor_tensor(out=to, in0=r, scalar=w, in1=s, op0=ALU.mult, op1=ALU.add)
                    relus[0] += 1
                    ins.then_inc(relu_used, 1)
                    dve.wait_ge(relu_used, relus[0])
                s = to
                link(v.tensor_tensor(s[:, n - P:n], s[:, n - P:n], causal[:, :], ALU.add))
                if apart:
                    return
                take_best(s, K_SEL // 8)
                link(v.tensor_scalar(bias_of[ch], s, 2 * MASKED, HIDDEN, ALU.is_gt, ALU.mult))

            def take_best(s, times):
                for _ in range(times):
                    link(v.max(out=top8[:, :], in_=s))
                    link(v.match_replace(out=s, in_to_replace=top8[:, :], in_values=s, imm_value=TAKEN))

            dve.wait_ge(consts, 2)
            dve.wait_ge(cnt_ok, 1)
            v.reciprocal(icnt[:, :, :], icnt[:, :, :]).then_inc(icnt_ok, 1)
            select(1)
            ada(4)
            ada(5)
            select(2)
            ada(6)
            ada(7)
            select(3, apart=True)
            dve.drain().then_inc(select_ok, 1)

            def ada_rows(j):
                r, half = (j - 4) // 2, (j - 4) % 2
                row = small[32 * r:32 * r + 1, 1536 * half:1536 * half + CH]
                v.tensor_tensor(row, job("row", j)[32 * r:32 * r + 1, :], row, ALU.add).then_inc(by_vec, 1)

            last_scores = relu[:, 1, :]
            TAKES = (4, 4, 4, 2, 2)
            dve.wait_ge(d_ok, PG)

            def maxima(g):
                ch = g // 2
                n = P * (ch + 1)
                for i in range(4):
                    s = 4 * g + i
                    if g:
                        dve.wait_ge(job_done, number["PT", s - 4] + 1)
                    v.tensor_tensor_reduce(out=Lt[:, i, 0:n], in0=job("L", s)[:, 0:n], in1=bias_of[ch], scale=1.0,
                                           scalar=-3.0e38, op0=ALU.add, op1=ALU.max,
                                           accum_out=am[:, 0, s:s + 1]).then_inc(by_vec, 1)
                    dve.wait_ge(by_vec, emptied[number["L", s]])
                    v.tensor_scalar(am[:, 1, s:s + 1], am[:, 0, s:s + 1], -SCALE, None, ALU.mult).then_inc(max_ok, 1)

            maxima(0)
            for g in range(NGR):
                n = P * (g // 2 + 1)
                for i in range(4):
                    s = 4 * g + i
                    dve.wait_ge(exp_ok, s + 1)
                    link(v.reciprocal(am[:, 3, s:s + 1], am[:, 2, s:s + 1]))
                    v.tensor_scalar(Lt[:, i, 0:n], Lt[:, i, 0:n], am[:, 3, s:s + 1], None,
                                    ALU.mult).then_inc(prob_ok, 1)
                if g == 2:
                    dve.wait_ge(brow_in, 32)
                    for j in range(4, 8):
                        ada_rows(j)
                if g < NGR - 1:
                    maxima(g + 1)
                if 3 <= g < 7:
                    ada(g + 5)
                if g < len(TAKES):
                    take_best(last_scores, TAKES[g])
                if g == len(TAKES) - 1:
                    link(v.tensor_scalar(bias_of[C - 1], last_scores, 2 * MASKED, HIDDEN, ALU.is_gt, ALU.mult))
            for j in range(8, 12):
                ada_rows(j)
            for m in range(KD):
                b_ = job("B", m)
                dve.wait_ge(by_act, emptied[number["gb", m]])
                v.scalar_tensor_tensor(out=mT[:, m, :], in0=mT[:, m, :], scalar=1.0, in1=b_, op0=ALU.add,
                                       op1=ALU.mult).then_inc(by_vec, 1)
            for m in range(KD):
                b_ = job("A", m)
                dve.wait_ge(by_act, emptied[number["ga", m]])
                t = relu[:, m % 2, :]
                link(v.scalar_tensor_tensor(out=t, in0=t, scalar=1.0, in1=b_, op0=ALU.add, op1=ALU.mult))
                v.tensor_tensor(mT[:, m, :], mT[:, m, :], t, ALU.add).then_inc(by_vec, 1)
            dve.wait_ge(rows_in, 64)
            link(v.scalar_tensor_tensor(out=A2b, in0=A2b, scalar=1.0, in1=n2b, op0=ALU.add, op1=ALU.mult))

            def weights_low(e, up):
                w = up_w if up else gate_w
                for j in range(GP):
                    dve.wait_ge(hi_ok, e * 2 * GP + (up * GP + j + 1))
                    v.tensor_tensor(whl[:, j % NG, 1, :, :], w[:, j * GK:(j + 1) * GK, :], whl[:, j % NG, 0, :, :],
                                    ALU.subtract).then_inc(lo_ok, 1)

            def h2_rows(ch):
                dve.wait_ge(ss3_ok, ch + 1)
                link(v.reciprocal(rstd3[:, ch:ch + 1], ss3[:, ch:ch + 1]))
                link(v.scalar_tensor_tensor(out=h2[:, ch, :], in0=X[:, ch, :], scalar=rstd3[:, ch:ch + 1],
                                            in1=A2b, op0=ALU.mult, op1=ALU.mult))
                v.tensor_tensor(h2[:, ch, :], h2[:, ch, :], sh2b, ALU.add).then_inc(h2_ok, 1)

            for ch in range(C):
                if ch:
                    h2_rows(ch - 1)
                for half in range(2):
                    b_ = job("out", 2 * ch + half)
                    sl = slice(half * CH, (half + 1) * CH)
                    t = relu[:, half, :]
                    link(v.scalar_tensor_tensor(out=t, in0=b_, scalar=0.5, in1=g1b[:, sl], op0=ALU.mult,
                                                op1=ALU.mult))
                    v.tensor_tensor(X[:, ch, sl], X[:, ch, sl], t, ALU.add).then_inc(by_vec, 1)
            dve.wait_ge(by_vec, emptied[number["out", 2 * C - 1]])
            h2_rows(C - 1)

            v.tensor_copy(lg[:, :, 0:NE], job("rt")[:, 0:C * NE].rearrange("p (c e) -> p c e", c=C)).then_inc(by_vec, 1)
            dve.wait_ge(by_vec, emptied[number["rt", 0]])
            for ch in range(C):
                last = v.max(out=m8[:, ch, :], in_=lg[:, ch, 0:NE])
            link(last)
            v.tensor_scalar(nm1[:, :], m8[:, :, 0], -1.0, None, ALU.mult).then_inc(nm_ok, 1)
            link(v.memset(m8[:, :, TOPK:8], MASKED))
            for ch in range(C):
                last = v.match_replace(out=lr[:, ch, :], in_to_replace=m8[:, ch, :], in_values=lg[:, ch, :],
                                       imm_value=TAKEN)
            link(last)
            link(v.tensor_scalar(mask[:, :, :], lr[:, :, 0:NE], 2 * MASKED, None, ALU.is_lt))
            v.tensor_copy(maskh[:, :, :], mask[:, :, :]).then_inc(mask_ok, 1)
            dve.wait_ge(ex_ok, C)
            link(v.tensor_tensor(wts[:, :, :], ex[:, :, :], mask[:, :, :], ALU.mult))
            link(v.reduce_sum(sm[:, 0, :], wts[:, :, :], axis=AX.X))
            link(v.reciprocal(sm[:, 1, :], sm[:, 0, :]))
            for ch in range(C):
                last = v.tensor_scalar(wts[:, ch, :], wts[:, ch, :], sm[:, 1, ch:ch + 1], None, ALU.mult)
            link(last)
            v.tensor_scalar(wth[:, :, :], wts[:, :, :], 0.5, None, ALU.mult).then_inc(wt_ok, 1)
            b_ = job("rank")
            v.tensor_reduce(cmax[:, :], b_[:, C * NE:(C + 1) * NE], op=ALU.max, axis=AX.X)
            link(v.scalar_tensor_tensor(out=rankm[:, :, :], in0=b_[:, 0:C * NE].rearrange("p (c e) -> p c e", c=C),
                                        scalar=1.0, in1=mask[:, :, :], op0=ALU.add, op1=ALU.mult))
            v.tensor_copy(cmaxi[:, :], cmax[:, :])
            v.tensor_scalar(rankm[:, :, :], rankm[:, :, :], -1.0, None, ALU.add).then_inc(by_vec, 1)
            dve.wait_ge(by_vec, emptied[number["rank", 0]])

            def rows_low(e):
                dve.wait_ge(xh_ok, e + 1)
                for half in range(2):
                    ks = slice(4 * half, 4 * half + 4)
                    last = v.tensor_tensor(xhl[:, 1, ks, :], turned(4 + half), xhl[:, 0, ks, :], ALU.subtract)
                last.then_inc(xl_ok, 1)

            def gate_limit(e):
                dve.wait_ge(granule_used, e * 2 * GP + GP)
                v.tensor_scalar(gt, ps[0:slots, 0, :], LIMIT, None, ALU.min).then_inc(gt_ok, 1)

            def token_rows(b_, lo, n):
                b_ = b_[:, 0:3 * n].rearrange("p (e a) -> p e a", a=3)
                v.tensor_scalar(ixa[:, 0, lo:lo + n], b_[:, :, 2], -NOWHERE, NOWHERE, ALU.mult, ALU.add)
                link(v.tensor_scalar(ixa[:, 1, lo:lo + n], b_[:, :, 0], float(P), None, ALU.mult))
                link(v.tensor_tensor(ixa[:, 1, lo:lo + n], b_[:, :, 1], ixa[:, 1, lo:lo + n], ALU.add))
                return v.tensor_tensor(idx[:, lo:lo + n], ixa[:, 0, lo:lo + n], ixa[:, 1, lo:lo + n], ALU.add)

            for g in range(NE // OHE):
                if g >= 2:
                    dve.wait_ge(oh_used, g - 1)
                places = rankm[:, :, g * OHE:(g + 1) * OHE].rearrange("p c e -> p e c")
                v.tensor_tensor(oh[g % 2], iota[:, 0:slots].rearrange("p (a b s) -> p a b s", a=1, b=1)
                                .broadcast_to([P, OHE, C, slots]),
                                places.rearrange("p e (c o) -> p e c o", o=1).broadcast_to([P, OHE, C, slots]),
                                ALU.is_equal).then_inc(oh_ok, 1)
                if g == 1:
                    dve.wait_ge(oh_used, 1)
                    token_rows(bank("ix", 0), 0, OHE).then_inc(idx_ok, 1)
                if g == 2:
                    weights_low(0, 0)
                if g == 3:
                    rows_low(0)
                if g == 5:
                    weights_low(0, 1)
                    gate_limit(0)
            dve.wait_ge(oh_used, NE // OHE)
            token_rows(bank("ix", 1), OHE, NE - OHE).then_inc(idx_ok, 1)

            def expert(e, first=False, last=False):
                if not first:
                    weights_low(e, 1)
                    gate_limit(e)
                    if not last:
                        weights_low(e + 1, 0)
                dve.wait_ge(granule_used, e * 2 * GP + 2 * GP)
                v.tensor_scalar(up1, ps[0:slots, 1, :], LIMIT, -LIMIT, ALU.min, ALU.max).then_inc(up_ok, 1)
                dve.wait_ge(up_ok, e + 1)
                v.scalar_tensor_tensor(out=up1, in0=up1, scalar=1.0, in1=gt, op0=ALU.add,
                                       op1=ALU.mult).then_inc(prod_ok, 1)
                if not last and not first:
                    rows_low(e + 1)
                dve.wait_ge(prod_ok, e + 1)
                dve.wait_ge(th_ok, e + 1)
                v.scalar_tensor_tensor(out=av, in0=th, scalar=1.0, in1=up1, op0=ALU.add,
                                       op1=ALU.mult).then_inc(av_ok, 1)
                if first:
                    weights_low(e + 1, 0)
                    rows_low(e + 1)

            expert(0, first=True)
            with dve.Fori(1, NE - 1) as e:
                expert(e)
            expert(NE - 1, last=True)

            most = dve.value_load(cmaxi[0:1, 0:1], min_val=0, max_val=T)
            with dve.If(most > slots):
                with dve.Fori(0, OVER) as r:
                    v.tensor_scalar(rankm[:, :, :], rankm[:, :, :], -float(slots), None, ALU.add).then_inc(ov_rk, 1)
                    dve.wait_ge(ov_rk, r + 1)
                    dve.sem_inc(dve_steps, 1)
                    with dve.Fori(0, NE) as e:
                        n = r * NE + e
                        dve.wait_ge(ov_go, n + 1)
                        for ch in range(C):
                            last = v.tensor_scalar(oh[0][:, 0, ch, :], iota[:, 0:slots], rankm[:, ch, bass.ds(e, 1)], None,
                                                   ALU.is_equal)
                        last.then_inc(ov_oh, 1)
                        dve.wait_ge(ov_ix, n + 1)
                        b_ = ps[:, 7, :]
                        v.tensor_scalar(ixa[:, 0, 0:1], b_[:, 2:3], -NOWHERE, NOWHERE, ALU.mult, ALU.add)
                        v.tensor_scalar(ixa[:, 1, 0:1], b_[:, 0:1], float(P), None, ALU.mult).then_inc(ov_i1, 1)
                        dve.wait_ge(ov_i1, n * 2 + 1)
                        v.tensor_tensor(ixa[:, 1, 0:1], b_[:, 1:2], ixa[:, 1, 0:1], ALU.add).then_inc(ov_i1, 1)
                        dve.wait_ge(ov_i1, n * 2 + 2)
                        v.tensor_tensor(iug[:, 0:1], ixa[:, 0, 0:1], ixa[:, 1, 0:1], ALU.add).then_inc(ov_idx, 1)
                        dve.wait_ge(ov_gu, n * 2 + 1)
                        v.tensor_scalar(gt, ps[0:slots, 0, :], LIMIT, None, ALU.min).then_inc(ov_gt, 1)
                        dve.wait_ge(ov_gu, n * 2 + 2)
                        v.tensor_scalar(up1, ps[0:slots, 1, :], LIMIT, -LIMIT, ALU.min, ALU.max).then_inc(ov_up, 1)
                        dve.wait_ge(ov_up, n * 2 + 1)
                        v.scalar_tensor_tensor(out=up1, in0=up1, scalar=1.0, in1=gt, op0=ALU.add,
                                               op1=ALU.mult).then_inc(ov_up, 1)
                        dve.wait_ge(ov_up, n * 2 + 2)
                        dve.wait_ge(ov_th, n + 1)
                        v.scalar_tensor_tensor(out=av, in0=th, scalar=1.0, in1=up1, op0=ALU.add,
                                               op1=ALU.mult).then_inc(ov_av, 1)

            dve.wait_ge(g2_in, 16)
            for ch in range(C):
                for half in range(2):
                    sl = slice(half * CH, (half + 1) * CH)
                    t = relu[:, half, :]
                    dve.wait_ge(yb_done, 2 * ch + half + 1)
                    link(v.tensor_tensor(t, ps[:, (2 * ch + half) % 8, :], g2b[:, sl], ALU.mult))
                    link(v.tensor_tensor(X[:, ch, sl], X[:, ch, sl], t, ALU.add))
            dve.wait_ge(fg_in, 16)

            def result(ch):
                dve.wait_ge(ss4_ok, ch + 1)
                link(v.reciprocal(rstd4[:, ch:ch + 1], ss4[:, ch:ch + 1]))
                v.scalar_tensor_tensor(out=res[:, ch, :], in0=X[:, ch, :], scalar=rstd4[:, ch:ch + 1], in1=fgb,
                                       op0=ALU.mult, op1=ALU.mult).then_inc(res_ok, 1)

            for ch in range(C):
                dve.wait_ge(y_in[ch], 16)
                link(v.tensor_tensor(Yin[:, ch, :], Yin[:, ch, :], g2b, ALU.mult))
                v.tensor_tensor(X[:, ch, :], X[:, ch, :], Yin[:, ch, :], ALU.add).then_inc(x2_ok, 1)
                if ch:
                    result(ch - 1)
            dve.wait_ge(x2_ok, C)
            result(C - 1)

        @block.tensor
        def _(pe):
            mm = nc.tensor.matmul

            def start(kind, i=0):
                n = number[kind, i]
                if n >= 8:
                    pe.wait_ge(by_act if JOBS[n - 8][2] == "A" else by_vec, emptied[n - 8])
                return bank(kind, i)

            def have(kind, i=0):
                n = place[kind, i]
                pe.wait_ge(piece_in[n % FR], 16 * (n // FR + 1))
                return piece(kind, i)

            def chain(out_, pairs, done=None, by=1, start_=True):
                for n, (a, b) in enumerate(pairs):
                    last = mm(out_, a, b, start=(n == 0 and start_), stop=(n == len(pairs) - 1))
                if done is not None:
                    last.then_inc(done, by)
                return last

            def emptied_by(kind, i=0):
                n = number[kind, i]
                pe.wait_ge(by_act if JOBS[n][2] == "A" else by_vec, emptied[n])

            pe.wait_ge(consts, 1)
            pe.wait_ge(sv_in, 48)
            nc.tensor.transpose(start("sv")[:, 0:28], sv[:, :], ident[0:28, 0:28]).then_inc(job_done, 1)
            for i in range(8):
                ch, half = i // 2, i % 2
                b_ = start("xT", i)
                pe.wait_ge(xn_ok, ch + 1)
                for k in range(4):
                    at = (4 * half + k) * P
                    last = nc.tensor.transpose(b_[:, k * P:(k + 1) * P], xn[:, ch, at:at + P], ident[:, :])
                last.then_inc(job_done, 1)
            b_ = start("adac")
            for j in range(4):
                pe.wait_ge(acc_ok, j + 1)
                for q in range(4):
                    last = mm(b_[:, 4 * j + q:4 * j + q + 1], acc[j][:, q * P:(q + 1) * P], ones[:, 0:1],
                              start=True, stop=True)
            last.then_inc(job_done, 1)
            w = have("tok")
            for ch in range(C):
                b_ = start("tok", ch)
                for k in range(KD):
                    pe.wait_ge(hT_ok, k + 1)
                    last = mm(b_[:, 0:TOKW], hT[:, k, ch * P:(ch + 1) * P], w[:, k, :], start=(k == 0), stop=(k == KD - 1))
                last.then_inc(job_done, 1)
            b_ = start("uk")
            pe.wait_ge(uk_in, 16)
            for i in range(4):
                last = nc.tensor.transpose(b_[:, i * P:(i + 1) * P], uk[:, i * P:(i + 1) * P], ident[:, :])
            last.then_inc(job_done, 1)
            for ch in range(C):
                b_ = start("tr", ch)
                emptied_by("tok", ch)
                nc.tensor.transpose(b_[:, 0:P], ckv[:, ch, :], ident[:, :])
                nc.tensor.transpose(b_[:, P:2 * P], qk[:, ch % 2, 0:P], ident[:, :])
                nc.tensor.transpose(b_[:, 2 * P:3 * P], qk[:, ch % 2, P:2 * P], ident[:, :]).then_inc(job_done, 1)

            def index_chunk(ch):
                emptied_by("tr", C - 1)
                for h in range(IH):
                    b_ = start("idx", 4 * ch + h)
                    r = slice(IDIM * h, IDIM * (h + 1))
                    mm(b_[:, 0:P * (ch + 1)], qiT[r, ch * P:(ch + 1) * P], kiT[r, 0:P * (ch + 1)], start=True,
                       stop=True, tile_position=(IDIM * h, 0)).then_inc(job_done, 1)

            def by_feature(kind, i, w, m):
                b_ = start(kind, i)
                return chain(b_, [(w[:, k, m * P:(m + 1) * P], hT[:, k, :]) for k in range(KD)], job_done)

            index_chunk(1)
            w = have("q")
            for m in range(4):
                by_feature("q", m, w, m)
            for h in range(H):
                b_ = start("qlat", h)
                emptied_by("q", h // 2)
                r = slice(HD * (h % 2), HD * (h % 2) + HD)
                mm(b_, ukT[r, h // 2, :], qT[r, h // 2, :], start=True, stop=True,
                   tile_position=(HD * (h % 2), 0)).then_inc(job_done, 1)
            index_chunk(2)
            w = have("pool")
            for m in range(PG):
                by_feature("pool", m, w, m)
            index_chunk(3)
            pe.wait_ge(pool_in, 16)
            for g in range(PG):
                b_ = start("z", g)
                pe.wait_ge(d_ok, g + 1)
                mm(b_, wpool[:, g, :], dT[:, g, :], start=True, stop=True).then_inc(job_done, 1)

            def ada_sum(j):
                b_ = start("row", j)
                pe.wait_ge(acc_ok, j + 1)
                mm(b_, ones[:, :], acc[j], start=True, stop=True).then_inc(job_done, 1)

            def logits(g):
                ch, hh = g // 2, g % 2
                for i in range(4):
                    b_ = start("L", 4 * g + i)
                    h = 4 * hh + i
                    emptied_by("qlat", h)
                    mm(b_[:, 0:P * (ch + 1)], q_latT[:, h, ch * P:(ch + 1) * P], ckvT[:, 0:P * (ch + 1)], start=True,
                       stop=True).then_inc(job_done, 1)

            def gate_b(g):
                by_feature("gb", g, have("gb", g // 4), g % 4)

            logits(0)
            gate_b(0)
            for g in range(NGR):
                ch, hh = g // 2, g % 2
                for i in range(4):
                    b_ = start("PT", 4 * g + i)
                    pe.wait_ge(prob_ok, 4 * g + i + 1)
                    for s in range(ch + 1):
                        last = nc.tensor.transpose(b_[:, s * P:(s + 1) * P], Lt[:, i, s * P:(s + 1) * P], ident[:, :])
                    last.then_inc(job_done, 1)
                if g < NGR - 1:
                    logits(g + 1)
                b_ = start("O", g)
                emptied_by("PT", 4 * g + 3)
                chain(b_, [(ckv[:, s, :], pT[:, s, :, :].rearrange("p h q -> p (h q)")) for s in range(ch + 1)], job_done)
                if g < NGR - 1:
                    gate_b(g + 1)
                if hh:
                    b_ = start("V", ch)
                    pe.wait_ge(uv_in, 16 * H)
                    emptied_by("O", g)
                    for a in range(4):
                        last = chain(b_[:, a * P:(a + 1) * P],
                                     [(uvp[:, 2 * a + q, :], o_latT[:, 2 * a + q, :]) for q in range(2)])
                    last.then_inc(job_done, 1)
                if g == 1:
                    for j in range(4, 8):
                        ada_sum(j)
            for j in range(8, 12):
                ada_sum(j)
            w = have("wb")
            emptied_by("z", PG - 1)
            for m in range(KD):
                chain(start("B", m), [(w[:, k, m * P:(m + 1) * P], zT[:, k, :]) for k in range(4)], job_done)
            emptied_by("V", C - 1)
            wa = have("wa")
            for m in range(KD):
                by_feature("ga", m, have("ga", m // 4), m % 4)
                chain(start("A", m), [(wa[:, k, m * P:(m + 1) * P], oT[:, k, :]) for k in range(4)], job_done)

            def h2_turn(ch):
                pe.wait_ge(h2_ok, ch + 1)
                for half in range(2):
                    b_ = start("h2T", 2 * ch + half)
                    for k in range(4):
                        at = (4 * half + k) * P
                        last = nc.tensor.transpose(b_[:, k * P:(k + 1) * P], h2[:, ch, at:at + P], ident[:, :])
                    last.then_inc(job_done, 1)

            def router(ch):
                b_ = start("rout", ch)
                emptied_by("h2T", 2 * ch + 1)
                pe.wait_ge(wr_in, 32)
                chain(b_[0:NE, 0:P], [(wr[:, k, :], h2T[:, k, ch * P:(ch + 1) * P]) for k in range(KD)], job_done)

            wo = [have("wo", half) for half in range(2)]
            for ch in range(C):
                for half in range(2):
                    b_ = start("out", 2 * ch + half)
                    for k in range(KD):
                        emptied_by("A", k)
                        last = mm(b_, mT[:, k, ch * P:(ch + 1) * P], wo[half][:, k, :], start=(k == 0), stop=(k == KD - 1))
                    last.then_inc(job_done, 1)
                if ch:
                    h2_turn(ch - 1)
                if ch > 1:
                    router(ch - 2)
            router(C - 2)
            h2_turn(C - 1)
            router(C - 1)
            b_ = start("rt")
            emptied_by("rout", C - 1)
            for ch in range(C):
                last = nc.tensor.transpose(b_[:, ch * NE:(ch + 1) * NE], lgT[:, ch * P:(ch + 1) * P], ident[0:NE, 0:NE])
            last.then_inc(job_done, 1)
            b_ = start("rank")
            pe.wait_ge(mask_ok, 1)
            pe.wait_ge(consts, 2)
            for ch in range(C):
                chain(b_[:, ch * NE:(ch + 1) * NE], [(onesb[:, :], maskh[:, k, :]) for k in range(ch)]
                      + [(tri[:, :], maskh[:, ch, :])])
            chain(b_[:, C * NE:(C + 1) * NE], [(onesb[:, :], maskh[:, k, :]) for k in range(C)], job_done)
            def turn_rows(b, done):
                for k in range(KD):
                    last = nc.tensor.transpose(ps[:, 4 + k // 4, (k % 4) * P:(k % 4) * P + slots],
                                               XG[0:slots, b, k * P:(k + 1) * P], ident[0:slots, 0:slots])
                last.then_inc(done, 1)

            def biases(e, half):
                pe.wait_ge(b3_ok, 1)
                mm(ps[0:slots, half, :], sel3[:, bass.ds(e, 1)].broadcast_to([3 * NE, slots]), b3[:, half * CH:(half + 1) * CH],
                   start=True, stop=False)

            def up_half(e, half, w, done):
                biases(e, half)
                for k in range(KD):
                    last = mm(ps[0:slots, half, :], xgT[:, k, :], w[:, k, :], start=False, stop=(k == KD - 1))
                last.then_inc(done, 1)

            def up_half_parts(e, half):
                biases(e, half)
                for j in range(GP):
                    pe.wait_ge(lo_ok, e * 2 * GP + (half * GP + j + 1))
                    for q in range(GK):
                        k = j * GK + q
                        for a, b in ((0, 0), (0, 1), (1, 0)):
                            last = mm(ps[0:slots, half, :], xhl[:, a, k, :], whl[:, j % NG, b, q, :], start=False,
                                      stop=(k == KD - 1 and a == 1))
                    last.then_inc(granule_used, 1)

            def places(g):
                pe.wait_ge(oh_ok, g + 1)
                for e in range(g * OHE, (g + 1) * OHE):
                    b_ = bank("ix", min(g, 1))
                    at = 3 * (e if g == 0 else e - OHE)
                    for ch in range(C):
                        last = mm(b_[0:slots, at:at + 3], oh[g % 2][:, e % OHE, ch, :], tokid[:, ch, :], start=(ch == 0),
                                  stop=(ch == C - 1))
                last.then_inc(oh_used, 1)

            start("ix", 0)
            places(0)
            start("ix", 1)
            places(1)
            places(2)
            pe.wait_ge(xg_in[0], 16)
            turn_rows(0, tx_done)
            places(3)
            pe.wait_ge(xl_ok, 1)
            up_half_parts(0, 0)
            places(4)
            places(5)
            up_half_parts(0, 1)
            places(6)
            places(7)


            def turn_act(done):
                for k in range(KF):
                    last = nc.tensor.transpose(ps[:, 6, k * P:k * P + slots], av[:, k * P:(k + 1) * P],
                                               ident[0:slots, 0:slots])
                last.then_inc(done, 1)

            def down(w, done):
                for half in range(2):
                    for k in range(KF):
                        last = mm(ps[0:slots, 2 + half, :], actT[:, k, :], w[:, k, half * CH:(half + 1) * CH],
                                  start=(k == 0), stop=(k == KF - 1))
                last.then_inc(done, 1)

            def expert(e, b, half_e, first=False, last=False):
                if not first:
                    pe.wait_ge(xl_ok, e + 1)
                    for half in range(2):
                        up_half_parts(e, half)
                if not last:
                    pe.wait_ge(xg_in[1 - b], (half_e + b) * 16 + 16)
                    turn_rows(1 - b, tx_done)
                if not first:
                    pb = 1 - b
                    came(pe, SD[pb], half_e + b - 1)
                    pe.wait_ge(actT_ok, e)
                    if not isinstance(e, int) or e > 1:
                        pe.wait_ge(y_ok, e - 1)
                    down(down_w[pb], dn_done)
                pe.wait_ge(av_ok, e + 1)
                turn_act(ta_done)

            expert(0, 0, 0, first=True)
            expert(1, 1, 0)
            with pe.Fori(1, NE // 2 - 1) as i:
                expert(i * 2, 0, i)
                expert(i * 2 + 1, 1, i)
            expert(NE - 2, 0, NE // 2 - 1)
            expert(NE - 1, 1, NE // 2 - 1, last=True)
            pe.wait_ge(actT_ok, NE)
            pe.wait_ge(y_ok, NE - 1)
            came(pe, SD[1], NE // 2 - 1)
            down(down_w[1], dn_done)

            most = pe.value_load(cmaxi[0:1, 0:1], min_val=0, max_val=T)
            with pe.If(most > slots):
                with pe.Fori(0, OVER) as r:
                    with pe.Fori(0, NE) as e:
                        n = r * NE + e
                        pe.wait_ge(ov_oh, n + 1)
                        for ch in range(C):
                            last = mm(ps[0:slots, 7, 0:3], oh[0][:, 0, ch, :], tokid[:, ch, :], start=(ch == 0), stop=(ch == C - 1))
                        last.then_inc(ov_ix, 1)
                        pe.wait_ge(ov_xg, n * 16 + 16)
                        turn_rows(0, ov_tx)
                        pe.wait_ge(ov_xt, n + 1)
                        pe.wait_ge(ov_w, n * 48 + 48)
                        for half, w in enumerate((gate_w, up_w)):
                            up_half(e, half, w, ov_gu)
                        pe.wait_ge(ov_av, n + 1)
                        turn_act(ov_ta)
                        pe.wait_ge(ov_at, n + 1)
                        down(down_w[0], ov_dn)
                pe.wait_ge(ov_y, OVER * NE)

            pe.wait_ge(wt_ok, 1)
            for ch in range(C):
                last = nc.tensor.transpose(ps[0:NE, 7, ch * P:(ch + 1) * P], wts[:, ch, :], ident[:, :])
            last.then_inc(wtT_done, 1)
            pe.wait_ge(wtT_ok, 1)
            pe.wait_ge(bd_in, 16)
            pe.wait_ge(y_ok, NE)
            for ch in range(C):
                for half in range(2):
                    mm(ps[:, (2 * ch + half) % 8, :], wtT[:, ch * P:(ch + 1) * P], bdn[:, half, :], start=True,
                       stop=True).then_inc(yb_done, 1)


_INS = ['x', 'c', 'norm1_g', 'norm2_g', 'w_ada', 'b_ada', 'w_in', 'kv_norm_g', 'w_uk', 'w_uv', 'w_pool',
        'pool_scale', 'w_a_up', 'w_b_up', 'w_out', 'w_router', 'b_router', 'w_gu', 'b_gu', 'w_down', 'b_down',
        'final_g']


def kernel(**inputs):
    import numpy as _np
    import concourse.bacc as _bacc
    from concourse import mybir as _mybir
    from concourse.bass_utils import run_bass_kernel_spmd as _run

    nc = _bacc.Bacc("TRN2", target_bir_lowering=False, num_devices=1)
    arrays, args = {}, []
    for name in _INS:
        a = _np.ascontiguousarray(inputs[name])
        arrays[f"in_{name}_dram"] = a
        args.append(nc.dram_tensor(f"in_{name}_dram", a.shape, _mybir.dt.from_np(a.dtype), kind="ExternalInput").ap())
    args.append(nc.dram_tensor("out_0_dram", (1, T, D), F32, kind="ExternalOutput").ap())
    trunk(nc, *args)
    r = _run(nc, [arrays], core_ids=[0])
    return r.results[0]["out_0_dram"]
```

```python
from contextlib import ExitStack

import concourse.bass as bass
from concourse import mybir
from concourse.alu_op_type import AluOpType as ALU

F32 = mybir.dt.float32
BF16 = mybir.dt.bfloat16
F32R = mybir.dt.float32r
U32 = mybir.dt.uint32
ACT = mybir.ActivationFunctionType
AX = mybir.AxisListType

P = 128
T, D = 512, 1024
C = T // P
KD = D // P
H, HD = 8, 64
AW = H * HD
LAT = 128
IH, IDIM = 4, 32
PG = 4
WINDOWS = (2, 4, 8, 16)
PAD = 16
PW = PG * P
NE, TOPK, DFF = 32, 4, 512
KF = DFF // P
LIMIT, ALPHA, EPS = 7.0, 1.702, 1e-6
K_SEL = min(256, T // 4)
SCALE = HD ** -0.5
IDX_SCALE = (IH ** -0.5) * (IDIM ** -0.5)
COL_Q, COL_TOK = 0, AW
TOKW = LAT + IH * IDIM + IDIM + IH
COL_POOL = COL_TOK + TOKW
COL_GA = COL_POOL + PW
COL_GB = COL_GA + D

MASKED = -1e38
TAKEN = -3e38
HIDDEN = -1e30
NOWHERE = 4096.0

SLOTS = 96
HX = D + NE
CH = 512
GK = 2
GP = KD // GK
NG = 4


def trunk(nc, x, c, norm1_g, norm2_g, w_ada, b_ada, w_in, kv_norm_g, w_uk, w_uv, w_pool, pool_scale,
          w_a_up, w_b_up, w_out, w_router, b_router, w_gu, b_gu, w_down, b_down, final_g, out,
          slots=SLOTS):
    ctx = ExitStack()
    with ctx:
        def sb(name, shape, dt=F32):
            return ctx.enter_context(nc.sbuf_tensor(name, shape, dt))

        def sem(name):
            return ctx.enter_context(nc.semaphore(name))

        h2_dram = nc.dram_tensor("h2_rows", (T, HX), F32).ap()
        y_dram = nc.dram_tensor("moe_rows", (T, D), F32).ap()
        ada_dram = nc.dram_tensor("ada_rows", (4, D), F32).ap()

        ring012 = sb("ring012", [P, 3, 4096])
        mix = sb("mix", [P, 4096])
        attn = sb("attn", [P, 5184])
        small = sb("small", [P, 2048])
        apad = sb("apad", [P, PG, PAD + T])
        T3 = sb("T3", [P, 3, T])
        ckv = sb("ckv", [P, C, LAT])
        wi = sb("wi", [P, C, IH])
        uvp = sb("uvp", [P, H, P])
        maskb = sb("maskb", [P, 1280])
        icnt = sb("icnt", [P, PG, PAD])
        ident = sb("ident", [P, P])
        ones = sb("ones", [P, P])
        iota = sb("iota", [P, P], BF16)
        tri = sb("tri", [P, P], BF16)
        onesb = sb("onesb", [P, P], BF16)
        tokid = sb("tokid", [P, C, 3], BF16)
        causal = sb("causal", [P, P])
        kvgb = sb("kvgb", [P, LAT])
        sv = sb("sv", [28, P])
        svT = sb("svT", [P, 28])
        cnd = sb("cnd", [P, 3, KD])
        col = sb("col", [P, 64])
        am = sb("am", [P, 4, C * H])
        top8 = sb("top8", [P, 8])
        wr = sb("wr", [P, KD, NE])
        br = sb("br", [NE, 1])
        lg = sb("lg", [P, C, NE + 8])
        m8 = sb("m8", [P, C, 8])
        nm1 = sb("nm1", [P, C])
        mask = sb("mask", [P, C, NE])
        maskh = sb("maskh", [P, C, NE], BF16)
        sm = sb("sm", [P, 2, C])
        wts = sb("wts", [P, C, NE])
        wth = sb("wth", [P, C, NE])
        rankm = sb("rankm", [P, C, NE])
        ixa = sb("ixa", [P, 2, NE])
        idx = sb("idx", [P, NE], U32)
        cmax = sb("cmax", [P, 1])
        cmaxi = sb("cmaxi", [P, 1], U32)
        sel3 = sb("sel3", [3 * NE, NE], BF16)
        WC = sb("WC", [P, 2])
        iug = sb("iug", [P, 2], U32)
        ius = sb("ius", [P, 2], U32)
        ps = ctx.enter_context(nc.psum_tensor("ps", [P, 8, CH], F32))
        parts = ExitStack()
        h_hi = parts.enter_context(nc.sbuf_tensor("h_hi", [P, KD, T], F32R))
        wb_hl = parts.enter_context(nc.sbuf_tensor("wb_hl", [P, 2, 2, KD, P], F32R))
        zo_hl = parts.enter_context(nc.sbuf_tensor("zo_hl", [P, 2, PG, T], F32R))
        parts.enter_context(nc.sbuf_tensor("parts_gap", [P, 4096], F32))
        h_lo = parts.enter_context(nc.sbuf_tensor("h_lo", [P, KD, T], F32R))
        parts.close()
        X = sb("X", [P, C, D])
        ring3 = sb("ring3", [P, 4096])
        ring = [ring012[:, 0, :], ring012[:, 1, :], ring012[:, 2, :], ring3[:, :]]
        early = ExitStack()
        hT = early.enter_context(nc.sbuf_tensor("hT", [P, KD, T], F32))
        area_b = early.enter_context(nc.sbuf_tensor("area_b", [P, 4096], F32))
        area_a = early.enter_context(nc.sbuf_tensor("area_a", [P, 4096], F32))
        early.close()
        late = sb("late", [P, 4, T])
        xhl = sb("xhl", [P, 2, KD, P], F32R)[:, :, :, 0:slots]
        whl = sb("whl", [P, NG, 2, GK, CH], F32R)

        q_latT = hT
        xn = area_a[:, :].rearrange("p (c d) -> p c d", c=C)
        zT = area_b[:, 0:2048].rearrange("p (g t) -> p g t", g=PG)
        qT = area_b[:, 2048:4096].rearrange("p (g t) -> p g t", g=PG)
        dT = qT
        h2 = area_a[:, :].rearrange("p (c d) -> p c d", c=C)
        acc_in = mix[:, :].rearrange("p (j n) -> p j n", j=8)
        acc = [acc_in[:, j, :] if j < 8 else dT[:, j - 8, :] for j in range(12)]
        mT = mix[:, :].rearrange("p (k t) -> p k t", k=KD)
        h2T = hT
        pT = attn[:, 0:2048].rearrange("p (s h q) -> p s h q", s=C, h=4)
        o_latT = attn[:, 2048:3072].rearrange("p (h q) -> p h q", h=H)
        Lt = attn[:, 3072:5120].rearrange("p (i s) -> p i s", i=4)
        g1b = attn[:, 0:1024]
        A2b = attn[:, 1024:2048]
        sh2b = attn[:, 2048:3072]
        g2b = attn[:, 3072:4096]
        sq = attn[:, 3072:4096]
        n2b = attn[:, 4096:5120]
        ada_half = [small[0:97:32, 0:512], small[0:97:32, 1536:2048]]
        win = attn[:, 1504:1504 + 2 * (PAD + T)].rearrange("p (i t) -> p i t", i=2)
        oT = apad[:, :, PAD:PAD + T]
        ckvT, qiT, kiT = (T3[:, i, :] for i in range(3))
        qk = area_b[:, 0:512].rearrange("p (i t) -> p i t", i=2)
        uk = small[:, 0:512]
        ukT = area_b[:, 512:1024].rearrange("p (i t) -> p i t", i=4)
        wpool = small[:, 1536:2048].rearrange("p (g d) -> p g d", g=PG)
        relu = small[:, 512:1536].rearrange("p (i s) -> p i s", i=2)
        score = small[:, 0:512]
        bias_of = [maskb[:, 64 * ch * (ch + 1):64 * ch * (ch + 1) + P * (ch + 1)] for ch in range(C)]
        sh1c, A1, ss, rstd, ss2, rstd2 = (col[:, 0:8], col[:, 8:16], col[:, 16:20], col[:, 20:24],
                                          col[:, 24:28], col[:, 28:32])
        ss3, rstd3, ss4, rstd4 = (col[:, 32 + 4 * i:36 + 4 * i] for i in range(4))
        eps = col[:, 48:49]
        lgT = T3[0:NE, 2, :]
        lr = attn[:, 640:640 + C * (NE + 8)].rearrange("p (c e) -> p c e", c=C)
        ex = attn[:, 512:512 + C * NE].rearrange("p (c e) -> p c e", c=C)
        OHE = 4
        ohw = OHE * C * slots // 2
        oh = [attn[:, at:at + ohw].bitcast(BF16).rearrange("p (e c s) -> p e c s", e=OHE, c=C)
              for at in (2048, 4096)]
        b3 = maskb[0:3 * NE, 0:512].bitcast(BF16)
        braw = T3[0:3 * NE, 0:2, :].rearrange("p a t -> p (a t)")
        bres = uvp[0:3 * NE, :, :].rearrange("p a t -> p (a t)")
        XG = apad[:, :, :].rearrange("p g t -> p (g t)").rearrange("p (b d) -> p b d", b=2)
        xgT = mix[:, 0:KD * slots].rearrange("p (k s) -> p k s", k=KD)
        Y = mix[:, 1024:3072].rearrange("p (b d) -> p b d", b=2)
        gt = mix[0:slots, 3072:3584]
        up1 = mix[0:slots, 3584:4096]
        th = attn[0:slots, 512:1024]
        av = attn[0:slots, 1024:1536]
        actT = attn[:, 1536:1536 + KF * slots].rearrange("p (k s) -> p k s", k=KF)
        wtT = T3[0:NE, 0, :]
        bdn = late[0:NE, 0:2, :]
        fgb = late[:, 2:4, :].rearrange("p a t -> p (a t)")
        YB_BANKS = (0, 1, 4, 5, 6, 7, 2, 3)
        Yin = ring[0].rearrange("p (c d) -> p c d", c=C)
        res = ring[1].rearrange("p (c d) -> p c d", c=C)
        zero = area_b[:, 0:512]

        def ada_piece(j):
            return w_ada[0, :, j * CH:(j + 1) * CH].rearrange("(p k) n -> p k n", k=KD)

        def in_piece(at, width):
            return w_in[0, :, at:at + width].rearrange("(k p) n -> p k n", p=P)

        PIECES = ([("a", j, ada_piece(j)) for j in range(4)]
                  + [("tok", 0, in_piece(COL_TOK, TOKW)), ("q", 0, in_piece(COL_Q, AW))]
                  + [("a", 4, ada_piece(4)), ("a", 5, ada_piece(5)), ("pool", 0, in_piece(COL_POOL, PW))]
                  + [("a", 6, ada_piece(6)), ("a", 7, ada_piece(7)), ("gb", 0, in_piece(COL_GB, CH))]
                  + [("a", 8, ada_piece(8)), ("a", 9, ada_piece(9)), ("gb", 1, in_piece(COL_GB + CH, CH))]
                  + [("a", 10, ada_piece(10)), ("a", 11, ada_piece(11))]
                  + [("wb", 0, w_b_up[0].rearrange("(k p) n -> p k n", p=P))]
                  + [("ga", i, in_piece(COL_GA + i * CH, CH)) for i in range(2)]
                  + [("wa", 0, w_a_up[0].rearrange("(k p) n -> p k n", p=P))]
                  + [("wo", i, w_out[0, :, i * CH:(i + 1) * CH].rearrange("(k p) n -> p k n", p=P))
                     for i in range(2)])
        FR = 4
        slot_of = [n if n < FR else (n - FR) % 3 for n in range(len(PIECES))]
        before = [None if n < FR else max(m for m in range(n) if slot_of[m] == slot_of[n])
                  for n in range(len(PIECES))]
        NFP = len(PIECES)
        place = {(k, i): n for n, (k, i, _) in enumerate(PIECES)}
        LAST_JOB = {("tok", 0): ("tok", C - 1), ("q", 0): ("q", 3), ("pool", 0): ("pool", PG - 1),
                    ("gb", 0): ("gb", 3), ("gb", 1): ("gb", 7), ("wb", 0): ("B", KD - 1),
                    ("ga", 0): ("ga", 3), ("ga", 1): ("ga", 7), ("wa", 0): ("A", KD - 1),
                    ("wo", 0): ("out", 2 * C - 2), ("wo", 1): ("out", 2 * C - 1)}

        def piece(kind, i=0):
            s = slot_of[place[kind, i]]
            src = PIECES[place[kind, i]][2]
            k, n = src.shape[1], src.shape[2]
            return ring[s][:, 0:k * n].rearrange("p (k n) -> p k n", k=k)

        JOBS = ([("sv", 0, "D")]
                + [("xT", i, "A") for i in range(8)]
                + [("adac", 0, "D")]
                + [("tok", i, "D") for i in range(C)] + [("uk", 0, "A")] + [("tr", i, "A") for i in range(C)]
                + [("idx", 4 + i, "A") for i in range(4)]
                + [("q", i, "A") for i in range(4)] + [("qlat", h, "A") for h in range(H)]
                + [("idx", 8 + i, "A") for i in range(4)]
                + [("pool", i, "A") for i in range(PG)]
                + [("idx", 12 + i, "A") for i in range(4)])
        NGR = 2 * C
        JOBS += [("L", i, "D") for i in range(4)] + [("gb", 0, "A")]
        for g in range(NGR):
            JOBS += [("PT", 4 * g + i, "A") for i in range(4)]
            if g < NGR - 1:
                JOBS += [("L", 4 * g + 4 + i, "D") for i in range(4)]
            JOBS += [("O", g, "A")]
            if g < NGR - 1:
                JOBS += [("gb", g + 1, "A")]
            if g == 0:
                JOBS += [("z", i, "A") for i in range(PG)]
            if g % 2:
                JOBS += [("V", g // 2, "A")]
            if g == 1:
                JOBS += [("row", j, "D") for j in range(4, 8)]
        JOBS += [("B", m, "D") for m in range(KD)]
        JOBS += [("row", j, "D") for j in range(8, 12)]
        JOBS += [("ga", 0, "A")]
        for m in range(KD):
            if m < KD - 1:
                JOBS += [("ga", m + 1, "A")]
            JOBS += [("A", m, "D")]
        JOBS += [("out", 2 * ch, "D") for ch in range(C)]
        for ch in range(C):
            JOBS += [("out", 2 * ch + 1, "D")]
            if ch:
                JOBS += [("h2T", 2 * ch - 2, "A"), ("h2T", 2 * ch - 1, "A")]
            if ch > 1:
                JOBS += [("rout", ch - 2, "A")]
        JOBS += [("rout", 2, "A"), ("h2T", 6, "A"), ("h2T", 7, "A"), ("rout", 3, "A"), ("rt", 0, "D"), ("rank", 0, "D"),
                 ("ix", 0, "D"), ("ix", 1, "D")]
        number = {(k, i): n for n, (k, i, _) in enumerate(JOBS)}
        emptied = [sum(1 for j in JOBS[:n + 1] if j[2] == JOBS[n][2]) for n in range(len(JOBS))]

        def bank(kind, i=0):
            return ps[:, number[kind, i] % 8, :]

        piece_in = [sem(f"piece_in{i}") for i in range(4)]
        x_back = [sem(f"x_back{i}") for i in range(C)]
        o_hi_ok, o_lo_ok = sem("o_hi_ok"), sem("o_lo_ok")
        o_used = sem("o_used")
        h_hi_ok, h_lo_ok = sem("h_hi_ok"), sem("h_lo_ok")
        u_hi_ok, u_lo_ok = sem("u_hi_ok"), sem("u_lo_ok")
        zo_hi_ok, zo_lo_ok = sem("zo_hi_ok"), sem("zo_lo_ok")
        b_hi_ok, b_lo_ok = sem("b_hi_ok"), sem("b_lo_ok")
        acc_ok = sem("acc_ok")
        job_done = sem("job_done")
        by_act, by_vec = sem("by_act"), sem("by_vec")
        c_in, x_in, sv_in, kvg_in = sem("c_in"), sem("x_in"), sem("sv_in"), sem("kvg_in")
        uk_in, uv_in, pool_in, wr_in, bg_in = (sem("uk_in"), sem("uv_in"), sem("pool_in"),
                                               sem("wr_in"), sem("bg_in"))
        brow_in, row_out, rows_in, g2_in = sem("brow_in"), sem("row_out"), sem("rows_in"), sem("g2_in")
        h2_out, wt_out, zero_out = sem("h2_out"), sem("wt_out"), sem("zero_out")
        consts, cnt_ok, icnt_ok = sem("consts"), sem("cnt_ok"), sem("icnt_ok")
        th_c = sem("th_c")
        ss_ok, rstd_ok, xn_ok = sem("ss_ok"), sem("rstd_ok"), sem("xn_ok")
        hT_ok = sem("hT_ok")
        ss2_ok = sem("ss2_ok")
        relu_used = sem("relu_used")
        d_ok = sem("d_ok")
        select_ok = sem("select_ok")
        max_ok, exp_ok, prob_ok = sem("max_ok"), sem("exp_ok"), sem("prob_ok")
        ss3_ok, h2_ok = sem("ss3_ok"), sem("h2_ok")
        nm_ok, ex_ok, wt_ok = sem("nm_ok"), sem("ex_ok"), sem("wt_ok")
        iug_ok, ius_ok, wc_ok = sem("iug_ok"), sem("ius_ok"), sem("wc_ok")
        pool_steps, dve_steps = sem("pool_steps"), sem("dve_steps")
        up_ok, prod_ok = sem("up_ok"), sem("prod_ok")
        mask_ok, oh_ok, oh_used, idx_ok = sem("mask_ok"), sem("oh_ok"), sem("oh_used"), sem("idx_ok")
        b3_ok = sem("b3_ok")
        act_chain, dve_chain, pool_chain = sem("act_chain"), sem("dve_chain"), sem("pool_chain")
        xg_in = [sem("xg_in0"), sem("xg_in1")]
        tx_done = sem("tx_done")
        gt_ok, th_ok, av_ok = sem("gt_ok"), sem("th_ok"), sem("av_ok")
        hi_ok, lo_ok = sem("hi_ok"), sem("lo_ok")
        granule_used = sem("granule_used")
        xh_ok, xl_ok = sem("xh_ok"), sem("xl_ok")
        ta_done, actT_ok, dn_done, y_ok = sem("ta_done"), sem("actT_ok"), sem("dn_done"), sem("y_ok")
        y_added = sem("y_added")
        ov_go, ov_w, ov_oh, ov_ix, ov_idx, ov_xg = (sem("ov_" + n) for n in
                                                    ("go", "w", "oh", "ix", "idx", "xg"))
        ov_tx, ov_xt, ov_gu, ov_gt, ov_th, ov_av = (sem("ov_" + n) for n in
                                                    ("tx", "xt", "gu", "gt", "th", "av"))
        ov_ta, ov_at, ov_dn, ov_y, ov_add = (sem("ov_" + n) for n in ("ta", "at", "dn", "y", "add"))
        ov_rk, ov_i1, ov_up, ov_wc = (sem("ov_" + n) for n in ("rk", "i1", "up", "wc"))
        OVER = (T - 1) // slots
        moe_done, bd_ok, bd_in, fg_in = sem("moe_done"), sem("bd_ok"), sem("bd_in"), sem("fg_in")
        y_in = [sem(f"y_in{i}") for i in range(C)]
        wtT_done, wtT_ok, yb_done = sem("wtT_done"), sem("wtT_ok"), sem("yb_done")
        x2_ok, ss4_ok, res_ok, out_done = sem("x2_ok"), sem("ss4_ok"), sem("res_ok"), sem("out_done")

        def rows(dram):
            return dram.rearrange("(c p) d -> p c d", p=P)

        def spread(row, n=D):
            return row.rearrange("(o n) -> o n", o=1).broadcast_to([P, n])

        def expert_pieces(e):
            gu = w_gu[0, bass.ds(e, 1), :, :].rearrange("a (k p) n -> p (a k) n", p=P)
            dn = w_down[0, bass.ds(e, 1), :, :].rearrange("a (k p) n -> p (a k) n", p=P)
            return gu[:, :, 0:DFF], gu[:, :, DFF:2 * DFF], dn

        SG, SU, SD = FR - 1, slot_of[NFP - 3], (slot_of[NFP - 2], slot_of[NFP - 1])
        gate_w, up_w = (ring[s].rearrange("p (k n) -> p k n", k=KD) for s in (SG, SU))
        down_w = [ring[s].rearrange("p (k n) -> p k n", k=KF) for s in SD]
        front_of = [slot_of.count(s) for s in range(FR)]

        def came(eng, slot, n):
            eng.wait_ge(piece_in[slot], n * 16 + 16 * (front_of[slot] + 1))

        def front_came(eng, kind, i=0):
            n = place[kind, i]
            eng.wait_ge(piece_in[slot_of[n]], 16 * (slot_of[:n + 1].count(slot_of[n])))

        BLOCKS = [(kind, m) for kind, count in (("q", 4), ("pool", PG), ("gb", KD), ("ga", KD)) for m in range(count)]
        block_no = {kb: n for n, kb in enumerate(BLOCKS)}
        turns = [(j[0], j[1]) for j in JOBS if (j[0], j[1]) in block_no or j[0] in ("B", "A")]
        turns += [("merged", k) for k in range(KD)]
        turn_no = {kb: n for n, kb in enumerate(turns)}
        wb_flat = wb_hl[:, :, :, :, :].rearrange("p b a k n -> p b a (k n)")

        def merged_part(k, a):
            return wb_flat[:, buffer_of(("merged", k)), a, 0:T]

        def w_out_part(k, a):
            return wb_flat[:, buffer_of(("merged", k)), a, T:T + CH]


        def buffer_of(kb):
            return turn_no[kb] % 2

        def buffer_free(eng, kb):
            if turn_no[kb] >= 2:
                kind, m = turns[turn_no[kb] - 2]
                if kind == "merged":
                    eng.wait_ge(o_used, m + 1)
                else:
                    eng.wait_ge(job_done, number[kind, m] + 1)

        def up_w_block(kind, m):
            return piece("wb" if kind == "B" else "wa")[:, :, m * P:(m + 1) * P]


        def block_w(n):
            kind, m = BLOCKS[n]
            return piece(kind, m // 4)[:, :, (m % 4) * P:(m % 4 + 1) * P]

        def turned(b):
            return ps[:, b, :].rearrange("p (k s) -> p k s", k=4)[:, :, 0:slots]

        block = ctx.enter_context(nc.Block())

        @block.sync
        def _(sp):
            sp.dma_start(cnd[:, 0, :], c[0, :].rearrange("(p k) -> p k", k=KD)).then_inc(c_in, 16)
            sp.dma_start(X[:, :, :], rows(x[0])).then_inc(x_in, 16)
            sp.dma_start(sv[0:16, :], b_ada[0, 0:2 * D].rearrange("(r n) -> r n", n=P)).then_inc(sv_in, 16)
            sp.dma_start(sv[16:24, :], norm1_g[0].rearrange("(r n) -> r n", n=P)).then_inc(sv_in, 16)
            sp.dma_start(sv[24:28, :], pool_scale[0].rearrange("(r n) -> r n", n=P)).then_inc(sv_in, 16)

            def used(n):
                kind, i, _ = PIECES[n]
                if kind == "a":
                    sp.wait_ge(acc_ok, i + 1)
                elif kind in ("wb", "wa"):
                    sp.wait_ge(u_lo_ok, KD if kind == "wb" else 2 * KD)
                elif kind in ("q", "pool", "gb", "ga"):
                    sp.wait_ge(b_lo_ok, block_no[LAST_JOB[kind, i]] + 1)
                else:
                    sp.wait_ge(job_done, number[LAST_JOB[kind, i]] + 1)

            for n, (kind, i, src) in enumerate(PIECES):
                if n >= FR:
                    used(before[n])
                sp.dma_start(piece(kind, i), src).then_inc(piece_in[slot_of[n]], 16)
                if n == 3:
                    sp.dma_start(kvgb[:, :], spread(kv_norm_g[0], LAT)).then_inc(kvg_in, 16)
                if n == 5:
                    sp.dma_start(wr[:, :, :], w_router[0].rearrange("(k p) n -> p k n", p=P)).then_inc(wr_in, 16)
                    sp.dma_start(br[:, :], b_router[0].rearrange("(e o) -> e o", o=1)).then_inc(wr_in, 16)
            sp.wait_ge(job_done, number["ga", KD - 1] + 1)
            for ch in range(C):
                sp.dma_start(X[:, ch, :], rows(x[0])[:, ch, :]).then_inc(x_back[ch], 16)
            srcs = expert_pieces(0)
            for j, slot, dst in ((1, SU, up_w), (0, SG, gate_w), (2, SD[0], down_w[0])):
                if j:
                    used(NFP - 4 + j)
                else:
                    sp.wait_ge(job_done, number["out", 2 * C - 2] + 1)
                sp.dma_start(dst, srcs[j]).then_inc(piece_in[slot], 16)

            def load_gate(e):
                sp.wait_ge(lo_ok, e * 2 * GP - GP)
                sp.dma_start(gate_w, expert_pieces(e)[0]).then_inc(piece_in[SG], 16)

            def load_rest(e, b, first=False, last=False):
                if first:
                    used(NFP - 1)
                    sp.dma_start(down_w[b], expert_pieces(e)[2]).then_inc(piece_in[SD[b]], 16)
                sp.wait_ge(lo_ok, e * 2 * GP)
                sp.dma_start(up_w, expert_pieces(e)[1]).then_inc(piece_in[SU], 16)
                if not last:
                    load_gate(e + 1)
                if not first:
                    sp.wait_ge(dn_done, e - 1)
                    sp.dma_start(down_w[b], expert_pieces(e)[2]).then_inc(piece_in[SD[b]], 16)

            load_gate(1)
            load_rest(1, 1, first=True)
            with sp.Fori(1, NE // 2 - 1) as i:
                load_rest(i * 2, 0)
                load_rest(i * 2 + 1, 1)
            load_rest(NE - 2, 0)
            load_rest(NE - 1, 1, last=True)
            sp.wait_ge(job_done, number["rout", C - 1] + 1)
            sp.dma_start(bdn, b_down[0].rearrange("e (a n) -> e a n", a=2)).then_inc(bd_in, 16)
            sp.dma_start(fgb, spread(final_g)).then_inc(fg_in, 16)
            most = sp.value_load(cmaxi[0:1, 0:1], min_val=0, max_val=T)
            with sp.If(most > slots):
                with sp.Fori(0, OVER) as r:
                    with sp.Fori(0, NE) as e:
                        sp.wait_ge(ov_go, r * NE + e + 1)
                        for d_, s_ in zip((gate_w, up_w, down_w[0]), expert_pieces(e)):
                            sp.dma_start(d_, s_).then_inc(ov_w, 16)
            sp.wait_ge(moe_done, 1)
            for ch in range(C):
                sp.dma_start(Yin[:, ch, :], rows(y_dram)[:, ch, :]).then_inc(y_in[ch], 16)
            for ch in range(C):
                sp.wait_ge(res_ok, ch + 1)
                sp.dma_start(rows(out[0])[:, ch, :], res[:, ch, :]).then_inc(out_done, 16)
            sp.wait_ge(out_done, 16 * C)

        @block.gpsimd
        def _(pool):
            chain = [0]

            def link(ins):
                chain[0] += 1
                ins.then_inc(pool_chain, 1)
                pool.wait_ge(pool_chain, chain[0])

            nc.gpsimd.memset(ones[:, :], 1.0)
            nc.gpsimd.memset(eps, EPS)
            nc.gpsimd.memset(onesb[:, :], 1.0)
            link(nc.gpsimd.memset(ident[:, :], 0.0))
            link(nc.gpsimd.affine_select(out=ident[:, :], in_=ident[:, :], compare_op=ALU.not_equal, fill=1.0,
                                         base=0, pattern=[[-1, P]], channel_multiplier=1))
            nc.gpsimd.drain().then_inc(consts, 1)
            link(nc.gpsimd.memset(uvp[:, :, :], 0.0))
            link(nc.gpsimd.memset(causal[:, :], 0.0))
            nc.gpsimd.affine_select(out=causal[:, :], in_=causal[:, :], compare_op=ALU.is_ge, fill=MASKED,
                                    base=0, pattern=[[-1, P]], channel_multiplier=1)
            link(nc.gpsimd.memset(bias_of[0], 0.0))
            nc.gpsimd.affine_select(out=bias_of[0], in_=bias_of[0], compare_op=ALU.is_ge, fill=HIDDEN,
                                    base=0, pattern=[[-1, P]], channel_multiplier=1)
            nc.gpsimd.affine_select(out=tri[:, :], in_=onesb[:, :], compare_op=ALU.is_gt, fill=0.0,
                                    base=0, pattern=[[1, P]], channel_multiplier=-1)
            nc.gpsimd.iota(iota[:, :], pattern=[[1, P]], base=0, channel_multiplier=0,
                           allow_small_or_imprecise_dtypes=True)
            nc.gpsimd.iota(tokid[:, :, 0], pattern=[[1, C]], base=0, channel_multiplier=0,
                           allow_small_or_imprecise_dtypes=True)
            nc.gpsimd.iota(tokid[:, :, 1], pattern=[[0, C]], base=0, channel_multiplier=1,
                           allow_small_or_imprecise_dtypes=True)
            nc.gpsimd.memset(tokid[:, :, 2], 1.0)
            link(nc.gpsimd.memset(sel3[:, :], 0.0))
            for part in range(3):
                link(nc.gpsimd.affine_select(out=sel3[:, :], in_=sel3[:, :], compare_op=ALU.not_equal, fill=1.0,
                                             base=-part * NE, pattern=[[-1, NE]], channel_multiplier=1))
            for g in range(PG):
                nc.gpsimd.iota(icnt[:, g, :], pattern=[[1, PAD]], base=1, channel_multiplier=0,
                               allow_small_or_imprecise_dtypes=True)
            nc.gpsimd.memset(lg[:, :, :], MASKED)
            nc.gpsimd.memset(apad[:, :, 0:PAD], 0.0)
            nc.gpsimd.memset(win[:, :, 0:PAD], 0.0)
            nc.gpsimd.drain().then_inc(consts, 1)
            front_came(pool, "tok")
            pool.dma_start(uk, w_uk[0].rearrange("l h d -> l (h d)")).then_inc(uk_in, 16)
            pool.dma_start(wpool, w_pool[0].rearrange("g c d -> c g d")).then_inc(pool_in, 16)
            for h in range(H):
                at = HD * (h % 2)
                pool.dma_start(uvp[:, h, at:at + HD], w_uv[0, :, h, :]).then_inc(uv_in, 16)
            pool.wait_ge(consts, 2)
            for g, w in enumerate(WINDOWS):
                last = nc.gpsimd.tensor_scalar(icnt[:, g, :], icnt[:, g, :], float(w), 0.0, ALU.min, ALU.max)
            last.then_inc(cnt_ok, 1)
            pool.wait_ge(icnt_ok, 1)

            def block_low(n):
                pool.wait_ge(b_hi_ok, n + 1)
                nc.gpsimd.tensor_tensor(wb_hl[:, buffer_of(BLOCKS[n]), 1, :, :], block_w(n),
                                        wb_hl[:, buffer_of(BLOCKS[n]), 0, :, :],
                                        ALU.subtract).then_inc(b_lo_ok, 1)

            for n in range(block_no["pool", 2]):
                block_low(n)
            for g, w in enumerate(WINDOWS):
                block_low(block_no["pool", g] + 2)
                pool.wait_ge(by_act, emptied[number["pool", g]])
                if g == 0:
                    pool.wait_ge(job_done, number["qlat", H - 1] + 1)
                src, span, n = apad[:, g, :], 1, 0
                while span < w:
                    dst = win[:, n % 2, :]
                    link(nc.gpsimd.tensor_tensor(dst[:, PAD:PAD + T], src[:, PAD:PAD + T],
                                                 src[:, PAD - span:PAD - span + T], ALU.add))
                    src, span, n = dst, 2 * span, n + 1
                link(nc.gpsimd.tensor_tensor(dT[:, g, 0:PAD], src[:, PAD:2 * PAD], icnt[:, g, :], ALU.mult))
                link(nc.gpsimd.tensor_scalar(dT[:, g, PAD:T], src[:, 2 * PAD:PAD + T], 1.0 / w, 0.0,
                                             ALU.mult, ALU.add))
                nc.gpsimd.tensor_tensor(dT[:, g, :], dT[:, g, :], apad[:, g, PAD:PAD + T],
                                        ALU.subtract).then_inc(d_ok, 1)

            pool.wait_ge(select_ok, 1)
            pool.wait_ge(job_done, number["z", PG - 1] + 1)
            for half in range(2):
                pool.dma_start(ada_half[half],
                               b_ada[0, 2 * D:6 * D].rearrange("(r a n) -> r a n", r=4, a=2)[:, half, :]
                               ).then_inc(brow_in, 16)
            for n in range(block_no["gb", 2], block_no["ga", 0]):
                block_low(n)
            pool.wait_ge(job_done, number["V", C - 1] + 1)
            for part in range(3):
                pool.dma_start(braw[part * NE:(part + 1) * NE, :], b_gu[0]).then_inc(bg_in, 16)
            pool.wait_ge(bg_in, 48)
            link(nc.gpsimd.tensor_copy(b3, braw))
            link(nc.gpsimd.tensor_tensor(bres, braw, b3, ALU.subtract))
            nc.gpsimd.tensor_copy(b3[NE:2 * NE, :], bres[NE:2 * NE, :])
            link(nc.gpsimd.tensor_copy(b3[2 * NE:3 * NE, :], bres[2 * NE:3 * NE, :]))
            link(nc.gpsimd.tensor_tensor(braw[2 * NE:3 * NE, :], bres[2 * NE:3 * NE, :],
                                         b3[2 * NE:3 * NE, :], ALU.subtract))
            nc.gpsimd.tensor_copy(b3[2 * NE:3 * NE, :], braw[2 * NE:3 * NE, :]).then_inc(b3_ok, 1)
            pool.wait_ge(b3_ok, 1)
            pool.wait_ge(zo_lo_ok, 1)
            link(nc.gpsimd.memset(zero, 0.0))
            yz = y_dram.rearrange("(p a) (b n) -> p (a b) n", a=T // P, n=CH)
            for j in range(8):
                pool.dma_start(yz[:, j, :], zero).then_inc(zero_out, 16)
            pool.wait_ge(by_vec, emptied[number["row", 11]])
            for half in range(2):
                pool.dma_start(ada_dram.rearrange("r (a n) -> r a n", a=2)[:, half, :],
                               ada_half[half]).then_inc(row_out, 16)
            pool.wait_ge(row_out, 32)
            pool.dma_start(g1b, spread(ada_dram[0])).then_inc(rows_in, 16)
            pool.dma_start(sh2b, spread(ada_dram[1])).then_inc(rows_in, 16)
            pool.dma_start(A2b, spread(ada_dram[2])).then_inc(rows_in, 16)
            pool.dma_start(n2b, spread(norm2_g[0])).then_inc(rows_in, 16)
            pool.wait_ge(job_done, number["A", KD - 1] + 1)
            link(nc.gpsimd.memset(XG[:, :, :], 0.0))
            for ch in range(C):
                pool.wait_ge(h2_ok, ch + 1)
                pool.dma_start(rows(h2_dram)[:, ch, 0:D], h2[:, ch, :]).then_inc(h2_out, 16)
            pool.wait_ge(ss3_ok, C)
            pool.dma_start(g2b, spread(ada_dram[3])).then_inc(g2_in, 16)
            pool.wait_ge(wt_ok, 1)
            pool.dma_start(rows(h2_dram)[:, :, D:HX], wth[:, :, :]).then_inc(wt_out, 16)
            last_row = pool.to_reg(T - 1)

            def gather(b, done):
                pool.indirect_dma_start(out=XG[0:slots, b, :], out_offset=None, in_=h2_dram,
                                        in_offset=bass.IndirectOffsetOnAxis(ap=iug[0:slots, b:b + 1], axis=0),
                                        bounds_check=last_row, oob_is_err=False).then_inc(done, 16)

            def scatter(b, which, done):
                pool.indirect_dma_start(out=y_dram, in_=Y[0:slots, b, :], in_offset=None,
                                        out_offset=bass.IndirectOffsetOnAxis(ap=which, axis=0),
                                        bounds_check=last_row, oob_is_err=False,
                                        compute_op=ALU.add).then_inc(done, 16)

            pool.wait_ge(h2_out, 16 * C)
            pool.wait_ge(wt_out, 16)
            pool.wait_ge(idx_ok, 1)
            for b in range(2):
                link(nc.gpsimd.tensor_copy(iug[:, b:b + 1], idx[:, b:b + 1]))
                gather(b, xg_in[b])
            pool.wait_ge(zero_out, 16 * 8)

            def wait_apart(s_, value):
                pool.wait_ge(s_, value)
                pool.sem_inc(pool_steps, 1)

            def gather_ahead(e, b):
                wait_apart(wc_ok, e + 1)
                nc.gpsimd.tensor_copy(iug[:, b:b + 1], idx[:, bass.ds(e + 2, 1)]).then_inc(iug_ok, 1)
                wait_apart(iug_ok, e + 1)
                gather(b, xg_in[b])

            def add_rows(e, b, first=False):
                if not first:
                    wait_apart(y_added, e * 16)
                nc.gpsimd.tensor_copy(ius[:, b:b + 1], idx[:, bass.ds(e, 1)]).then_inc(ius_ok, 1)
                pool.wait_ge(ius_ok, e + 1)
                wait_apart(y_ok, e + 1)
                scatter(b, ius[0:slots, b:b + 1], y_added)

            gather_ahead(0, 0)
            gather_ahead(1, 1)
            add_rows(0, 0, first=True)
            with pool.Fori(1, NE // 2 - 1) as i:
                gather_ahead(i * 2, 0)
                add_rows(i * 2 - 1, 1)
                gather_ahead(i * 2 + 1, 1)
                add_rows(i * 2, 0)
            add_rows(NE - 3, 1)
            pool.wait_ge(bd_in, 16)
            pool.wait_ge(g2_in, 16)
            nc.gpsimd.tensor_tensor(bdn, bdn, g2b[0:NE, :].rearrange("e (a n) -> e a n", a=2),
                                    ALU.mult).then_inc(bd_ok, 1)
            pool.wait_ge(bd_ok, 1)
            add_rows(NE - 2, 0)
            add_rows(NE - 1, 1)
            pool.wait_ge(y_added, 16 * NE)
            most = pool.value_load(cmaxi[0:1, 0:1], min_val=0, max_val=T)
            with pool.If(most > slots):
                pool.sem_inc(ov_go, 1)
                with pool.Fori(0, OVER) as r:
                    with pool.Fori(0, NE) as e:
                        n = r * NE + e
                        wait_apart(ov_idx, n + 1)
                        gather(0, ov_xg)
                        wait_apart(ov_y, n + 1)
                        scatter(0, iug[0:slots, 0:1], ov_add)
                        pool.wait_ge(ov_add, n * 16 + 16)
                        pool.sem_inc(ov_go, 1)
            pool.sem_inc(moe_done, 1)

        @block.scalar
        def _(act):
            chain = [0]

            def link(ins):
                chain[0] += 1
                ins.then_inc(act_chain, 1)
                act.wait_ge(act_chain, chain[0])

            def job(kind, i=0):
                act.wait_ge(job_done, number[kind, i] + 1)
                return bank(kind, i)

            act.wait_ge(c_in, 16)
            nc.scalar.activation(cnd[:, 1, :], cnd[:, 0, :], ACT.Tanh, scale=0.5).then_inc(th_c, 1)
            act.wait_ge(x_in, 16)
            act.wait_ge(consts, 1)
            for ch in range(C):
                link(nc.scalar.activation(xn[:, ch, :], X[:, ch, :], ACT.Square, accum_out=ss[:, ch:ch + 1]))
            nc.scalar.activation(ss, ss, ACT.Sqrt, scale=1.0 / D, bias=eps).then_inc(ss_ok, 1)
            act.wait_ge(rstd_ok, 1)
            for ch in range(C):
                nc.scalar.activation(xn[:, ch, :], X[:, ch, :], ACT.Copy,
                                     scale=rstd[:, ch:ch + 1]).then_inc(xn_ok, 1)
            for i in range(8):
                ch, half = i // 2, i % 2
                nc.scalar.activation(hT[:, 4 * half:4 * half + 4, ch * P:(ch + 1) * P],
                                     job("xT", i).rearrange("p (k t) -> p k t", k=4), ACT.Copy).then_inc(by_act, 1)
            act.wait_ge(xn_ok, C)
            act.wait_ge(hT_ok, KD)
            for k in range(KD):
                last = nc.scalar.activation(h_hi[:, k, :], hT[:, k, :], ACT.Copy)
            last.then_inc(h_hi_ok, 1)
            def block_high(n):
                if n >= len(BLOCKS):
                    return
                front_came(act, BLOCKS[n][0], BLOCKS[n][1] // 4)
                buffer_free(act, BLOCKS[n])
                nc.scalar.activation(wb_hl[:, buffer_of(BLOCKS[n]), 0, :, :], block_w(n), ACT.Copy).then_inc(b_hi_ok, 1)

            act.wait_ge(acc_ok, 4)
            block_high(block_no["q", 0])
            block_high(block_no["q", 1])
            for ch in range(C):
                link(nc.scalar.activation(ckv[:, ch, :], job("tok", ch)[:, 0:LAT], ACT.Square,
                                          accum_out=ss2[:, ch:ch + 1]))
                nc.scalar.activation(ss2[:, ch:ch + 1], ss2[:, ch:ch + 1], ACT.Sqrt, scale=1.0 / LAT,
                                     bias=eps).then_inc(ss2_ok, 1)
            nc.scalar.activation(ukT[:, :, :].rearrange("p a l -> p (a l)"), job("uk"), ACT.Copy).then_inc(by_act, 1)
            for ch in range(C):
                nc.scalar.activation(T3[:, :, ch * P:(ch + 1) * P],
                                     job("tr", ch)[:, 0:3 * P].rearrange("p (a t) -> p a t", a=3),
                                     ACT.Copy).then_inc(by_act, 1)

            relus = [0]

            def index_chunk(ch):
                n = P * (ch + 1)
                for h in range(IH):
                    src = job("idx", 4 * ch + h)
                    if relus[0] >= 2:
                        act.wait_ge(relu_used, relus[0] - 1)
                    nc.scalar.activation(relu[:, relus[0] % 2, 0:n], src[:, 0:n], ACT.Relu).then_inc(by_act, 1)
                    relus[0] += 1

            def up_high(kind, m):
                front_came(act, "wb" if kind == "B" else "wa")
                buffer_free(act, (kind, m))
                nc.scalar.activation(wb_hl[:, buffer_of((kind, m)), 0, 0:PG, :], up_w_block(kind, m),
                                     ACT.Copy).then_inc(u_hi_ok, 1)

            index_chunk(1)
            for i in range(4):
                nc.scalar.activation(qT[:, i, :], job("q", i), ACT.Copy).then_inc(by_act, 1)
                block_high(block_no["q", i] + 2)
            for h in range(H):
                nc.scalar.activation(q_latT[:, h, :], job("qlat", h), ACT.Copy).then_inc(by_act, 1)
            index_chunk(2)
            for g in range(PG):
                nc.scalar.activation(apad[:, g, PAD:PAD + T], job("pool", g), ACT.Copy).then_inc(by_act, 1)
                block_high(block_no["pool", g] + 2)
            index_chunk(3)
            def exponentials(g):
                n = P * (g // 2 + 1)
                for i in range(4):
                    s = 4 * g + i
                    act.wait_ge(max_ok, s + 1)
                    nc.scalar.activation(Lt[:, i, 0:n], Lt[:, i, 0:n], ACT.Exp, scale=SCALE,
                                         bias=am[:, 1, s:s + 1], accum_out=am[:, 2, s:s + 1]).then_inc(exp_ok, 1)

            def gate_b(g):
                nc.scalar.activation(mT[:, g, :], job("gb", g), ACT.Tanh, scale=0.5).then_inc(by_act, 1)
                if g < KD - 2:
                    block_high(block_no["gb", g + 2])

            exponentials(0)
            gate_b(0)
            for g in range(NGR):
                ch, hh = g // 2, g % 2
                n = P * (ch + 1)
                for i in range(4):
                    src = job("PT", 4 * g + i)
                    nc.scalar.activation(pT[:, 0:ch + 1, i, :], src[:, 0:n].rearrange("p (s q) -> p s q", q=P),
                                         ACT.Copy).then_inc(by_act, 1)
                if g == NGR - 1:
                    act.wait_ge(job_done, number["L", 4 * NGR - 1] + 1)
                    for k in range(PG):
                        last = nc.scalar.activation(zo_hl[:, 0, k, :], zT[:, k, :], ACT.Copy)
                    last.then_inc(zo_hi_ok, 1)
                    up_high("B", 0)
                    up_high("B", 1)
                if g == 0:
                    act.wait_ge(d_ok, PG)
                nc.scalar.activation(o_latT[:, 4 * hh:4 * hh + 4, :].rearrange("p h q -> p (h q)"),
                                     job("O", g), ACT.Copy).then_inc(by_act, 1)
                if g < NGR - 1:
                    exponentials(g + 1)
                    gate_b(g + 1)
                if g == 0:
                    for i in range(PG):
                        nc.scalar.activation(zT[:, i, :], job("z", i), ACT.Copy,
                                             scale=svT[:, 24 + i:25 + i]).then_inc(by_act, 1)
                if hh:
                    nc.scalar.activation(oT[:, :, ch * P:(ch + 1) * P],
                                         job("V", ch).rearrange("p (a q) -> p a q", a=4),
                                         ACT.Copy).then_inc(by_act, 1)
            for m in range(2, KD):
                up_high("B", m)
            block_high(block_no["ga", 0])
            block_high(block_no["ga", 1])
            act.wait_ge(job_done, number["B", KD - 1] + 1)
            for k in range(PG):
                last = nc.scalar.activation(zo_hl[:, 0, k, :], oT[:, k, :], ACT.Copy)
            last.then_inc(zo_hi_ok, 1)
            for m in range(KD):
                src = job("ga", m)
                if m >= 2:
                    act.wait_ge(by_vec, emptied[number["A", m - 2]])
                nc.scalar.activation(relu[:, m % 2, :], src, ACT.Tanh, scale=0.5).then_inc(by_act, 1)
                up_high("A", m)
                block_high(block_no["ga", m] + 2)
            def weights_high(e, up, first=False):
                came(act, SU if up else SG, e)
                w = up_w if up else gate_w
                for j in range(GP):
                    if not first:
                        act.wait_ge(granule_used, e * 2 * GP + (up * GP + j - NG + 1))
                    nc.scalar.activation(whl[:, j % NG, 0, :, :], w[:, j * GK:(j + 1) * GK, :],
                                         ACT.Copy).then_inc(hi_ok, 1)

            for k in range(KD):
                front_came(act, "wo", 0)
                act.wait_ge(by_vec, emptied[number["A", k]])
                buffer_free(act, ("merged", k))
                nc.scalar.activation(merged_part(k, 0), mT[:, k, :], ACT.Copy)
                nc.scalar.activation(w_out_part(k, 0), piece("wo", 0)[:, k, :], ACT.Copy).then_inc(o_hi_ok, 1)
            def h2T_copy(ch):
                for half in range(2):
                    nc.scalar.activation(h2T[:, 4 * half:4 * half + 4, ch * P:(ch + 1) * P],
                                         job("h2T", 2 * ch + half).rearrange("p (k t) -> p k t", k=4),
                                         ACT.Copy).then_inc(by_act, 1)

            def logits(ch):
                act.wait_ge(wr_in, 32)
                nc.scalar.activation(lgT[:, ch * P:(ch + 1) * P], job("rout", ch)[0:NE, 0:P], ACT.Identity,
                                     bias=br[:, 0:1]).then_inc(by_act, 1)

            for ch in range(C):
                act.wait_ge(by_vec, emptied[number["out", 2 * ch + 1]])
                link(nc.scalar.activation(sq, X[:, ch, :], ACT.Square, accum_out=ss3[:, ch:ch + 1]))
                nc.scalar.activation(ss3[:, ch:ch + 1], ss3[:, ch:ch + 1], ACT.Sqrt, scale=1.0 / D,
                                     bias=eps).then_inc(ss3_ok, 1)
                if ch:
                    h2T_copy(ch - 1)
                if ch > 1:
                    logits(ch - 2)
            logits(C - 2)
            h2T_copy(C - 1)
            logits(C - 1)
            act.wait_ge(nm_ok, 1)
            for ch in range(C):
                nc.scalar.activation(ex[:, ch, :], lg[:, ch, 0:NE], ACT.Exp, bias=nm1[:, ch:ch + 1]).then_inc(ex_ok, 1)
            act.wait_ge(h2_out, 16 * C)
            act.wait_ge(zero_out, 16 * 8)
            weights_high(0, 0, first=True)

            def xgT_copy(ok):
                nc.scalar.activation(xgT[:, 0:4, :], turned(4), ACT.Copy)
                nc.scalar.activation(xgT[:, 4:8, :], turned(5), ACT.Copy).then_inc(ok, 1)

            def rows_high(e):
                act.wait_ge(tx_done, e + 1)
                nc.scalar.activation(xhl[:, 0, 0:4, :], turned(4), ACT.Copy)
                nc.scalar.activation(xhl[:, 0, 4:8, :], turned(5), ACT.Copy).then_inc(xh_ok, 1)

            def tanh_gate(e):
                act.wait_ge(gt_ok, e + 1)
                nc.scalar.activation(th, gt, ACT.Tanh, scale=0.5 * ALPHA).then_inc(th_ok, 1)

            def token_weights(e, b):
                nc.scalar.activation(WC[0:slots, b:b + 1], XG[0:slots, b, bass.ds(e + D, 1)], ACT.Copy).then_inc(wc_ok, 1)

            def actT_copy(e):
                act.wait_ge(ta_done, e + 1)
                nc.scalar.activation(actT[:, :, :], turned(6), ACT.Copy).then_inc(actT_ok, 1)

            def expert(e, b, last=False):
                weights_high(e, 1)
                tanh_gate(e)
                if not last:
                    weights_high(e + 1, 0)
                    rows_high(e + 1)
                actT_copy(e)
                if not last:
                    act.wait_ge(y_ok, e)
                    token_weights(e + 1, 1 - b)

            rows_high(0)
            token_weights(0, 0)
            weights_high(0, 1)
            tanh_gate(0)
            weights_high(1, 0)
            rows_high(1)
            token_weights(1, 1)
            actT_copy(0)
            expert(1, 1)
            expert(2, 0)
            with act.Fori(1, NE // 2 - 1) as i:
                expert(i * 2 + 1, 1)
                expert(i * 2 + 2, 0)
            act.wait_ge(wtT_done, 1)
            nc.scalar.activation(wtT, ps[0:NE, 7, :], ACT.Copy).then_inc(wtT_ok, 1)
            expert(NE - 1, 1, last=True)

            most = act.value_load(cmaxi[0:1, 0:1], min_val=0, max_val=T)
            with act.If(most > slots):
                with act.Fori(0, OVER) as r:
                    with act.Fori(0, NE) as e:
                        n = r * NE + e
                        act.wait_ge(ov_tx, n + 1)
                        xgT_copy(ov_xt)
                        act.wait_ge(ov_gt, n + 1)
                        nc.scalar.activation(th, gt, ACT.Tanh, scale=0.5 * ALPHA).then_inc(ov_th, 1)
                        act.wait_ge(ov_ta, n + 1)
                        nc.scalar.activation(actT[:, :, :], turned(6), ACT.Copy).then_inc(ov_at, 1)
                        nc.scalar.activation(WC[0:slots, 0:1], XG[0:slots, 0, bass.ds(e + D, 1)], ACT.Copy).then_inc(ov_wc, 1)

            act.wait_ge(ss_ok, 1)
            link(nc.scalar.activation(ss4[:, 0:1], eps, ACT.Sqrt))
            for ch in range(C):
                act.wait_ge(x2_ok, ch + 1)
                link(nc.scalar.activation(res[:, ch, :], X[:, ch, :], ACT.Square, accum_out=ss4[:, ch:ch + 1]))
                nc.scalar.activation(ss4[:, ch:ch + 1], ss4[:, ch:ch + 1], ACT.Sqrt, scale=1.0 / D,
                                     bias=eps).then_inc(ss4_ok, 1)

        @block.vector
        def _(dve):
            chain = [0]

            def link(ins):
                chain[0] += 1
                ins.then_inc(dve_chain, 1)
                dve.wait_ge(dve_chain, chain[0])

            def job(kind, i=0):
                dve.wait_ge(job_done, number[kind, i] + 1)
                return bank(kind, i)

            v = nc.vector
            dve.wait_ge(th_c, 1)
            link(v.scalar_tensor_tensor(out=cnd[:, 1, :], in0=cnd[:, 1, :], scalar=1.0, in1=cnd[:, 0, :],
                                        op0=ALU.add, op1=ALU.mult))
            link(v.tensor_scalar(cnd[:, 2, :], cnd[:, 1, :], 0.5, None, ALU.mult))
            dve.wait_ge(ss_ok, 1)
            v.reciprocal(rstd, ss).then_inc(rstd_ok, 1)
            v.tensor_copy(svT[:, :], job("sv")[:, 0:28]).then_inc(by_vec, 1)

            def ada(j):
                front_came(dve, "a", j)
                if j == 8:
                    dve.wait_ge(job_done, number["z", PG - 1] + 1)
                w, a = piece("a", j), acc[j]
                link(v.tensor_scalar(a, w[:, 0, :], cnd[:, 2, 0:1], None, ALU.mult))
                for k in range(1, KD):
                    ins = v.scalar_tensor_tensor(out=a, in0=w[:, k, :], scalar=cnd[:, 2, k:k + 1], in1=a,
                                                 op0=ALU.mult, op1=ALU.add)
                    if k < KD - 1:
                        link(ins)
                    else:
                        ins.then_inc(acc_ok, 1)

            for j in range(4):
                ada(j)
            b_ = job("adac")
            v.tensor_tensor(sh1c, b_[:, 0:8], svT[:, 0:8], ALU.add)
            link(v.tensor_tensor(A1, b_[:, 8:16], svT[:, 8:16], ALU.add))
            v.scalar_tensor_tensor(out=A1, in0=A1, scalar=1.0, in1=svT[:, 16:24], op0=ALU.add,
                                   op1=ALU.mult).then_inc(by_vec, 1)
            dve.wait_ge(by_vec, emptied[number["adac", 0]])
            dve.wait_ge(by_act, emptied[number["xT", 7]])
            for k in range(KD):
                v.tensor_scalar(hT[:, k, :], hT[:, k, :], A1[:, k:k + 1], sh1c[:, k:k + 1], ALU.mult,
                                ALU.add).then_inc(hT_ok, 1)
            dve.wait_ge(h_hi_ok, 1)
            for k in range(KD):
                last = v.tensor_tensor(h_lo[:, k, :], hT[:, k, :], h_hi[:, k, :], ALU.subtract)
            last.then_inc(h_lo_ok, 1)
            dve.wait_ge(kvg_in, 16)
            for ch in range(C):
                b_ = job("tok", ch)
                dve.wait_ge(ss2_ok, ch + 1)
                if ch >= 2:
                    dve.wait_ge(job_done, number["tr", ch - 2] + 1)
                link(v.reciprocal(rstd2[:, ch:ch + 1], ss2[:, ch:ch + 1]))
                v.scalar_tensor_tensor(out=ckv[:, ch, :], in0=b_[:, 0:LAT], scalar=rstd2[:, ch:ch + 1],
                                       in1=kvgb[:, :], op0=ALU.mult, op1=ALU.mult)
                v.tensor_copy(qk[:, ch % 2, 0:P], b_[:, LAT:LAT + P])
                v.tensor_copy(qk[:, ch % 2, P:2 * P].rearrange("p (a d) -> p a d", a=IH),
                              b_[:, 2 * P:2 * P + IDIM].rearrange("p (a d) -> p a d", a=1).broadcast_to([P, IH, IDIM]))
                v.tensor_scalar(wi[:, ch, :], b_[:, 2 * P + IDIM:2 * P + IDIM + IH], IDX_SCALE, None,
                                ALU.mult).then_inc(by_vec, 1)
            dve.wait_ge(by_vec, emptied[number["tok", C - 1]])

            relus = [0]

            def select(ch, apart=False):
                n = P * (ch + 1)
                s = score[:, 0:n]
                for h in range(IH):
                    dve.wait_ge(by_act, emptied[number["idx", 4 * ch + h]])
                    r = relu[:, relus[0] % 2, 0:n]
                    w = wi[:, ch, h:h + 1]
                    if h == 0:
                        ins = v.tensor_scalar(s, r, w, None, ALU.mult)
                    else:
                        to = r if apart and h == IH - 1 else s
                        ins = v.scalar_tensor_tensor(out=to, in0=r, scalar=w, in1=s, op0=ALU.mult, op1=ALU.add)
                    relus[0] += 1
                    ins.then_inc(relu_used, 1)
                    dve.wait_ge(relu_used, relus[0])
                s = to
                link(v.tensor_tensor(s[:, n - P:n], s[:, n - P:n], causal[:, :], ALU.add))
                if apart:
                    return
                take_best(s, K_SEL // 8)
                link(v.tensor_scalar(bias_of[ch], s, 2 * MASKED, HIDDEN, ALU.is_gt, ALU.mult))

            def take_best(s, times):
                for _ in range(times):
                    link(v.max(out=top8[:, :], in_=s))
                    link(v.match_replace(out=s, in_to_replace=top8[:, :], in_values=s, imm_value=TAKEN))

            dve.wait_ge(consts, 2)
            dve.wait_ge(cnt_ok, 1)
            v.reciprocal(icnt[:, :, :], icnt[:, :, :]).then_inc(icnt_ok, 1)
            select(1)
            ada(4)
            ada(5)
            select(2)
            ada(6)
            select(3, apart=True)
            dve.drain().then_inc(select_ok, 1)

            def ada_rows(j):
                r, half = (j - 4) // 2, (j - 4) % 2
                row = small[32 * r:32 * r + 1, 1536 * half:1536 * half + CH]
                v.tensor_tensor(row, job("row", j)[32 * r:32 * r + 1, :], row, ALU.add).then_inc(by_vec, 1)

            last_scores = relu[:, 1, :]
            TAKES = (2, 4, 1, 5, 4)
            ADAS = (2, 5, 6, 7)

            def maxima(g):
                ch = g // 2
                n = P * (ch + 1)
                for i in range(4):
                    s = 4 * g + i
                    if g:
                        dve.wait_ge(job_done, number["PT", s - 4] + 1)
                    v.tensor_tensor_reduce(out=Lt[:, i, 0:n], in0=job("L", s)[:, 0:n], in1=bias_of[ch], scale=1.0,
                                           scalar=-3.0e38, op0=ALU.add, op1=ALU.max,
                                           accum_out=am[:, 0, s:s + 1]).then_inc(by_vec, 1)
                    dve.wait_ge(by_vec, emptied[number["L", s]])
                    v.tensor_scalar(am[:, 1, s:s + 1], am[:, 0, s:s + 1], -SCALE, None, ALU.mult).then_inc(max_ok, 1)

            def zo_low(src, nth):
                dve.wait_ge(zo_hi_ok, nth)
                for k in range(PG):
                    last = v.tensor_tensor(zo_hl[:, 1, k, :], src[:, k, :], zo_hl[:, 0, k, :], ALU.subtract)
                last.then_inc(zo_lo_ok, 1)

            def up_low(kind, m):
                dve.wait_ge(u_hi_ok, (KD if kind == "A" else 0) + m + 1)
                at = buffer_of((kind, m))
                v.tensor_tensor(wb_hl[:, at, 1, 0:PG, :], up_w_block(kind, m), wb_hl[:, at, 0, 0:PG, :],
                                ALU.subtract).then_inc(u_lo_ok, 1)

            def block_low(m):
                n = block_no["ga", m]
                dve.wait_ge(b_hi_ok, n + 1)
                v.tensor_tensor(wb_hl[:, buffer_of(BLOCKS[n]), 1, :, :], block_w(n),
                                wb_hl[:, buffer_of(BLOCKS[n]), 0, :, :], ALU.subtract).then_inc(b_lo_ok, 1)

            maxima(0)
            for g in range(NGR):
                n = P * (g // 2 + 1)
                for i in range(4):
                    s = 4 * g + i
                    dve.wait_ge(exp_ok, s + 1)
                    link(v.reciprocal(am[:, 3, s:s + 1], am[:, 2, s:s + 1]))
                    v.tensor_scalar(Lt[:, i, 0:n], Lt[:, i, 0:n], am[:, 3, s:s + 1], None,
                                    ALU.mult).then_inc(prob_ok, 1)
                if g == 2:
                    dve.wait_ge(brow_in, 32)
                    for j in range(4, 8):
                        ada_rows(j)
                if g < NGR - 1:
                    maxima(g + 1)
                if g == NGR - 1:
                    zo_low(zT, 1)
                    up_low("B", 0)
                    up_low("B", 1)
                if g == 0:
                    ada(7)
                if g in ADAS:
                    ada(8 + ADAS.index(g))
                if g < len(TAKES):
                    take_best(last_scores, TAKES[g])
                if g == len(TAKES) - 1:
                    link(v.tensor_scalar(bias_of[C - 1], last_scores, 2 * MASKED, HIDDEN, ALU.is_gt, ALU.mult))
            for m in range(KD):
                b_ = job("B", m)
                dve.wait_ge(by_act, emptied[number["gb", m]])
                v.scalar_tensor_tensor(out=mT[:, m, :], in0=mT[:, m, :], scalar=1.0, in1=b_, op0=ALU.add,
                                       op1=ALU.mult).then_inc(by_vec, 1)
                if m < KD - 2:
                    up_low("B", m + 2)
                else:
                    block_low(m + 2 - KD)
            for j in range(8, 12):
                ada_rows(j)
            zo_low(oT, 2)
            up_low("A", 0)
            def merged_low(k):
                dve.wait_ge(o_hi_ok, k + 1)
                v.tensor_tensor(merged_part(k, 1), mT[:, k, :], merged_part(k, 0), ALU.subtract)
                v.tensor_tensor(w_out_part(k, 1), piece("wo", 0)[:, k, :], w_out_part(k, 0),
                                ALU.subtract).then_inc(o_lo_ok, 1)

            for m in range(KD):
                if m < KD - 2:
                    block_low(m + 2)
                if m == KD - 2:
                    up_low("A", m + 1)
                if m == KD - 1:
                    merged_low(0)
                b_ = job("A", m)
                dve.wait_ge(by_act, emptied[number["ga", m]])
                t = relu[:, m % 2, :]
                link(v.scalar_tensor_tensor(out=t, in0=t, scalar=1.0, in1=b_, op0=ALU.add, op1=ALU.mult))
                v.tensor_tensor(mT[:, m, :], mT[:, m, :], t, ALU.add).then_inc(by_vec, 1)
                if m < KD - 2:
                    up_low("A", m + 1)
            for k in range(1, KD):
                merged_low(k)
            dve.wait_ge(rows_in, 64)
            link(v.scalar_tensor_tensor(out=A2b, in0=A2b, scalar=1.0, in1=n2b, op0=ALU.add, op1=ALU.mult))

            def weights_low(e, up, granules=range(GP)):
                w = up_w if up else gate_w
                for j in granules:
                    dve.wait_ge(hi_ok, e * 2 * GP + (up * GP + j + 1))
                    v.tensor_tensor(whl[:, j % NG, 1, :, :], w[:, j * GK:(j + 1) * GK, :], whl[:, j % NG, 0, :, :],
                                    ALU.subtract).then_inc(lo_ok, 1)

            def h2_rows(ch):
                dve.wait_ge(ss3_ok, ch + 1)
                link(v.reciprocal(rstd3[:, ch:ch + 1], ss3[:, ch:ch + 1]))
                link(v.scalar_tensor_tensor(out=h2[:, ch, :], in0=X[:, ch, :], scalar=rstd3[:, ch:ch + 1],
                                            in1=A2b, op0=ALU.mult, op1=ALU.mult))
                v.tensor_tensor(h2[:, ch, :], h2[:, ch, :], sh2b, ALU.add).then_inc(h2_ok, 1)

            def x1_half(ch, half):
                b_ = job("out", 2 * ch + half)
                sl = slice(half * CH, (half + 1) * CH)
                t = relu[:, ch % 2, :]
                link(v.scalar_tensor_tensor(out=t, in0=b_, scalar=0.5, in1=g1b[:, sl], op0=ALU.mult,
                                            op1=ALU.mult))
                v.tensor_tensor(X[:, ch, sl], X[:, ch, sl], t, ALU.add).then_inc(by_vec, 1)

            for ch in range(C):
                dve.wait_ge(x_back[ch], 16)
                x1_half(ch, 0)
            for ch in range(C):
                if ch:
                    h2_rows(ch - 1)
                x1_half(ch, 1)
            dve.wait_ge(by_vec, emptied[number["out", 2 * C - 1]])
            h2_rows(C - 1)

            v.tensor_copy(lg[:, :, 0:NE], job("rt")[:, 0:C * NE].rearrange("p (c e) -> p c e", c=C)).then_inc(by_vec, 1)
            dve.wait_ge(by_vec, emptied[number["rt", 0]])
            for ch in range(C):
                last = v.max(out=m8[:, ch, :], in_=lg[:, ch, 0:NE])
            link(last)
            v.tensor_scalar(nm1[:, :], m8[:, :, 0], -1.0, None, ALU.mult).then_inc(nm_ok, 1)
            link(v.memset(m8[:, :, TOPK:8], MASKED))
            for ch in range(C):
                last = v.match_replace(out=lr[:, ch, :], in_to_replace=m8[:, ch, :], in_values=lg[:, ch, :],
                                       imm_value=TAKEN)
            link(last)
            link(v.tensor_scalar(mask[:, :, :], lr[:, :, 0:NE], 2 * MASKED, None, ALU.is_lt))
            v.tensor_copy(maskh[:, :, :], mask[:, :, :]).then_inc(mask_ok, 1)
            def token_softmax():
                dve.wait_ge(ex_ok, C)
                link(v.tensor_tensor(wts[:, :, :], ex[:, :, :], mask[:, :, :], ALU.mult))
                link(v.reduce_sum(sm[:, 0, :], wts[:, :, :], axis=AX.X))
                link(v.reciprocal(sm[:, 1, :], sm[:, 0, :]))
                for ch in range(C):
                    last = v.tensor_scalar(wts[:, ch, :], wts[:, ch, :], sm[:, 1, ch:ch + 1], None, ALU.mult)
                link(last)
                v.tensor_scalar(wth[:, :, :], wts[:, :, :], 0.5, None, ALU.mult).then_inc(wt_ok, 1)

            b_ = job("rank")
            v.tensor_reduce(cmax[:, :], b_[:, C * NE:(C + 1) * NE], op=ALU.max, axis=AX.X)
            link(v.scalar_tensor_tensor(out=rankm[:, :, :], in0=b_[:, 0:C * NE].rearrange("p (c e) -> p c e", c=C),
                                        scalar=1.0, in1=mask[:, :, :], op0=ALU.add, op1=ALU.mult))
            v.tensor_copy(cmaxi[:, :], cmax[:, :])
            v.tensor_scalar(rankm[:, :, :], rankm[:, :, :], -1.0, None, ALU.add).then_inc(by_vec, 1)
            dve.wait_ge(by_vec, emptied[number["rank", 0]])

            def rows_low(e):
                dve.wait_ge(xh_ok, e + 1)
                for half in range(2):
                    ks = slice(4 * half, 4 * half + 4)
                    last = v.tensor_tensor(xhl[:, 1, ks, :], turned(4 + half), xhl[:, 0, ks, :], ALU.subtract)
                last.then_inc(xl_ok, 1)

            def gate_limit(e):
                dve.wait_ge(granule_used, e * 2 * GP + GP)
                v.tensor_scalar(gt, ps[0:slots, 0, :], LIMIT, None, ALU.min).then_inc(gt_ok, 1)

            def token_rows(b_, lo, n):
                b_ = b_[:, 0:3 * n].rearrange("p (e a) -> p e a", a=3)
                v.tensor_scalar(ixa[:, 0, lo:lo + n], b_[:, :, 2], -NOWHERE, NOWHERE, ALU.mult, ALU.add)
                link(v.tensor_scalar(ixa[:, 1, lo:lo + n], b_[:, :, 0], float(P), None, ALU.mult))
                link(v.tensor_tensor(ixa[:, 1, lo:lo + n], b_[:, :, 1], ixa[:, 1, lo:lo + n], ALU.add))
                return v.tensor_tensor(idx[:, lo:lo + n], ixa[:, 0, lo:lo + n], ixa[:, 1, lo:lo + n], ALU.add)

            for g in range(NE // OHE):
                if g >= 2:
                    dve.wait_ge(oh_used, g - 1)
                places = rankm[:, :, g * OHE:(g + 1) * OHE].rearrange("p c e -> p e c")
                v.tensor_tensor(oh[g % 2], iota[:, 0:slots].rearrange("p (a b s) -> p a b s", a=1, b=1)
                                .broadcast_to([P, OHE, C, slots]),
                                places.rearrange("p e (c o) -> p e c o", o=1).broadcast_to([P, OHE, C, slots]),
                                ALU.is_equal).then_inc(oh_ok, 1)
                if g == 0:
                    token_softmax()
                if g == 1:
                    dve.wait_ge(oh_used, 1)
                    token_rows(bank("ix", 0), 0, OHE).then_inc(idx_ok, 1)
                if g == 2:
                    weights_low(0, 0)
                if g == 3:
                    rows_low(0)
                if g == 5:
                    weights_low(0, 1)
                    gate_limit(0)
            weights_low(1, 0, range(1))
            dve.wait_ge(oh_used, NE // OHE)
            token_rows(bank("ix", 1), OHE, NE - OHE).then_inc(idx_ok, 1)

            def weighted(e, b, reused=True):
                dve.wait_ge(dn_done, e + 1)
                dve.wait_ge(wc_ok, e + 1)
                if reused:
                    dve.wait_ge(y_added, e * 16 - 16)
                for half in range(2):
                    sl = slice(half * CH, (half + 1) * CH)
                    last = v.scalar_tensor_tensor(out=Y[0:slots, b, sl], in0=ps[0:slots, 2 + half, :],
                                                  scalar=WC[0:slots, b:b + 1], in1=g2b[0:slots, sl],
                                                  op0=ALU.mult, op1=ALU.mult)
                last.then_inc(y_ok, 1)

            def expert(e, first=False, last=False):
                if not first:
                    weights_low(e, 1)
                    gate_limit(e)
                    if not last:
                        weights_low(e + 1, 0)
                dve.wait_ge(granule_used, e * 2 * GP + 2 * GP)
                v.tensor_scalar(up1, ps[0:slots, 1, :], LIMIT, -LIMIT, ALU.min, ALU.max).then_inc(up_ok, 1)
                dve.wait_ge(up_ok, e + 1)
                v.scalar_tensor_tensor(out=up1, in0=up1, scalar=1.0, in1=gt, op0=ALU.add,
                                       op1=ALU.mult).then_inc(prod_ok, 1)
                if not last and not first:
                    rows_low(e + 1)
                dve.wait_ge(prod_ok, e + 1)
                dve.wait_ge(th_ok, e + 1)
                v.scalar_tensor_tensor(out=av, in0=th, scalar=1.0, in1=up1, op0=ALU.add,
                                       op1=ALU.mult).then_inc(av_ok, 1)
                if first:
                    rows_low(e + 1)
                    weights_low(e + 1, 0, range(1, GP))

            dve.wait_ge(g2_in, 16)
            expert(0, first=True)
            expert(1)
            weighted(0, 0, reused=False)
            expert(2)
            weighted(1, 1, reused=False)
            with dve.Fori(1, NE // 2 - 1) as i:
                expert(i * 2 + 1)
                weighted(i * 2, 0)
                expert(i * 2 + 2)
                weighted(i * 2 + 1, 1)
            expert(NE - 1, last=True)
            weighted(NE - 2, 0)
            weighted(NE - 1, 1)

            most = dve.value_load(cmaxi[0:1, 0:1], min_val=0, max_val=T)
            with dve.If(most > slots):
                with dve.Fori(0, OVER) as r:
                    v.tensor_scalar(rankm[:, :, :], rankm[:, :, :], -float(slots), None, ALU.add).then_inc(ov_rk, 1)
                    dve.wait_ge(ov_rk, r + 1)
                    dve.sem_inc(dve_steps, 1)
                    with dve.Fori(0, NE) as e:
                        n = r * NE + e
                        dve.wait_ge(ov_go, n + 1)
                        for ch in range(C):
                            last = v.tensor_scalar(oh[0][:, 0, ch, :], iota[:, 0:slots], rankm[:, ch, bass.ds(e, 1)], None,
                                                   ALU.is_equal)
                        last.then_inc(ov_oh, 1)
                        dve.wait_ge(ov_ix, n + 1)
                        b_ = ps[:, 7, :]
                        v.tensor_scalar(ixa[:, 0, 0:1], b_[:, 2:3], -NOWHERE, NOWHERE, ALU.mult, ALU.add)
                        v.tensor_scalar(ixa[:, 1, 0:1], b_[:, 0:1], float(P), None, ALU.mult).then_inc(ov_i1, 1)
                        dve.wait_ge(ov_i1, n * 2 + 1)
                        v.tensor_tensor(ixa[:, 1, 0:1], b_[:, 1:2], ixa[:, 1, 0:1], ALU.add).then_inc(ov_i1, 1)
                        dve.wait_ge(ov_i1, n * 2 + 2)
                        v.tensor_tensor(iug[:, 0:1], ixa[:, 0, 0:1], ixa[:, 1, 0:1], ALU.add).then_inc(ov_idx, 1)
                        dve.wait_ge(ov_gu, n * 2 + 1)
                        v.tensor_scalar(gt, ps[0:slots, 0, :], LIMIT, None, ALU.min).then_inc(ov_gt, 1)
                        dve.wait_ge(ov_gu, n * 2 + 2)
                        v.tensor_scalar(up1, ps[0:slots, 1, :], LIMIT, -LIMIT, ALU.min, ALU.max).then_inc(ov_up, 1)
                        dve.wait_ge(ov_up, n * 2 + 1)
                        v.scalar_tensor_tensor(out=up1, in0=up1, scalar=1.0, in1=gt, op0=ALU.add,
                                               op1=ALU.mult).then_inc(ov_up, 1)
                        dve.wait_ge(ov_up, n * 2 + 2)
                        dve.wait_ge(ov_th, n + 1)
                        v.scalar_tensor_tensor(out=av, in0=th, scalar=1.0, in1=up1, op0=ALU.add,
                                               op1=ALU.mult).then_inc(ov_av, 1)
                        dve.wait_ge(ov_wc, n + 1)
                        dve.wait_ge(ov_dn, n + 1)
                        for half in range(2):
                            sl = slice(half * CH, (half + 1) * CH)
                            last = v.scalar_tensor_tensor(out=Y[0:slots, 0, sl], in0=ps[0:slots, 2 + half, :],
                                                          scalar=WC[0:slots, 0:1], in1=g2b[0:slots, sl],
                                                          op0=ALU.mult, op1=ALU.mult)
                        last.then_inc(ov_y, 1)

            def bias_rows(ch):
                for half in range(2):
                    sl = slice(half * CH, (half + 1) * CH)
                    dve.wait_ge(yb_done, 2 * ch + half + 1)
                    last = v.tensor_tensor(X[:, ch, sl], X[:, ch, sl], ps[:, YB_BANKS[2 * ch + half], :], ALU.add)
                link(last)

            for ch in range(C):
                bias_rows(ch)
            dve.wait_ge(fg_in, 16)

            def result(ch):
                dve.wait_ge(ss4_ok, ch + 1)
                link(v.reciprocal(rstd4[:, ch:ch + 1], ss4[:, ch:ch + 1]))
                v.scalar_tensor_tensor(out=res[:, ch, :], in0=X[:, ch, :], scalar=rstd4[:, ch:ch + 1], in1=fgb,
                                       op0=ALU.mult, op1=ALU.mult).then_inc(res_ok, 1)

            for ch in range(C):
                dve.wait_ge(y_in[ch], 16)
                v.tensor_tensor(X[:, ch, :], X[:, ch, :], Yin[:, ch, :], ALU.add).then_inc(x2_ok, 1)
                if ch:
                    result(ch - 1)
            dve.wait_ge(x2_ok, C)
            result(C - 1)

        @block.tensor
        def _(pe):
            mm = nc.tensor.matmul

            def start(kind, i=0):
                n = number[kind, i]
                if n >= 8:
                    pe.wait_ge(by_act if JOBS[n - 8][2] == "A" else by_vec, emptied[n - 8])
                return bank(kind, i)

            def have(kind, i=0):
                front_came(pe, kind, i)
                return piece(kind, i)

            def chain(out_, pairs, done=None, by=1, start_=True):
                for n, (a, b) in enumerate(pairs):
                    last = mm(out_, a, b, start=(n == 0 and start_), stop=(n == len(pairs) - 1))
                if done is not None:
                    last.then_inc(done, by)
                return last

            def emptied_by(kind, i=0):
                n = number[kind, i]
                pe.wait_ge(by_act if JOBS[n][2] == "A" else by_vec, emptied[n])

            pe.wait_ge(consts, 1)
            pe.wait_ge(sv_in, 48)
            nc.tensor.transpose(start("sv")[:, 0:28], sv[:, :], ident[0:28, 0:28]).then_inc(job_done, 1)
            for i in range(8):
                ch, half = i // 2, i % 2
                b_ = start("xT", i)
                pe.wait_ge(xn_ok, ch + 1)
                for k in range(4):
                    at = (4 * half + k) * P
                    last = nc.tensor.transpose(b_[:, k * P:(k + 1) * P], xn[:, ch, at:at + P], ident[:, :])
                last.then_inc(job_done, 1)
            b_ = start("adac")
            for j in range(4):
                pe.wait_ge(acc_ok, j + 1)
                for q in range(4):
                    last = mm(b_[:, 4 * j + q:4 * j + q + 1], acc[j][:, q * P:(q + 1) * P], ones[:, 0:1],
                              start=True, stop=True)
            last.then_inc(job_done, 1)
            w = have("tok")
            for ch in range(C):
                b_ = start("tok", ch)
                for k in range(KD):
                    pe.wait_ge(hT_ok, k + 1)
                    last = mm(b_[:, 0:TOKW], hT[:, k, ch * P:(ch + 1) * P], w[:, k, :], start=(k == 0), stop=(k == KD - 1))
                last.then_inc(job_done, 1)
            b_ = start("uk")
            pe.wait_ge(uk_in, 16)
            for i in range(4):
                last = nc.tensor.transpose(b_[:, i * P:(i + 1) * P], uk[:, i * P:(i + 1) * P], ident[:, :])
            last.then_inc(job_done, 1)
            for ch in range(C):
                b_ = start("tr", ch)
                emptied_by("tok", ch)
                nc.tensor.transpose(b_[:, 0:P], ckv[:, ch, :], ident[:, :])
                nc.tensor.transpose(b_[:, P:2 * P], qk[:, ch % 2, 0:P], ident[:, :])
                nc.tensor.transpose(b_[:, 2 * P:3 * P], qk[:, ch % 2, P:2 * P], ident[:, :]).then_inc(job_done, 1)

            def index_chunk(ch):
                emptied_by("tr", C - 1)
                for h in range(IH):
                    b_ = start("idx", 4 * ch + h)
                    r = slice(IDIM * h, IDIM * (h + 1))
                    mm(b_[:, 0:P * (ch + 1)], qiT[r, ch * P:(ch + 1) * P], kiT[r, 0:P * (ch + 1)], start=True,
                       stop=True, tile_position=(IDIM * h, 0)).then_inc(job_done, 1)

            def by_feature_parts(kind, m):
                n = block_no[kind, m]
                b_ = start(kind, m)
                pe.wait_ge(h_lo_ok, 1)
                pe.wait_ge(b_lo_ok, n + 1)
                at = buffer_of((kind, m))
                return chain(b_, [(wb_hl[:, at, a, k, :], h[:, k, :]) for k in range(KD)
                                  for a, h in ((0, h_hi), (0, h_lo), (1, h_hi))], job_done)

            index_chunk(1)
            for m in range(4):
                by_feature_parts("q", m)
            for h in range(H):
                b_ = start("qlat", h)
                emptied_by("q", h // 2)
                r = slice(HD * (h % 2), HD * (h % 2) + HD)
                mm(b_, ukT[r, h // 2, :], qT[r, h // 2, :], start=True, stop=True,
                   tile_position=(HD * (h % 2), 0)).then_inc(job_done, 1)
            index_chunk(2)
            for m in range(PG):
                by_feature_parts("pool", m)
            index_chunk(3)

            def ada_sum(j):
                b_ = start("row", j)
                pe.wait_ge(acc_ok, j + 1)
                mm(b_, ones[:, :], acc[j], start=True, stop=True).then_inc(job_done, 1)

            def logits(g):
                ch, hh = g // 2, g % 2
                for i in range(4):
                    b_ = start("L", 4 * g + i)
                    h = 4 * hh + i
                    emptied_by("qlat", h)
                    mm(b_[:, 0:P * (ch + 1)], q_latT[:, h, ch * P:(ch + 1) * P], ckvT[:, 0:P * (ch + 1)], start=True,
                       stop=True).then_inc(job_done, 1)

            def gate_b(g):
                by_feature_parts("gb", g)

            logits(0)
            gate_b(0)
            for g in range(NGR):
                ch, hh = g // 2, g % 2
                for i in range(4):
                    b_ = start("PT", 4 * g + i)
                    pe.wait_ge(prob_ok, 4 * g + i + 1)
                    for s in range(ch + 1):
                        last = nc.tensor.transpose(b_[:, s * P:(s + 1) * P], Lt[:, i, s * P:(s + 1) * P], ident[:, :])
                    last.then_inc(job_done, 1)
                if g < NGR - 1:
                    logits(g + 1)
                b_ = start("O", g)
                emptied_by("PT", 4 * g + 3)
                chain(b_, [(ckv[:, s, :], pT[:, s, :, :].rearrange("p h q -> p (h q)")) for s in range(ch + 1)], job_done)
                if g < NGR - 1:
                    gate_b(g + 1)
                if g == 0:
                    pe.wait_ge(pool_in, 16)
                    for i in range(PG):
                        b_ = start("z", i)
                        pe.wait_ge(d_ok, i + 1)
                        mm(b_, wpool[:, i, :], dT[:, i, :], start=True, stop=True).then_inc(job_done, 1)
                if hh:
                    b_ = start("V", ch)
                    pe.wait_ge(uv_in, 16 * H)
                    emptied_by("O", g)
                    for a in range(4):
                        last = chain(b_[:, a * P:(a + 1) * P],
                                     [(uvp[:, 2 * a + q, :], o_latT[:, 2 * a + q, :]) for q in range(2)])
                    last.then_inc(job_done, 1)
                if g == 1:
                    for j in range(4, 8):
                        ada_sum(j)
            def branch(kind, m):
                b_ = start(kind, m)
                pe.wait_ge(zo_lo_ok, 1 if kind == "B" else 2)
                pe.wait_ge(u_lo_ok, (KD if kind == "A" else 0) + m + 1)
                at = buffer_of((kind, m))
                chain(b_, [(wb_hl[:, at, a, k, :], zo_hl[:, b, k, :]) for k in range(PG)
                           for a, b in ((0, 0), (0, 1), (1, 0))], job_done)

            for m in range(KD):
                branch("B", m)
            for j in range(8, 12):
                ada_sum(j)
            emptied_by("V", C - 1)
            by_feature_parts("ga", 0)
            for m in range(KD):
                if m < KD - 1:
                    by_feature_parts("ga", m + 1)
                branch("A", m)

            def h2_turn(ch):
                pe.wait_ge(h2_ok, ch + 1)
                for half in range(2):
                    b_ = start("h2T", 2 * ch + half)
                    for k in range(4):
                        at = (4 * half + k) * P
                        last = nc.tensor.transpose(b_[:, k * P:(k + 1) * P], h2[:, ch, at:at + P], ident[:, :])
                    last.then_inc(job_done, 1)

            def router(ch):
                b_ = start("rout", ch)
                emptied_by("h2T", 2 * ch + 1)
                pe.wait_ge(wr_in, 32)
                chain(b_[0:NE, 0:P], [(wr[:, k, :], h2T[:, k, ch * P:(ch + 1) * P]) for k in range(KD)], job_done)

            firsts = [start("out", 2 * ch) for ch in range(C)]
            for k in range(KD):
                pe.wait_ge(o_lo_ok, k + 1)
                for ch in range(C):
                    for a, b in ((0, 0), (0, 1), (1, 0)):
                        last = mm(firsts[ch], merged_part(k, a)[:, ch * P:(ch + 1) * P], w_out_part(k, b),
                                  start=(k == 0 and a + b == 0), stop=(k == KD - 1 and a == 1))
                    if k == KD - 1:
                        last.then_inc(job_done, 1)
                if k < KD - 1:
                    last.then_inc(o_used, 1)
            for ch in range(C):
                b_ = start("out", 2 * ch + 1)
                w = have("wo", 1)
                for k in range(KD):
                    last = mm(b_, mT[:, k, ch * P:(ch + 1) * P], w[:, k, :], start=(k == 0), stop=(k == KD - 1))
                last.then_inc(job_done, 1)
                if ch:
                    h2_turn(ch - 1)
                if ch > 1:
                    router(ch - 2)
            router(C - 2)
            h2_turn(C - 1)
            router(C - 1)
            b_ = start("rt")
            emptied_by("rout", C - 1)
            for ch in range(C):
                last = nc.tensor.transpose(b_[:, ch * NE:(ch + 1) * NE], lgT[:, ch * P:(ch + 1) * P], ident[0:NE, 0:NE])
            last.then_inc(job_done, 1)
            b_ = start("rank")
            pe.wait_ge(mask_ok, 1)
            pe.wait_ge(consts, 2)
            for ch in range(C):
                chain(b_[:, ch * NE:(ch + 1) * NE], [(onesb[:, :], maskh[:, k, :]) for k in range(ch)]
                      + [(tri[:, :], maskh[:, ch, :])])
            chain(b_[:, C * NE:(C + 1) * NE], [(onesb[:, :], maskh[:, k, :]) for k in range(C)], job_done)
            def turn_rows(b, done):
                for k in range(KD):
                    last = nc.tensor.transpose(ps[:, 4 + k // 4, (k % 4) * P:(k % 4) * P + slots],
                                               XG[0:slots, b, k * P:(k + 1) * P], ident[0:slots, 0:slots])
                last.then_inc(done, 1)

            def biases(e, half):
                pe.wait_ge(b3_ok, 1)
                mm(ps[0:slots, half, :], sel3[:, bass.ds(e, 1)].broadcast_to([3 * NE, slots]), b3[:, half * CH:(half + 1) * CH],
                   start=True, stop=False)

            def up_half(e, half, w, done):
                biases(e, half)
                for k in range(KD):
                    last = mm(ps[0:slots, half, :], xgT[:, k, :], w[:, k, :], start=False, stop=(k == KD - 1))
                last.then_inc(done, 1)

            def up_half_parts(e, half):
                biases(e, half)
                for j in range(GP):
                    pe.wait_ge(lo_ok, e * 2 * GP + (half * GP + j + 1))
                    for q in range(GK):
                        k = j * GK + q
                        for a, b in ((0, 0), (0, 1), (1, 0)):
                            last = mm(ps[0:slots, half, :], xhl[:, a, k, :], whl[:, j % NG, b, q, :], start=False,
                                      stop=(k == KD - 1 and a == 1))
                    last.then_inc(granule_used, 1)

            def places(g):
                pe.wait_ge(oh_ok, g + 1)
                for e in range(g * OHE, (g + 1) * OHE):
                    b_ = bank("ix", min(g, 1))
                    at = 3 * (e if g == 0 else e - OHE)
                    for ch in range(C):
                        last = mm(b_[0:slots, at:at + 3], oh[g % 2][:, e % OHE, ch, :], tokid[:, ch, :], start=(ch == 0),
                                  stop=(ch == C - 1))
                last.then_inc(oh_used, 1)

            start("ix", 0)
            places(0)
            start("ix", 1)
            places(1)
            places(2)
            pe.wait_ge(xg_in[0], 16)
            turn_rows(0, tx_done)
            places(3)
            pe.wait_ge(xl_ok, 1)
            up_half_parts(0, 0)
            places(4)
            places(5)
            up_half_parts(0, 1)
            places(6)
            places(7)


            def turn_act(done):
                for k in range(KF):
                    last = nc.tensor.transpose(ps[:, 6, k * P:k * P + slots], av[:, k * P:(k + 1) * P],
                                               ident[0:slots, 0:slots])
                last.then_inc(done, 1)

            def down(w, done):
                for half in range(2):
                    for k in range(KF):
                        last = mm(ps[0:slots, 2 + half, :], actT[:, k, :], w[:, k, half * CH:(half + 1) * CH],
                                  start=(k == 0), stop=(k == KF - 1))
                last.then_inc(done, 1)

            def expert(e, b, half_e, first=False, last=False):
                if not first:
                    pe.wait_ge(xl_ok, e + 1)
                    for half in range(2):
                        up_half_parts(e, half)
                if not last:
                    pe.wait_ge(xg_in[1 - b], (half_e + b) * 16 + 16)
                    turn_rows(1 - b, tx_done)
                if not first:
                    pb = 1 - b
                    came(pe, SD[pb], half_e + b - 1)
                    pe.wait_ge(actT_ok, e)
                    if not isinstance(e, int) or e > 1:
                        pe.wait_ge(y_ok, e - 1)
                    down(down_w[pb], dn_done)
                pe.wait_ge(av_ok, e + 1)
                turn_act(ta_done)

            expert(0, 0, 0, first=True)
            expert(1, 1, 0)
            with pe.Fori(1, NE // 2 - 1) as i:
                expert(i * 2, 0, i)
                expert(i * 2 + 1, 1, i)
            expert(NE - 2, 0, NE // 2 - 1)
            pe.wait_ge(wt_ok, 1)
            for ch in range(C):
                last = nc.tensor.transpose(ps[0:NE, 7, ch * P:(ch + 1) * P], wts[:, ch, :], ident[:, :])
            last.then_inc(wtT_done, 1)
            expert(NE - 1, 1, NE // 2 - 1, last=True)
            pe.wait_ge(actT_ok, NE)
            pe.wait_ge(y_ok, NE - 1)
            came(pe, SD[1], NE // 2 - 1)
            down(down_w[1], dn_done)

            most = pe.value_load(cmaxi[0:1, 0:1], min_val=0, max_val=T)
            with pe.If(most > slots):
                with pe.Fori(0, OVER) as r:
                    with pe.Fori(0, NE) as e:
                        n = r * NE + e
                        pe.wait_ge(ov_oh, n + 1)
                        for ch in range(C):
                            last = mm(ps[0:slots, 7, 0:3], oh[0][:, 0, ch, :], tokid[:, ch, :], start=(ch == 0), stop=(ch == C - 1))
                        last.then_inc(ov_ix, 1)
                        pe.wait_ge(ov_xg, n * 16 + 16)
                        turn_rows(0, ov_tx)
                        pe.wait_ge(ov_xt, n + 1)
                        pe.wait_ge(ov_w, n * 48 + 48)
                        for half, w in enumerate((gate_w, up_w)):
                            up_half(e, half, w, ov_gu)
                        pe.wait_ge(ov_av, n + 1)
                        turn_act(ov_ta)
                        pe.wait_ge(ov_at, n + 1)
                        down(down_w[0], ov_dn)
                pe.wait_ge(ov_y, OVER * NE)

            pe.wait_ge(wtT_ok, 1)
            pe.wait_ge(bd_ok, 1)
            for ch in range(C):
                if ch == C - 1:
                    pe.wait_ge(y_ok, NE)
                for half in range(2):
                    mm(ps[:, YB_BANKS[2 * ch + half], :], wtT[:, ch * P:(ch + 1) * P], bdn[:, half, :], start=True,
                       stop=True).then_inc(yb_done, 1)


_INS = ['x', 'c', 'norm1_g', 'norm2_g', 'w_ada', 'b_ada', 'w_in', 'kv_norm_g', 'w_uk', 'w_uv', 'w_pool',
        'pool_scale', 'w_a_up', 'w_b_up', 'w_out', 'w_router', 'b_router', 'w_gu', 'b_gu', 'w_down', 'b_down',
        'final_g']


def kernel(**inputs):
    import numpy as _np
    import concourse.bacc as _bacc
    from concourse import mybir as _mybir
    from concourse.bass_utils import run_bass_kernel_spmd as _run

    nc = _bacc.Bacc("TRN2", target_bir_lowering=False, num_devices=1)
    arrays, args = {}, []
    for name in _INS:
        a = _np.ascontiguousarray(inputs[name])
        arrays[f"in_{name}_dram"] = a
        args.append(nc.dram_tensor(f"in_{name}_dram", a.shape, _mybir.dt.from_np(a.dtype), kind="ExternalInput").ap())
    args.append(nc.dram_tensor("out_0_dram", (1, T, D), F32, kind="ExternalOutput").ap())
    trunk(nc, *args)
    r = _run(nc, [arrays], core_ids=[0])
    return r.results[0]["out_0_dram"]
```
